# Optimizing a Trainium2 kernel written in Bass

```python
import math
import jax
import jax.numpy as jnp
from jax import lax
import numpy as np

D_MODEL = 1024
BATCH = 1
SEQ = 256
DEPTH = 2

RMS_EPS = 1e-6
CONV_WIDTH = 4
N_BRANCH = 3

LRU_WIDTH = 1024
LRU_BLOCKS = 16
LRU_BLOCK_DIM = LRU_WIDTH // LRU_BLOCKS
LRU_C = 8.0

GDN_HEADS = 8
GDN_DK = 128
GDN_DV = 128
GDN_QK_WIDTH = GDN_HEADS * GDN_DK
GDN_V_WIDTH = GDN_HEADS * GDN_DV
GDN_CHUNK = 64

RWKV_HEADS = 16
RWKV_HD = 64
RWKV_WIDTH = RWKV_HEADS * RWKV_HD
RWKV_DECAY_RANK = 64
RWKV_ICLR_RANK = 64
RWKV_GATE_RANK = 128
RWKV_GN_EPS = 64e-5
RWKV_SIZES = (RWKV_WIDTH, RWKV_WIDTH, RWKV_WIDTH, RWKV_DECAY_RANK, RWKV_ICLR_RANK, RWKV_GATE_RANK)
RWKV_IN_WIDTH = sum(RWKV_SIZES)
RWKV_OFFSETS = tuple(sum(RWKV_SIZES[:i + 1]) for i in range(len(RWKV_SIZES) - 1))

IN_SIZES = (LRU_WIDTH, LRU_WIDTH, 2 * GDN_QK_WIDTH + GDN_V_WIDTH, GDN_V_WIDTH, GDN_HEADS, GDN_HEADS, RWKV_IN_WIDTH, N_BRANCH * D_MODEL)
IN_WIDTH = sum(IN_SIZES)
IN_OFFSETS = tuple(sum(IN_SIZES[:i + 1]) for i in range(len(IN_SIZES) - 1))

PEER_HEADS = 8
PEER_NKEYS = 128
PEER_EXPERTS = PEER_NKEYS * PEER_NKEYS
PEER_DKEY = 256
PEER_HALF = PEER_DKEY // 2
PEER_TOPK = 16
PEER_BLOCK = 128

kernel_name = 'hybrid_rglru_gdn_rwkv7_peer_trunk'

def rmsnorm(x, w):
    xf = x.astype(jnp.float32)
    y = xf * lax.rsqrt(jnp.mean(xf * xf, axis=-1, keepdims=True) + RMS_EPS)
    return (y * w.astype(jnp.float32)).astype(x.dtype)

def l2norm(x):
    return x * lax.rsqrt(jnp.sum(x * x, axis=-1, keepdims=True) + RMS_EPS)

def causal_depthwise_conv(x, w):
    taps, seq = w.shape[0], x.shape[1]
    xp = jnp.pad(x, ((0, 0), (taps - 1, 0), (0, 0)))
    return sum(xp[:, j:j + seq] * w[j] for j in range(taps))

def token_shift(z, mu):
    z_prev = jnp.pad(z, ((0, 0), (1, 0), (0, 0)))[:, :-1]
    return z + mu * (z_prev - z)

def rglru_branch(u, gate, conv_w, conv_b, w_a, b_a, w_x, b_x, lam):
    bsz, seq, _ = u.shape
    f32 = jnp.float32
    xc = causal_depthwise_conv(u, conv_w) + conv_b
    xh = xc.reshape(bsz, seq, LRU_BLOCKS, LRU_BLOCK_DIM)
    r = jax.nn.sigmoid(jnp.einsum('btni,nij->btnj', xh, w_a).reshape(bsz, seq, LRU_WIDTH) + b_a)
    i = jax.nn.sigmoid(jnp.einsum('btni,nij->btnj', xh, w_x).reshape(bsz, seq, LRU_WIDTH) + b_x)
    log_a = (-LRU_C * r.astype(f32)) * jax.nn.softplus(-lam.astype(f32))
    a = jnp.exp(log_a)
    b = jnp.sqrt(-jnp.expm1(2.0 * log_a)) * (i * xc).astype(f32)

    def combine(left, right):
        a_l, b_l = left
        a_r, b_r = right
        return a_l * a_r, a_r * b_l + b_r

    _, h = lax.associative_scan(combine, (a, b), axis=1)
    return h.astype(u.dtype) * jax.nn.gelu(gate)

def chunked_gated_delta_rule(q, k, v, beta, g):
    bsz, seq, heads, dk = q.shape
    dv = v.shape[-1]
    c = GDN_CHUNK
    n = seq // c

    def to_chunks(t):
        t = t.reshape((bsz, n, c, heads) + t.shape[3:])
        return jnp.moveaxis(t, 3, 1)

    q, k, v, beta, g = (to_chunks(t) for t in (q, k, v, beta, g))
    g = jnp.cumsum(g, axis=-1)
    incl = jnp.tril(jnp.ones((c, c), dtype=bool))
    strict = jnp.tril(jnp.ones((c, c), dtype=bool), -1)
    decay = jnp.exp(jnp.where(incl, g[..., :, None] - g[..., None, :], -jnp.inf))
    k_beta = k * beta[..., None]
    a_mat = jnp.where(strict, jnp.einsum('bhnik,bhnjk->bhnij', k_beta, k) * decay, 0.0)
    lower = a_mat + jnp.eye(c, dtype=a_mat.dtype)
    rhs = jnp.concatenate([v * beta[..., None], k_beta * jnp.exp(g)[..., None]], axis=-1)
    sol = lax.linalg.triangular_solve(lower, rhs, left_side=True, lower=True, unit_diagonal=True)
    u_c, w_c = sol[..., :dv], sol[..., dv:]
    qk = jnp.einsum('bhnik,bhnjk->bhnij', q, k) * decay
    q_dec = q * jnp.exp(g)[..., None]
    k_dec = k * jnp.exp(g[..., -1:] - g)[..., None]
    g_tot = jnp.exp(g[..., -1])

    def step(state, inp):
        qk_n, qd_n, kd_n, u_n, w_n, gt_n = inp
        v_new = u_n - jnp.einsum('bhck,bhkv->bhcv', w_n, state)
        o = jnp.einsum('bhck,bhkv->bhcv', qd_n, state) + jnp.einsum('bhcs,bhsv->bhcv', qk_n, v_new)
        state = state * gt_n[..., None, None] + jnp.einsum('bhck,bhcv->bhkv', kd_n, v_new)
        return state, o

    xs = tuple(jnp.moveaxis(t, 2, 0) for t in (qk, q_dec, k_dec, u_c, w_c, g_tot))
    s0 = jnp.zeros((bsz, heads, dk, dv), q.dtype)
    _, o = lax.scan(step, s0, xs)
    return jnp.transpose(o, (1, 0, 3, 2, 4)).reshape(bsz, seq, heads, dv)

def gdn_branch(qkv, z, alpha, beta_pre, conv_w, a_log, dt_bias, norm_w):
    bsz, seq, _ = qkv.shape
    f32 = jnp.float32
    qkv = jax.nn.silu(causal_depthwise_conv(qkv, conv_w)).astype(f32)
    q, k, v = jnp.split(qkv, (GDN_QK_WIDTH, 2 * GDN_QK_WIDTH), axis=-1)
    q = l2norm(q.reshape(bsz, seq, GDN_HEADS, GDN_DK)) * (GDN_DK ** -0.5)
    k = l2norm(k.reshape(bsz, seq, GDN_HEADS, GDN_DK))
    v = v.reshape(bsz, seq, GDN_HEADS, GDN_DV)
    beta = jax.nn.sigmoid(beta_pre.astype(f32))
    g = -jnp.exp(a_log.astype(f32)) * jax.nn.softplus(alpha.astype(f32) + dt_bias.astype(f32))
    o = chunked_gated_delta_rule(q, k, v, beta, g)
    o = o * lax.rsqrt(jnp.mean(o * o, axis=-1, keepdims=True) + RMS_EPS) * norm_w.astype(f32)
    o = o * jax.nn.silu(z.astype(f32).reshape(bsz, seq, GDN_HEADS, GDN_DV))
    return o.reshape(bsz, seq, GDN_V_WIDTH).astype(z.dtype)

def rwkv7_branch(z_rw, mu, w0, w_up, a0, a_up, g_up, k_k, k_a, r_k, lnx_w, lnx_b):
    bsz, seq, _ = z_rw.shape
    f32 = jnp.float32
    zs = token_shift(z_rw, mu)
    r, k, v, wl, al, gl = jnp.split(zs, RWKV_OFFSETS, axis=-1)
    w_log = -jax.nn.softplus(-(w0 + jnp.tanh(wl) @ w_up)) - 0.5
    decay = jnp.exp(-jnp.exp(w_log.astype(f32)))
    a = jax.nn.sigmoid(a0 + al @ a_up)
    gate = jax.nn.sigmoid(gl) @ g_up
    heads = lambda t: t.astype(f32).reshape(bsz, seq, RWKV_HEADS, RWKV_HD)
    kk = l2norm(heads(k * k_k))
    k = k * (1.0 + (a - 1.0) * k_a)
    r_h, k_h, v_h, a_h, w_h = heads(r), heads(k), heads(v), heads(a), heads(decay)

    def step(state, inp):
        r_t, w_t, k_t, v_t, kk_t, kka_t = inp
        s_kk = jnp.einsum('bhvk,bhk->bhv', state, kk_t)
        state = state * w_t[:, :, None, :] - s_kk[..., None] * kka_t[:, :, None, :] + v_t[..., None] * k_t[:, :, None, :]
        return state, jnp.einsum('bhvk,bhk->bhv', state, r_t)

    xs = tuple(jnp.swapaxes(t, 0, 1) for t in (r_h, w_h, k_h, v_h, kk, kk * a_h))
    s0 = jnp.zeros((bsz, RWKV_HEADS, RWKV_HD, RWKV_HD), f32)
    _, o = lax.scan(step, s0, xs)
    o = jnp.swapaxes(o, 0, 1)
    mean = jnp.mean(o, axis=-1, keepdims=True)
    var = jnp.mean(jnp.square(o - mean), axis=-1, keepdims=True)
    o = ((o - mean) * lax.rsqrt(var + RWKV_GN_EPS)).reshape(bsz, seq, RWKV_WIDTH)
    o = o * lnx_w.astype(f32) + lnx_b.astype(f32)
    bonus = jnp.sum(r_h * k_h * r_k.astype(f32), axis=-1, keepdims=True) * v_h
    o = (o + bonus.reshape(bsz, seq, RWKV_WIDTH)) * gate.astype(f32)
    return o.astype(z_rw.dtype)

def hybrid_mixer(xn, w_in, lru_conv_w, lru_conv_b, lru_w_a, lru_b_a, lru_w_x, lru_b_x, lru_lambda,
                 gdn_conv_w, gdn_a_log, gdn_dt_bias, gdn_norm_w,
                 rwkv_mu, rwkv_w0, rwkv_w_up, rwkv_a0, rwkv_a_up, rwkv_g_up, rwkv_k_k, rwkv_k_a,
                 rwkv_r_k, rwkv_lnx_w, rwkv_lnx_b, merge_b, p_lru, p_gdn, p_rwkv, w_out):
    z = xn @ w_in
    u_lru, g_lru, qkv, z_gdn, alpha, beta_pre, z_rw, z_merge = jnp.split(z, IN_OFFSETS, axis=-1)
    y_a = rglru_branch(u_lru, g_lru, lru_conv_w, lru_conv_b, lru_w_a, lru_b_a, lru_w_x, lru_b_x, lru_lambda)
    y_b = gdn_branch(qkv, z_gdn, alpha, beta_pre, gdn_conv_w, gdn_a_log, gdn_dt_bias, gdn_norm_w)
    y_c = rwkv7_branch(z_rw, rwkv_mu, rwkv_w0, rwkv_w_up, rwkv_a0, rwkv_a_up, rwkv_g_up, rwkv_k_k,
                       rwkv_k_a, rwkv_r_k, rwkv_lnx_w, rwkv_lnx_b)
    g_a, g_b, g_c = jnp.split(jax.nn.sigmoid(z_merge + merge_b), N_BRANCH, axis=-1)
    merged = g_a * (y_a @ p_lru) + g_b * (y_b @ p_gdn) + g_c * (y_c @ p_rwkv)
    return merged @ w_out

def peer_ffn(xn, w_query, sub_keys, expert_u, expert_v):
    bsz, seq, dim = xn.shape
    q = (xn @ w_query).reshape(bsz, seq, PEER_HEADS, 2, PEER_HALF)
    s = jnp.einsum('bthsc,hsnc->bthsn', q, sub_keys).astype(jnp.float32)
    top_s, top_i = lax.top_k(s, PEER_TOPK)
    cand_s = (top_s[..., 0, :, None] + top_s[..., 1, None, :]).reshape(bsz, seq, PEER_HEADS, PEER_TOPK * PEER_TOPK)
    cand_i = (top_i[..., 0, :, None] * PEER_NKEYS + top_i[..., 1, None, :]).reshape(bsz, seq, PEER_HEADS, PEER_TOPK * PEER_TOPK)
    best_s, best_pos = lax.top_k(cand_s, PEER_TOPK)
    expert_idx = jnp.take_along_axis(cand_i, best_pos, axis=-1)
    gate = jax.nn.softmax(best_s, axis=-1)
    n_blocks = (bsz * seq) // PEER_BLOCK
    x_blk = xn.reshape(n_blocks, PEER_BLOCK, dim)
    i_blk = expert_idx.reshape(n_blocks, PEER_BLOCK, PEER_HEADS * PEER_TOPK)
    g_blk = gate.reshape(n_blocks, PEER_BLOCK, PEER_HEADS * PEER_TOPK)

    def block(args):
        xb, ib, gb = args
        u = jnp.take(expert_u, ib, axis=0)
        act = gb.astype(xb.dtype) * jax.nn.gelu(jnp.einsum('pkd,pd->pk', u, xb))
        vv = jnp.take(expert_v, ib, axis=0)
        return jnp.einsum('pk,pkd->pd', act, vv)

    y = lax.map(block, (x_blk, i_blk, g_blk))
    return y.reshape(bsz, seq, dim)

def setup_inputs(seed: int = 0) -> dict:
    key = jax.random.key(seed)
    ks = iter(jax.random.split(key, 48))
    f32 = jnp.float32
    L = DEPTH

    def normal(shape, scale):
        return scale * jax.random.normal(next(ks), shape, f32)

    def uniform(shape, lo, hi):
        return jax.random.uniform(next(ks), shape, f32, lo, hi)

    x = normal((BATCH, SEQ, D_MODEL), 1.0)
    norm_mix_w = 1.0 + normal((L, D_MODEL), 0.02)
    norm_ffn_w = 1.0 + normal((L, D_MODEL), 0.02)
    final_norm_w = 1.0 + normal((D_MODEL,), 0.02)
    w_in = normal((L, D_MODEL, IN_WIDTH), D_MODEL ** -0.5)
    lru_conv_w = normal((L, CONV_WIDTH, LRU_WIDTH), CONV_WIDTH ** -0.5)
    lru_conv_b = normal((L, LRU_WIDTH), 0.02)
    lru_w_a = normal((L, LRU_BLOCKS, LRU_BLOCK_DIM, LRU_BLOCK_DIM), LRU_BLOCK_DIM ** -0.5)
    lru_b_a = normal((L, LRU_WIDTH), 0.02)
    lru_w_x = normal((L, LRU_BLOCKS, LRU_BLOCK_DIM, LRU_BLOCK_DIM), LRU_BLOCK_DIM ** -0.5)
    lru_b_x = normal((L, LRU_WIDTH), 0.02)
    a_pow = uniform((L, LRU_WIDTH), 0.9, 0.999) ** (1.0 / LRU_C)
    lru_lambda = jnp.log(a_pow) - jnp.log1p(-a_pow)
    gdn_conv_w = normal((L, CONV_WIDTH, 2 * GDN_QK_WIDTH + GDN_V_WIDTH), CONV_WIDTH ** -0.5)
    gdn_a_log = jnp.log(uniform((L, GDN_HEADS), 1.0, 16.0))
    dt = jnp.exp(uniform((L, GDN_HEADS), math.log(1e-3), math.log(1e-1)))
    gdn_dt_bias = dt + jnp.log(-jnp.expm1(-dt))
    gdn_norm_w = 1.0 + normal((L, GDN_DV), 0.02)
    rwkv_mu = uniform((L, RWKV_IN_WIDTH), 0.0, 1.0)
    rwkv_w0 = uniform((L, RWKV_WIDTH), -6.5, -1.5)
    rwkv_w_up = normal((L, RWKV_DECAY_RANK, RWKV_WIDTH), 0.5 * RWKV_DECAY_RANK ** -0.5)
    rwkv_a0 = normal((L, RWKV_WIDTH), 0.1)
    rwkv_a_up = normal((L, RWKV_ICLR_RANK, RWKV_WIDTH), 0.5 * RWKV_ICLR_RANK ** -0.5)
    rwkv_g_up = normal((L, RWKV_GATE_RANK, RWKV_WIDTH), RWKV_GATE_RANK ** -0.5)
    rwkv_k_k = 0.85 + normal((L, RWKV_WIDTH), 0.02)
    rwkv_k_a = 1.0 + normal((L, RWKV_WIDTH), 0.02)
    rwkv_r_k = normal((L, RWKV_HEADS, RWKV_HD), 0.1)
    rwkv_lnx_w = 1.0 + normal((L, RWKV_WIDTH), 0.02)
    rwkv_lnx_b = normal((L, RWKV_WIDTH), 0.02)
    merge_b = normal((L, N_BRANCH * D_MODEL), 0.02)
    p_lru = normal((L, LRU_WIDTH, D_MODEL), LRU_WIDTH ** -0.5)
    p_gdn = normal((L, GDN_V_WIDTH, D_MODEL), GDN_V_WIDTH ** -0.5)
    p_rwkv = normal((L, RWKV_WIDTH, D_MODEL), RWKV_WIDTH ** -0.5)
    w_out = normal((L, D_MODEL, D_MODEL), D_MODEL ** -0.5)
    peer_wq = normal((L, D_MODEL, PEER_HEADS * PEER_DKEY), D_MODEL ** -0.5)
    peer_keys = normal((L, PEER_HEADS, 2, PEER_NKEYS, PEER_HALF), PEER_HALF ** -0.5)
    peer_u = normal((L, PEER_EXPERTS, D_MODEL), D_MODEL ** -0.5)
    peer_v = normal((L, PEER_EXPERTS, D_MODEL), PEER_TOPK ** -0.5)
    return {'x': x, 'norm_mix_w': norm_mix_w, 'norm_ffn_w': norm_ffn_w, 'final_norm_w': final_norm_w,
            'w_in': w_in, 'lru_conv_w': lru_conv_w, 'lru_conv_b': lru_conv_b, 'lru_w_a': lru_w_a,
            'lru_b_a': lru_b_a, 'lru_w_x': lru_w_x, 'lru_b_x': lru_b_x, 'lru_lambda': lru_lambda,
            'gdn_conv_w': gdn_conv_w, 'gdn_a_log': gdn_a_log, 'gdn_dt_bias': gdn_dt_bias,
            'gdn_norm_w': gdn_norm_w, 'rwkv_mu': rwkv_mu, 'rwkv_w0': rwkv_w0, 'rwkv_w_up': rwkv_w_up,
            'rwkv_a0': rwkv_a0, 'rwkv_a_up': rwkv_a_up, 'rwkv_g_up': rwkv_g_up, 'rwkv_k_k': rwkv_k_k,
            'rwkv_k_a': rwkv_k_a, 'rwkv_r_k': rwkv_r_k, 'rwkv_lnx_w': rwkv_lnx_w, 'rwkv_lnx_b': rwkv_lnx_b,
            'merge_b': merge_b, 'p_lru': p_lru, 'p_gdn': p_gdn, 'p_rwkv': p_rwkv, 'w_out': w_out,
            'peer_wq': peer_wq, 'peer_keys': peer_keys, 'peer_u': peer_u, 'peer_v': peer_v}

def reference(x, norm_mix_w, norm_ffn_w, final_norm_w, w_in, lru_conv_w, lru_conv_b, lru_w_a,
              lru_b_a, lru_w_x, lru_b_x, lru_lambda, gdn_conv_w, gdn_a_log, gdn_dt_bias, gdn_norm_w,
              rwkv_mu, rwkv_w0, rwkv_w_up, rwkv_a0, rwkv_a_up, rwkv_g_up, rwkv_k_k, rwkv_k_a,
              rwkv_r_k, rwkv_lnx_w, rwkv_lnx_b, merge_b, p_lru, p_gdn, p_rwkv, w_out,
              peer_wq, peer_keys, peer_u, peer_v):
    h = x
    for l in range(DEPTH):
        xn = rmsnorm(h, norm_mix_w[l])
        h = h + hybrid_mixer(xn, w_in[l], lru_conv_w[l], lru_conv_b[l], lru_w_a[l], lru_b_a[l],
                             lru_w_x[l], lru_b_x[l], lru_lambda[l], gdn_conv_w[l], gdn_a_log[l],
                             gdn_dt_bias[l], gdn_norm_w[l], rwkv_mu[l], rwkv_w0[l], rwkv_w_up[l],
                             rwkv_a0[l], rwkv_a_up[l], rwkv_g_up[l], rwkv_k_k[l], rwkv_k_a[l],
                             rwkv_r_k[l], rwkv_lnx_w[l], rwkv_lnx_b[l], merge_b[l], p_lru[l],
                             p_gdn[l], p_rwkv[l], w_out[l])
        xn = rmsnorm(h, norm_ffn_w[l])
        h = h + peer_ffn(xn, peer_wq[l], peer_keys[l], peer_u[l], peer_v[l])
    return rmsnorm(h, final_norm_w)


_drawn_inputs = setup_inputs


def setup_inputs(seed=0):
    import zlib

    import numpy as np

    out = dict(_drawn_inputs(seed))
    spreads = {}
    factors = {'final_norm_w': 8.969,
     'lru_b_a': 39.851,
     'lru_b_x': 25.425,
     'gdn_norm_w': 3.149,
     'rwkv_w_up': 3.196,
     'rwkv_k_k': 10.956,
     'rwkv_k_a': 2.931,
     'rwkv_lnx_w': 3.082,
     'rwkv_lnx_b': 3.033,
     'merge_b': 4.129,
     'norm_ffn_w': 3.018}
    for name, (base, spread) in spreads.items():
        noise = np.random.default_rng([zlib.crc32(name.encode()), seed]).standard_normal(out[name].shape)
        drawn = base * np.exp(spread * noise) if base else spread * noise
        out[name] = jnp.asarray(drawn.astype(out[name].dtype))
    for name, factor in factors.items():
        out[name] = (out[name] * factor).astype(out[name].dtype)
    return out
```

```python
import math
from contextlib import ExitStack

import concourse.bass as bass
from concourse import mybir

F32 = mybir.dt.float32
U32 = mybir.dt.uint32
F32R = mybir.dt.float32r
ALU = mybir.AluOpType
ACT = mybir.ActivationFunctionType
AX = mybir.AxisListType

P = 128
T = 256
D = 1024
KT = D // P
NB = T // P
L = 2
EPS = 1e-6
GN_EPS = 64e-5
LRU_C = 8.0
HD = 64
CH = 64
GDN_SCALE = 128 ** -0.5
DECAY = math.exp(-0.5)
TOPK = 16
PH = 8
NK = 128

LRU_COLS = ["w0", "w1", "w2", "w3", "cb", "ba", "bx", "lam"]
RWKV_COLS = ["mu_r", "mu_k", "mu_v", "w0", "a0", "k_k", "k_a", "r_k", "ln_w", "ln_b"]
RWKV_MADE = ["om_r", "om_k", "om_v", "om_ka"]
GDN_COLS = [f"{x}{j}" for x in "qkv" for j in range(4)]
N_LEVELS = 7


class Steps:

    def __init__(self, sem, book, name, looped):
        self.sem, self.book, self.name, self.looped, self.n = sem, book, name, looped, 0

    def per(self):
        return self.book.get((self.name, "per"), 1)

    def prime(self, engine):
        engine.sem_inc(self.sem, self.per())

    def begin(self):
        self.n = 0

    def one(self, label=None):
        self.n += 1
        if label:
            self.book[self.name, label] = self.n
        return 1

    def end(self):
        self.book[self.name, "per"] = self.n

    def index(self, label):
        assert self.book.get("first") or (self.name, label) in self.book, (self.name, label)
        return self.book.get((self.name, label), 1)

    def at(self, label, i=0):
        return (i + 1) * self.per() + self.index(label) if self.looped else self.index(label)

    def before(self, label, i):
        return i * self.per() + self.index(label)

    def now(self, i=0):
        assert self.n > 0
        return (i + 1) * self.per() + self.n if self.looped else self.n


def build(nc, A, out, book):
    ctx = ExitStack()
    with ctx:
        _program(nc, ctx, A, out, book)


def _program(nc, ctx, A, out, book):
    def sb(name, shape, dt=F32):
        return ctx.enter_context(nc.sbuf_tensor(name, shape, dt))

    def sem(name):
        return ctx.enter_context(nc.semaphore(name))

    cleared = []

    def lsem(name):
        s = sem(name)
        cleared.append(s)
        return s

    def steps(name, looped=False):
        return Steps(lsem(name), book, name, looped)

    h = sb("h", [P, KT, T])
    ident = sb("ident", [P, P])
    ones = sb("ones", [P, P])
    blk64 = sb("blk64", [P, P])
    upto = sb("upto", [P, P])
    after = sb("after", [P, P])
    gmask = sb("gmask", [P, 2, P])
    rmask = sb("rmask", [P, 2, P])
    lmask = sb("lmask", [P, N_LEVELS, P])
    restart = sb("restart", [P, T])
    half = sb("half", [P, 2])
    iota = sb("iota", [P, P])
    zrow = sb("zrow", [P, 1])
    norm_w = sb("norm_w", [P, 2 * L + 1, KT])
    ARENA = 32768
    arena = sb("arena", [P, ARENA])
    banks = [ctx.enter_context(nc.psum_tensor(f"bank{i}", [P, 512], F32)) for i in range(8)]

    class Region:

        def __init__(self, at):
            self.at_ = at

        def __call__(self, *shape, dt=F32):
            n = math.prod(shape)
            assert self.at_ + n <= ARENA, (self.at_, n)
            v = arena[:, self.at_:self.at_ + n]
            self.at_ += n
            if dt is not F32:
                v = v.bitcast(dt)
            if len(shape) == 1:
                return v
            names = "abcd"[:len(shape)]
            return v.rearrange(f"p ({' '.join(names)}) -> p {' '.join(names)}", **{k: s for k, s in zip(names[1:], shape[1:])})

    base = Region(0)
    xn = base(KT, T)
    PEER = base.at_
    ya, yb, yc = base(KT, T), base(KT, T), base(KT, T)
    BRANCH = base.at_

    consts_sem = sem("consts")
    pool_sem = sem("consts_pool")
    vec_sem = sem("consts_vec")
    load_x = sem("load_x")

    with nc.Block() as block:
        @block.sync
        def _(sp):
            sp.dma_start(h[:], A["x"]).then_inc(load_x, 16)
            sp.dma_start(norm_w[:], A["norms"]).then_inc(load_x, 16)
            sp.wait_ge(load_x, 32)

        @block.gpsimd
        def _(g):
            n = 0

            def fill(ap, value):
                nonlocal n
                g.memset(ap, value).then_inc(pool_sem, 1)
                n += 1
                g.wait_ge(pool_sem, n)

            def keep(ap, op, basev, pattern, mult, fill_value=0.0):
                nonlocal n
                g.affine_select(out=ap, in_=ap, compare_op=op, fill=fill_value, base=basev,
                                pattern=pattern, channel_multiplier=mult).then_inc(pool_sem, 1)
                n += 1
                g.wait_ge(pool_sem, n)

            for m in (ones, upto, after, gmask, rmask, lmask, restart, half, blk64):
                fill(m[:], 1.0)
            fill(ident[:], 0.0)
            keep(ident[:], ALU.not_equal, 0, [[-1, P]], 1, 1.0)
            keep(upto[:], ALU.is_ge, 0, [[1, P]], -1)
            keep(after[:], ALU.is_gt, 0, [[-1, P]], 1)
            for m in (gmask, rmask):
                keep(m[:, 0], ALU.is_gt, 0, [[1, P]], -1)
                keep(m[:, 1], ALU.is_ge, 0, [[1, P]], -1)
            for m in (blk64[:], rmask[:, 0], rmask[:, 1]):
                keep(m[:, 0:64], ALU.is_ge, 63, [[0, 64]], -1)
                keep(m[:, 64:128], ALU.is_ge, -64, [[0, 64]], 1)
            keep(half[:, 0:1], ALU.is_ge, 63, [[0, 1]], -1)
            keep(half[:, 1:2], ALU.is_ge, -64, [[0, 1]], 1)
            for lev in range(N_LEVELS):
                w = 1 << lev
                nb = P // (2 * w)
                m = lmask[:, lev].rearrange("p (b h w) -> p b h w", b=nb, h=2)
                keep(m, ALU.is_ge, 0, [[-2 * w, nb], [0, 2], [0, w]], 1)
                keep(m, ALU.is_ge, w - 1, [[2 * w, nb], [0, 2], [0, w]], -1)
                fill(m[:, :, 0, :], 0.0)
            fill(restart[:].rearrange("p (c t) -> p c t", t=CH)[:, :, 0], 0.0)
            fill(zrow[:], 0.0)
            g.iota(iota[:], pattern=[[1, P]], base=0, channel_multiplier=0,
                   allow_small_or_imprecise_dtypes=True).then_inc(pool_sem, 1)
            g.wait_ge(pool_sem, n + 1)

    def rmsnorm(tag, w, dst):
        V, E, S = steps(tag + "_vec"), steps(tag + "_pe"), steps(tag + "_act")
        r = Region(BRANCH)
        sq, rs = r(KT, T), r(T)
        ss = banks[0][:, 0:T]
        with nc.Block() as block:
            @block.vector
            def _(v):
                v.tensor_tensor(sq, h[:], h[:], ALU.mult).then_inc(V.sem, V.one("sq"))
                v.wait_ge(E.sem, E.at("ss"))
                v.tensor_scalar(rs, ss, 1.0 / D, EPS, ALU.mult, ALU.add).then_inc(V.sem, V.one("ms"))
                v.wait_ge(S.sem, S.at("root"))
                v.reciprocal(rs, rs).then_inc(V.sem, V.one())
                v.wait_ge(V.sem, V.now())
                for k in range(KT):
                    v.scalar_tensor_tensor(dst[:, k, :], h[:, k, :], w[:, k:k + 1], rs, ALU.mult, ALU.mult)\
                        .then_inc(V.sem, V.one())
                v.wait_ge(V.sem, V.now())

            @block.tensor
            def _(te):
                te.wait_ge(V.sem, V.at("sq"))
                for k in range(KT):
                    mm = te.matmul(ss, ones[:], sq[:, k, :], start=(k == 0), stop=(k == KT - 1))
                mm.then_inc(E.sem, E.one("ss"))

            @block.scalar
            def _(a):
                a.wait_ge(V.sem, V.at("ms"))
                a.activation(rs, rs, ACT.Sqrt).then_inc(S.sem, S.one("root"))

    def load_slots(sp, source, loaded, E, labels, n_iter, first=0):
        for s in range(len(labels)):
            sp.dma_start(ring[:, first + s, :], source(0, s)).then_inc(loaded[s], 16)
        with sp.Fori(1, n_iter) as i:
            for s, label in enumerate(labels):
                sp.wait_ge(E.sem, E.before(label, i))
                sp.dma_start(ring[:, first + s, :], source(i, s)).then_inc(loaded[s], 16)

    def project(te, ps, slot, x=None, ks=range(KT)):
        x = xn if x is None else x
        for k in ks:
            mm = te.matmul(ps, ring[:, slot, k * P:(k + 1) * P], x[:, k, :], start=(k == 0), stop=(k == KT - 1))
        return mm

    def softplus_exp(a, S, x, e, tag):
        a.activation(e, x, ACT.Abs).then_inc(S.sem, S.one())
        a.wait_ge(S.sem, S.now())
        a.activation(e, e, ACT.Exp, scale=-1.0).then_inc(S.sem, S.one(tag + "_e"))

    def softplus_log(v, V, x, e, z, z2, p, m):
        v.tensor_scalar(z, e, 2.0, None, ALU.add).then_inc(V.sem, V.one())
        v.wait_ge(V.sem, V.now())
        v.reciprocal(z, z).then_inc(V.sem, V.one())
        v.wait_ge(V.sem, V.now())
        v.tensor_tensor(z, z, e, ALU.mult).then_inc(V.sem, V.one())
        v.wait_ge(V.sem, V.now())
        v.tensor_tensor(z2, z, z, ALU.mult).then_inc(V.sem, V.one())
        v.wait_ge(V.sem, V.now())
        v.tensor_scalar(p, z2, 1.0 / 17, None, ALU.mult).then_inc(V.sem, V.one())
        for k in range(7, 0, -1):
            v.wait_ge(V.sem, V.now())
            v.scalar_tensor_tensor(p, p, 1.0 / (2 * k + 1), z2, ALU.add, ALU.mult).then_inc(V.sem, V.one())
        v.wait_ge(V.sem, V.now())
        v.scalar_tensor_tensor(p, p, 1.0, z, ALU.add, ALU.mult).then_inc(V.sem, V.one())
        v.tensor_scalar(m, x, 0.0, None, ALU.max).then_inc(V.sem, V.one())
        v.wait_ge(V.sem, V.now())
        v.scalar_tensor_tensor(p, p, 2.0, m, ALU.mult, ALU.add).then_inc(V.sem, V.one())

    def lru_phase(l):
        NI = KT // 2
        VA, SA, EA = steps("lruA_vec", True), steps("lruA_act", True), steps("lruA_pe", True)
        VB, SB, EB = steps("lruB_vec"), steps("lruB_act"), steps("lruB_pe")
        loaded = [lsem(f"lru_tile{s}") for s in range(4)]
        pload = lsem("lru_params")
        r = Region(BRANCH)
        par = r(KT, len(LRU_COLS))
        wax = r(KT, 2, P)
        xc, rr, ii, aa, bb = r(KT, T), r(KT, T), r(KT, T), r(KT, T), r(KT, T)
        lam_n, e, z, z2, spl, m8 = (r(KT) for _ in range(6))
        c = {n: k for k, n in enumerate(LRU_COLS)}
        with nc.Block() as block:
            @block.sync
            def _(sp):
                sp.dma_start(par, A["lru_par"][l]).then_inc(pload, 16)
                sp.dma_start(wax, A["lru_gates"][l]).then_inc(pload, 16)
                load_slots(sp, lambda i, s: A["w_lru"][l, i, s], loaded, EA, [f"z{s}" for s in range(4)], NI)

            @block.tensor
            def _(te):
                EA.prime(te)
                with te.Fori(0, NI) as i:
                    EA.begin()
                    for s in range(4):
                        te.wait_ge(loaded[s], 16 * i + 16)
                        if s % 2:
                            te.wait_ge(SA.sem, SA.before(f"gelu{s}", i))
                        else:
                            te.wait_ge(VA.sem, VA.before(f"tap3_{s}", i))
                        project(te, banks[s][:, 0:T], s).then_inc(EA.sem, EA.one(f"z{s}"))
                    EA.end()
                te.wait_ge(pload, 32)
                te.wait_ge(VA.sem, VA.at("tap3_2", NI - 1))
                te.wait_ge(SA.sem, SA.at("gelu3", NI - 1))
                for k in range(KT):
                    if k >= 4:
                        te.wait_ge(SB.sem, SB.at(f"i{k - 4}"))
                    te.matmul(banks[k % 4][:, 0:T], wax[:, k, 0, :], xc[:, k, :], start=True, stop=True)\
                        .then_inc(EB.sem, EB.one(f"r{k}"))
                    te.matmul(banks[4 + k % 4][:, 0:T], wax[:, k, 1, :], xc[:, k, :], start=True, stop=True)\
                        .then_inc(EB.sem, EB.one(f"i{k}"))

            @block.scalar
            def _(a):
                SA.prime(a)
                a.wait_ge(pload, 32)
                with a.Fori(0, NI) as i:
                    SA.begin()
                    for u in range(2):
                        k = 2 * i + u
                        a.wait_ge(EA.sem, EA.at(f"z{2 * u}", i))
                        a.activation(xc[:, k, :], banks[2 * u][:, 0:T], ACT.Identity, bias=par[:, k, c["cb"]:c["cb"] + 1],
                                     scale=par[:, k, c["w3"]:c["w3"] + 1]).then_inc(SA.sem, SA.one(f"xc{2 * u}"))
                        a.wait_ge(EA.sem, EA.at(f"z{2 * u + 1}", i))
                        a.activation(ya[:, k, :], banks[2 * u + 1][:, 0:T], ACT.Gelu_apprx_tanh)\
                            .then_inc(SA.sem, SA.one(f"gelu{2 * u + 1}"))
                    SA.end()
                a.wait_ge(VB.sem, VB.at("neg"))
                softplus_exp(a, SB, lam_n, e, "sp")
                for k in range(KT):
                    a.wait_ge(EB.sem, EB.at(f"r{k}"))
                    a.activation(rr[:, k, :], banks[k % 4][:, 0:T], ACT.Sigmoid, bias=par[:, k, c["ba"]:c["ba"] + 1])\
                        .then_inc(SB.sem, SB.one())
                    a.wait_ge(EB.sem, EB.at(f"i{k}"))
                    a.activation(ii[:, k, :], banks[4 + k % 4][:, 0:T], ACT.Sigmoid, bias=par[:, k, c["bx"]:c["bx"] + 1])\
                        .then_inc(SB.sem, SB.one(f"i{k}"))
                a.wait_ge(VB.sem, VB.at("nla"))
                a.activation(aa, rr, ACT.Exp, scale=-1.0).then_inc(SB.sem, SB.one("a"))
                a.activation(bb, rr, ACT.Tanh).then_inc(SB.sem, SB.one("tanh"))
                a.wait_ge(VB.sem, VB.at("b2"))
                a.activation(bb, bb, ACT.Sqrt).then_inc(SB.sem, SB.one("b"))

            @block.vector
            def _(v):
                VA.prime(v)
                v.wait_ge(pload, 32)
                with v.Fori(0, NI) as i:
                    VA.begin()
                    for u in range(2):
                        k = 2 * i + u
                        v.wait_ge(SA.sem, SA.at(f"xc{2 * u}", i))
                        for sh in (1, 2, 3):
                            if sh > 1:
                                v.wait_ge(VA.sem, VA.now(i))
                            v.scalar_tensor_tensor(xc[:, k, sh:T], banks[2 * u][:, 0:T - sh], par[:, k, 3 - sh:4 - sh],
                                                   xc[:, k, sh:T], ALU.mult, ALU.add)\
                                .then_inc(VA.sem, VA.one(f"tap{sh}_{2 * u}"))
                    VA.end()
                v.tensor_scalar(lam_n, par[:, :, c["lam"]], -1.0, None, ALU.mult).then_inc(VB.sem, VB.one("neg"))
                v.wait_ge(SB.sem, SB.at("sp_e"))
                v.wait_ge(VB.sem, VB.now())
                softplus_log(v, VB, lam_n, e, z, z2, spl, m8)
                v.wait_ge(VB.sem, VB.now())
                v.wait_ge(SB.sem, SB.at(f"i{KT - 1}"))
                for k in range(KT):
                    v.tensor_scalar(rr[:, k, :], rr[:, k, :], spl[:, k:k + 1], LRU_C, ALU.mult, ALU.mult)\
                        .then_inc(VB.sem, VB.one("nla"))
                v.wait_ge(VA.sem, VA.at("tap3_2", NI - 1))
                v.tensor_tensor(ii, ii, xc, ALU.mult).then_inc(VB.sem, VB.one("ix"))
                v.wait_ge(SB.sem, SB.at("tanh"))
                v.tensor_tensor(rr, aa, aa, ALU.mult).then_inc(VB.sem, VB.one("a2"))
                v.wait_ge(VB.sem, VB.now())
                v.scalar_tensor_tensor(bb, rr, 1.0, bb, ALU.add, ALU.mult).then_inc(VB.sem, VB.one("b2"))
                v.wait_ge(SB.sem, SB.at("b"))
                v.tensor_tensor(bb, bb, ii, ALU.mult).then_inc(VB.sem, VB.one("bx"))
                for k in range(KT):
                    v.wait_ge(VB.sem, VB.now())
                    v.tensor_tensor_scan(rr[:, k, :], aa[:, k, :], bb[:, k, :], 0.0, ALU.mult, ALU.add)\
                        .then_inc(VB.sem, VB.one("scan"))
                v.wait_ge(VB.sem, VB.now())
                v.tensor_tensor(ya, ya, rr, ALU.mult).then_inc(VB.sem, VB.one("ya"))

    def invert_levels(te, a, v, g, name, E, S, V, G, i, NLM, T_, TT, X, bX, bY, bYT, levels, fill=None):
        m4 = range(4)
        view = lambda b: b[:, :].rearrange("p (m c) -> p m c", m=4)
        for lev in range(1, levels):
            last = lev == levels - 1
            t = f"{name}{lev}"
            if te is not None:
                te.wait_ge(G.sem, G.at(f"{t}mask", i))
                if lev == 1:
                    te.wait_ge(S.sem, S.at(f"{name}T", i))
                else:
                    te.wait_ge(V.sem, V.at(f"{name}{lev - 1}TT", i))
                for m in m4:
                    mm = te.matmul(view(bX)[:, m], NLM[:, lev - 1, m], T_[:, m], start=True, stop=True)
                mm.then_inc(E.sem, E.one(f"{t}X"))
                if fill:
                    fill(lev)
                te.wait_ge(S.sem, S.at(f"{t}X", i))
                if not last:
                    for m in m4:
                        mm = te.matmul(view(bY)[:, m], TT[:, m], X[:, m], start=True, stop=True)
                    mm.then_inc(E.sem, E.one(f"{t}Y"))
                for m in m4:
                    mm = te.matmul(view(bYT)[:, m], X[:, m], TT[:, m], start=True, stop=True)
                mm.then_inc(E.sem, E.one(f"{t}YT"))
            if a is not None:
                a.wait_ge(E.sem, E.at(f"{t}X", i))
                a.activation(X, view(bX), ACT.Copy).then_inc(S.sem, S.one(f"{t}X"))
                if fill:
                    fill(lev)
            if v is not None:
                if not last:
                    v.wait_ge(E.sem, E.at(f"{t}Y", i))
                    v.tensor_tensor(T_, T_, view(bY), ALU.add).then_inc(V.sem, V.one())
                v.wait_ge(E.sem, E.at(f"{t}YT", i))
                v.tensor_tensor(TT, TT, view(bYT), ALU.add).then_inc(V.sem, V.one(f"{t}TT"))
                if fill:
                    fill(lev)

    def rwkv_phase(l):
        NI = KT
        VA, SA, EA = steps("rwA_vec", True), steps("rwA_act", True), steps("rwA_pe", True)
        V, S, E, G = steps("rwB_vec", True), steps("rwB_act", True), steps("rwB_pe", True), steps("rwB_pool", True)
        V0, S0, E0 = steps("rw0_vec"), steps("rw0_act"), steps("rw0_pe")
        loaded = [lsem(f"rw_tile{s}") for s in range(4)]
        pload, wload = lsem("rw_params"), lsem("rw_lora_tiles")
        r_ = Region(BRANCH)
        NC_, NM = len(RWKV_COLS), len(RWKV_MADE)
        par = r_(KT, NC_)
        made = r_(KT, NM)
        lmu, lom = r_(2), r_(2)
        Z = r_(3, T)
        WA, SG = r_(T), r_(T)
        (kkr, sq, sg, cs, cm, Pm, Pp, Pi, rs, aa, kk, kf, kp, rk, nb, NBt, KH, bv, gt, y) = (r_(T) for _ in range(20))
        KR = r_(NB, 2, P)
        BK = r_(4, P)
        Vt, Vh = r_(NB, P), r_(2, NB, P)
        G1, G2 = r_(4, 2, P), r_(4, 2, P)
        NLM = r_(5, 4, P)
        T_, TT, X = r_(4, P), r_(4, P), r_(4, P)
        AVO = r_(4, P)
        Rs, Um, St, SP, t1 = r_(P), r_(P), r_(P), r_(P), r_(P)
        sqo = r_(4, HD)
        mu4, va4 = r_(4), r_(4)
        c = {n: k for k, n in enumerate(RWKV_COLS)}
        cmade = {n: k for k, n in enumerate(RWKV_MADE)}
        b2, b3, b4, b5, b6, b7 = banks[2:8]
        ps_in = [banks[s % 2][:, 0:T] for s in range(3)]
        small = ring[:, 3, 0:2 * P]
        O = AVO[:, 2:4]
        O4 = O.rearrange("p b (h c) -> p (b h) c", h=2)

        def col(i, name):
            return par[:, i, c[name]:c[name] + 1] if name in c else made[:, i, cmade[name]:cmade[name] + 1]

        with nc.Block() as block:
            @block.sync
            def _(sp):
                sp.dma_start(par, A["rwkv_par"][l]).then_inc(pload, 16)
                sp.dma_start(lmu, A["rwkv_lora_par"][l]).then_inc(pload, 16)
                for s in range(2):
                    sp.dma_start(ring[:, 4 + s, :], A["w_rwkv_lora"][l, s]).then_inc(wload, 16)

                def source(i, s):
                    return A["w_rwkv"][l, i, s]

                for s in range(3):
                    sp.dma_start(ring[:, s, :], source(0, s)).then_inc(loaded[s], 16)
                sp.dma_start(small, A["rwkv_up"][l, 0]).then_inc(loaded[3], 16)
                with sp.Fori(1, NI) as i:
                    for s, what in enumerate("rkv"):
                        sp.wait_ge(EA.sem, EA.before(what, i))
                        sp.dma_start(ring[:, s, :], source(i, s)).then_inc(loaded[s], 16)
                    sp.wait_ge(E.sem, E.before("gate", i))
                    sp.dma_start(small, A["rwkv_up"][l, i]).then_inc(loaded[3], 16)

            def pe_piece(te, i, j):
                s, part = divmod(j, 2)
                if part == 0:
                    te.wait_ge(loaded[s], 16 * i + 16)
                    te.wait_ge(VA.sem, VA.at("shift0", i) if s == 2 else VA.before(f"shift{(2, 1)[s]}", i))
                mm = project(te, ps_in[s], s, ks=range(4 * part, 4 * part + 4))
                if part:
                    mm.then_inc(EA.sem, EA.one("rkv"[s]))

            def act_piece(a, i, s):
                if s == 0:
                    a.wait_ge(V.sem, V.before("bv", i))
                    a.wait_ge(E.sem, E.before("vT", i))
                a.wait_ge(EA.sem, EA.at("rkv"[s], i))
                a.activation(Z[:, s, :], ps_in[s], ACT.Copy, scale=col(i, "om_" + "rkv"[s])).then_inc(SA.sem, SA.one(f"z{s}"))

            def vec_piece(v, i, s):
                v.wait_ge(SA.sem, SA.at(f"z{s}", i))
                v.scalar_tensor_tensor(Z[:, s, 1:T], ps_in[s][:, 0:T - 1], col(i, "mu_" + "rkv"[s]), Z[:, s, 1:T],
                                       ALU.mult, ALU.add).then_inc(VA.sem, VA.one(f"shift{s}"))

            def pe_body(te, i, more):
                def fill(n):
                    if more and n < 6:
                        pe_piece(te, i + 1, n)

                if more:
                    EA.begin()
                E.begin()
                rows = lambda q: slice(64 * q, 64 * q + 64)
                te.wait_ge(loaded[3], 16 * i + 16)
                te.wait_ge(V.sem, V.before("y0", i))
                te.matmul(b2[:, 0:T], small[rows(0), 0:P], WA[rows(0), :], start=True, stop=True).then_inc(E.sem, E.one("w"))
                te.matmul(b3[:, 0:T], small[rows(1), 0:P], WA[rows(1), :], start=True, stop=True).then_inc(E.sem, E.one("a"))
                te.matmul(b4[:, 0:T], small[:, P:2 * P], SG, start=True, stop=True).then_inc(E.sem, E.one("gate"))
                te.wait_ge(V.sem, V.at("sq", i))
                te.matmul(b5[:, 0:T], blk64[:], sq, start=True, stop=True).then_inc(E.sem, E.one("ss"))
                for b in range(NB):
                    mm = te.transpose(b6[:, b * P:(b + 1) * P], Z[:, 2, b * P:(b + 1) * P], ident[:])
                mm.then_inc(E.sem, E.one("vT"))
                te.wait_ge(V.sem, V.at("rk", i))
                te.matmul(b7[:, 0:T], blk64[:], rk, start=True, stop=True).then_inc(E.sem, E.one("bonus"))
                te.wait_ge(V.sem, V.at("KH", i))
                for x, src in enumerate((NBt, KH)):
                    for b in range(NB):
                        mm = te.transpose(b5[:, (2 * x + b) * P:(2 * x + b + 1) * P], src[:, b * P:(b + 1) * P], ident[:])
                mm.then_inc(E.sem, E.one("bkT"))
                te.wait_ge(S.sem, S.at("gate", i))
                te.wait_ge(S.sem, S.at("a", i))
                te.wait_ge(V.sem, V.at("bv", i))
                for x, (src, bk) in enumerate(((NBt, (b2, b4)), (KH, (b3, b7)))):
                    for hh in range(2):
                        for b in range(NB):
                            mm = te.matmul(bk[hh][:, b * T:(b + 1) * T], src[rows(hh), b * P:(b + 1) * P],
                                           KR[rows(hh), b], start=True, stop=True)
                        mm.then_inc(E.sem, E.one(f"g{x}{hh}"))
                fill(0)
                te.wait_ge(S.sem, S.at("BK", i))
                te.wait_ge(V.sem, V.at("TT0", i))
                for m in range(4):
                    mm = te.transpose(b5[:, m * P:(m + 1) * P], TT[:, m], ident[:])
                mm.then_inc(E.sem, E.one("T0"))
                te.wait_ge(S.sem, S.at("Vt", i))
                te.wait_ge(V.sem, V.at("m11", i))
                for x in range(2):
                    for b in range(NB):
                        for hh in range(2):
                            mm = te.matmul(b6[:, x * T + b * P + hh * HD:x * T + b * P + hh * HD + HD], G2[:, 2 * hh + b, x],
                                           Vt[:, b, hh * HD:(hh + 1) * HD], start=True, stop=True)
                mm.then_inc(E.sem, E.one("AV"))
                invert_levels(te, None, None, None, "inv", E, S, V, G, i, NLM, T_, TT, X, b2, b3, b4, 6, fill)
                te.wait_ge(V.sem, V.at("inv5TT", i))
                te.wait_ge(S.sem, S.at("AVO", i))
                for q in range(T // CH):
                    b, hf = divmod(q, 2)
                    if q:
                        te.wait_ge(V.sem, V.at(f"S{q - 1}", i))
                        te.matmul(b5[:, 0:P], KR[:, b, 0], St, start=True, stop=True).then_inc(E.sem, E.one(f"R{q}"))
                        te.wait_ge(V.sem, V.at(f"R{q}", i))
                    rhs = Rs if q else AVO[:, 0]
                    for hh in range(2):
                        mm = te.matmul(b7[:, hh * HD:(hh + 1) * HD], TT[:, 2 * hh + b], rhs[:, hh * HD:(hh + 1) * HD],
                                       start=True, stop=True)
                    mm.then_inc(E.sem, E.one(f"U{q}"))
                    if q:
                        te.wait_ge(V.sem, V.at(f"o{q - 1}", i))
                        te.matmul(b3[:, 0:P], KR[:, b, 1], St, start=True, stop=False)
                    te.wait_ge(S.sem, S.at(f"U{q}", i))
                    if q < 3:
                        te.matmul(b2[:, 0:P], BK[:, 2 + b], Vh[:, hf, b], start=True, stop=False)
                        te.matmul(b2[:, 0:P], BK[:, b], Um, start=False, stop=True).then_inc(E.sem, E.one(f"S{q}"))
                    for hh in range(2):
                        mm = te.matmul(b3[:, hh * HD:(hh + 1) * HD], G1[:, 2 * hh + b, 1], Um[:, hh * HD:(hh + 1) * HD],
                                       start=(q == 0), stop=(hh == 1) or q == 0)
                    mm.then_inc(E.sem, E.one(f"O{q}"))
                te.wait_ge(V.sem, V.at("on", i))
                for b in range(NB):
                    mm = te.transpose(b4[:, b * P:(b + 1) * P], O[:, b], ident[:])
                mm.then_inc(E.sem, E.one("yT"))
                E.end()
                if more:
                    EA.end()

            @block.tensor
            def _(te):
                te.wait_ge(wload, 32)
                for s in range(2):
                    project(te, banks[2 + s][:, 0:T], 4 + s).then_inc(E0.sem, E0.one(f"lora{s}"))
                EA.prime(te)
                E.prime(te)
                EA.begin()
                for j in range(6):
                    pe_piece(te, 0, j)
                EA.end()
                te.wait_ge(S0.sem, S0.at("SG"))
                with te.Fori(0, NI - 1) as i:
                    pe_body(te, i, True)
                pe_body(te, NI - 1, False)

            def act_body(a, i, more):
                def fill(n):
                    if more and n in (1, 3, 5):
                        act_piece(a, i + 1, n // 2)

                if more:
                    SA.begin()
                S.begin()
                a.wait_ge(E.sem, E.at("w", i))
                a.activation(sg, b2[:, 0:T], ACT.Sigmoid, bias=col(i, "w0")).then_inc(S.sem, S.one("sg"))
                a.wait_ge(E.sem, E.at("a", i))
                a.activation(aa, b3[:, 0:T], ACT.Sigmoid, bias=col(i, "a0")).then_inc(S.sem, S.one("a"))
                a.wait_ge(E.sem, E.at("gate", i))
                a.wait_ge(V.sem, V.before("y2", i))
                a.activation(gt, b4[:, 0:T], ACT.Copy).then_inc(S.sem, S.one("gate"))
                a.wait_ge(V.sem, V.at("cm", i))
                a.activation(Pp, cs, ACT.Exp, scale=-DECAY).then_inc(S.sem, S.one("Pp"))
                a.activation(Pm, cm, ACT.Exp, scale=-DECAY).then_inc(S.sem, S.one("Pm"))
                a.activation(Pi, cs, ACT.Exp, scale=DECAY).then_inc(S.sem, S.one("Pi"))
                a.wait_ge(V.sem, V.at("rs0", i))
                a.activation(rs, rs, ACT.Sqrt).then_inc(S.sem, S.one("rs"))
                a.wait_ge(E.sem, E.at("vT", i))
                vps = b6[:, 0:2 * P].rearrange("p (b c) -> p b c", b=NB)
                a.activation(Vt, vps, ACT.Copy).then_inc(S.sem, S.one())
                for q in range(2):
                    a.activation(Vh[:, q], vps, ACT.Copy, scale=half[:, q:q + 1]).then_inc(S.sem, S.one("Vt"))
                a.wait_ge(E.sem, E.at("bkT", i))
                a.activation(BK, b5[:, :].rearrange("p (m c) -> p m c", m=4), ACT.Copy).then_inc(S.sem, S.one("BK"))
                a.wait_ge(E.sem, E.at("T0", i))
                a.activation(T_, b5[:, :].rearrange("p (m c) -> p m c", m=4), ACT.Copy).then_inc(S.sem, S.one("invT"))
                a.wait_ge(E.sem, E.at("AV", i))
                a.activation(AVO, b6[:, :].rearrange("p (m c) -> p m c", m=4), ACT.Copy).then_inc(S.sem, S.one("AVO"))
                invert_levels(None, a, None, None, "inv", E, S, V, G, i, NLM, T_, TT, X, b2, b3, b4, 6, fill)
                for q in range(T // CH):
                    a.wait_ge(E.sem, E.at(f"U{q}", i))
                    if q:
                        a.wait_ge(E.sem, E.at(f"O{q - 1}", i))
                    a.activation(Um, b7[:, 0:P], ACT.Copy, scale=half[:, q % 2:q % 2 + 1]).then_inc(S.sem, S.one(f"U{q}"))
                a.wait_ge(V.sem, V.at("var", i))
                a.activation(va4, va4, ACT.Sqrt).then_inc(S.sem, S.one("sd"))
                S.end()
                if more:
                    SA.end()

            @block.scalar
            def _(a):
                a.wait_ge(V0.sem, V0.at("made"))
                for s in range(2):
                    a.wait_ge(E0.sem, E0.at(f"lora{s}"))
                    dst = (WA, SG)[s]
                    a.activation(dst, banks[2 + s][:, 0:T], ACT.Copy, scale=lom[:, s:s + 1]).then_inc(S0.sem, S0.one(f"l{s}"))
                a.wait_ge(V0.sem, V0.at("shift1"))
                a.activation(WA[0:64, :], WA[0:64, :], ACT.Tanh).then_inc(S0.sem, S0.one())
                a.activation(SG, SG, ACT.Sigmoid).then_inc(S0.sem, S0.one("SG"))
                SA.prime(a)
                S.prime(a)
                SA.begin()
                for s in range(3):
                    act_piece(a, 0, s)
                SA.end()
                with a.Fori(0, NI - 1) as i:
                    act_body(a, i, True)
                act_body(a, NI - 1, False)

            def vec_body(v, i, more):
                def fill(n):
                    if more and n in (1, 3, 5):
                        vec_piece(v, i + 1, n // 2)

                tt = lambda o, a0, a1, op, label=None: v.tensor_tensor(o, a0, a1, op).then_inc(V.sem, V.one(label))
                if more:
                    VA.begin()
                V.begin()
                v.wait_ge(VA.sem, VA.at("shift2", i))
                v.tensor_scalar(kkr, Z[:, 1], col(i, "k_k"), None, ALU.mult).then_inc(V.sem, V.one())
                v.wait_ge(V.sem, V.now(i))
                v.tensor_tensor(sq, kkr, kkr, ALU.mult).then_inc(V.sem, V.one("sq"))
                v.wait_ge(S.sem, S.at("sg", i))
                v.tensor_tensor_scan(cs, restart[:], sg, 0.0, ALU.mult, ALU.add).then_inc(V.sem, V.one())
                v.wait_ge(V.sem, V.now(i))
                v.tensor_tensor(cm, cs, sg, ALU.subtract).then_inc(V.sem, V.one("cm"))
                v.wait_ge(E.sem, E.at("ss", i))
                v.tensor_scalar(rs, b5[:, 0:T], EPS, None, ALU.add).then_inc(V.sem, V.one("rs0"))
                v.wait_ge(S.sem, S.at("a", i))
                v.tensor_scalar(kf, aa, col(i, "k_a"), col(i, "om_ka"), ALU.mult, ALU.add).then_inc(V.sem, V.one())
                v.wait_ge(V.sem, V.now(i))
                v.tensor_tensor(kp, Z[:, 1], kf, ALU.mult).then_inc(V.sem, V.one())
                v.wait_ge(V.sem, V.now(i))
                v.scalar_tensor_tensor(rk, Z[:, 0], col(i, "r_k"), kp, ALU.mult, ALU.mult).then_inc(V.sem, V.one("rk"))
                two = lambda x: x.rearrange("p (b c) -> p b c", b=NB)
                v.wait_ge(S.sem, S.at("Pi", i))
                v.tensor_tensor(KR[:, :, 1], two(Z[:, 0]), two(Pp), ALU.mult).then_inc(V.sem, V.one())
                v.wait_ge(S.sem, S.at("rs", i))
                v.reciprocal(rs, rs).then_inc(V.sem, V.one())
                v.wait_ge(V.sem, V.now(i))
                v.tensor_tensor(kk, kkr, rs, ALU.mult).then_inc(V.sem, V.one())
                v.wait_ge(V.sem, V.now(i))
                v.tensor_tensor(KR[:, :, 0], two(kk), two(Pm), ALU.mult).then_inc(V.sem, V.one())
                v.scalar_tensor_tensor(nb, kk, -1.0, aa, ALU.mult, ALU.mult).then_inc(V.sem, V.one())
                v.wait_ge(V.sem, V.now(i))
                v.tensor_tensor(NBt, nb, Pi, ALU.mult).then_inc(V.sem, V.one())
                v.tensor_tensor(KH, kp, Pi, ALU.mult).then_inc(V.sem, V.one("KH"))
                v.wait_ge(E.sem, E.at("bonus", i))
                v.tensor_tensor(bv, b7[:, 0:T], Z[:, 2], ALU.mult).then_inc(V.sem, V.one("bv"))
                for x, (dst, bk) in enumerate(((G1, (b2, b4)), (G2, (b3, b7)))):
                    for hh in range(2):
                        v.wait_ge(E.sem, E.at(f"g{x}{hh}", i))
                        v.tensor_tensor(dst[:, 2 * hh:2 * hh + 2].rearrange("p b x c -> p b (x c)"),
                                        bk[hh][:, :].rearrange("p (b c) -> p b c", b=NB),
                                        rmask[:].rearrange("p x c -> p (x c)").unsqueeze(1).to_broadcast([P, NB, 2 * P]),
                                        ALU.mult).then_inc(V.sem, V.one(f"m{x}{hh}"))
                    if x == 0:
                        v.wait_ge(V.sem, V.now(i))
                        v.tensor_tensor(TT, G1[:, :, 0], lmask[:, 0].unsqueeze(1).to_broadcast([P, 4, P]), ALU.mult)\
                            .then_inc(V.sem, V.one())
                        v.wait_ge(V.sem, V.now(i))
                        v.tensor_tensor(TT, TT, ident[:].unsqueeze(1).to_broadcast([P, 4, P]), ALU.add)\
                            .then_inc(V.sem, V.one("TT0"))
                v.wait_ge(S.sem, S.at("invT", i))
                invert_levels(None, None, v, None, "inv", E, S, V, G, i, NLM, T_, TT, X, b2, b3, b4, 6, fill)
                for q in range(T // CH):
                    b, hf = divmod(q, 2)
                    end = Pp[:, q * CH + CH - 1:q * CH + CH]
                    if q:
                        v.wait_ge(E.sem, E.at(f"R{q}", i))
                        v.tensor_tensor(Rs, b5[:, 0:P], AVO[:, b], ALU.add).then_inc(V.sem, V.one(f"R{q}"))
                        if q < 3:
                            v.tensor_scalar(SP, St, end, None, ALU.mult).then_inc(V.sem, V.one())
                    if q < 3:
                        v.wait_ge(E.sem, E.at(f"S{q}", i))
                        v.tensor_tensor(t1, b2[:, 0:P], blk64[:], ALU.mult).then_inc(V.sem, V.one("t1"))
                        v.wait_ge(V.sem, V.now(i))
                        if q:
                            v.scalar_tensor_tensor(St, t1, end, SP, ALU.mult, ALU.add).then_inc(V.sem, V.one(f"S{q}"))
                        else:
                            v.tensor_scalar(St, t1, end, None, ALU.mult).then_inc(V.sem, V.one(f"S{q}"))
                    v.wait_ge(E.sem, E.at(f"O{q}", i))
                    v.wait_ge(S.sem, S.at("AVO", i))
                    v.scalar_tensor_tensor(O[:, b], b3[:, 0:P], half[:, hf:hf + 1], O[:, b], ALU.mult, ALU.add)\
                        .then_inc(V.sem, V.one(f"o{q}"))
                bc = lambda x: x.unsqueeze(2).to_broadcast([P, 4, HD])
                v.wait_ge(V.sem, V.now(i))
                v.tensor_reduce(mu4, O4, AX.X, ALU.add).then_inc(V.sem, V.one())
                v.wait_ge(V.sem, V.now(i))
                v.tensor_scalar(mu4, mu4, -1.0 / HD, None, ALU.mult).then_inc(V.sem, V.one())
                v.wait_ge(V.sem, V.now(i))
                v.tensor_tensor(O4, O4, bc(mu4), ALU.add).then_inc(V.sem, V.one())
                v.wait_ge(V.sem, V.now(i))
                v.tensor_tensor(sqo, O4, O4, ALU.mult).then_inc(V.sem, V.one())
                v.wait_ge(V.sem, V.now(i))
                v.tensor_reduce(va4, sqo, AX.X, ALU.add).then_inc(V.sem, V.one())
                v.wait_ge(V.sem, V.now(i))
                v.tensor_scalar(va4, va4, 1.0 / HD, GN_EPS, ALU.mult, ALU.add).then_inc(V.sem, V.one("var"))
                v.wait_ge(S.sem, S.at("sd", i))
                v.reciprocal(va4, va4).then_inc(V.sem, V.one())
                v.wait_ge(V.sem, V.now(i))
                v.tensor_tensor(O4, O4, bc(va4), ALU.mult).then_inc(V.sem, V.one("on"))
                v.wait_ge(E.sem, E.at("yT", i))
                v.tensor_scalar(y, b4[:, 0:T], col(i, "ln_w"), col(i, "ln_b"), ALU.mult, ALU.add).then_inc(V.sem, V.one("y0"))
                v.wait_ge(V.sem, V.now(i))
                v.tensor_tensor(y, y, bv, ALU.add).then_inc(V.sem, V.one())
                v.wait_ge(V.sem, V.now(i))
                v.tensor_tensor(yc[:, i], y, gt, ALU.mult).then_inc(V.sem, V.one("y2"))
                V.end()
                if more:
                    VA.end()

            @block.vector
            def _(v):
                v.wait_ge(pload, 32)
                v.tensor_scalar(made[:, :, 0:3], par[:, :, 0:3], -1.0, 1.0, ALU.mult, ALU.add).then_inc(V0.sem, V0.one())
                v.tensor_scalar(made[:, :, 3], par[:, :, c["k_a"]], -1.0, 1.0, ALU.mult, ALU.add).then_inc(V0.sem, V0.one())
                v.tensor_scalar(lom, lmu, -1.0, 1.0, ALU.mult, ALU.add).then_inc(V0.sem, V0.one("made"))
                for s in range(2):
                    dst = (WA, SG)[s]
                    v.wait_ge(S0.sem, S0.at(f"l{s}"))
                    v.scalar_tensor_tensor(dst[:, 1:T], banks[2 + s][:, 0:T - 1], lmu[:, s:s + 1], dst[:, 1:T],
                                           ALU.mult, ALU.add).then_inc(V0.sem, V0.one(f"shift{s}"))
                VA.prime(v)
                V.prime(v)
                VA.begin()
                for s in range(3):
                    vec_piece(v, 0, s)
                VA.end()
                with v.Fori(0, NI - 1) as i:
                    vec_body(v, i, True)
                vec_body(v, NI - 1, False)

            def pool_body(g, i):
                G.begin()
                g.wait_ge(V.sem, V.at("m01", i))
                for lev in range(1, 6):
                    g.tensor_tensor(NLM[:, lev - 1], G1[:, :, 0], lmask[:, lev].unsqueeze(1).to_broadcast([P, 4, P]), ALU.mult)\
                        .then_inc(G.sem, G.one(f"inv{lev}mask"))
                G.end()

            @block.gpsimd
            def _(g):
                G.prime(g)
                with g.Fori(0, NI) as i:
                    pool_body(g, i)

    def gdn_phase(l):
        NI = 4
        VA, SA, EA = steps("gdA_vec", True), steps("gdA_act", True), steps("gdA_pe", True)
        V, S, E, G = steps("gdB_vec", True), steps("gdB_act", True), steps("gdB_pe", True), steps("gdB_pool", True)
        V0, S0, E0 = steps("gd0_vec"), steps("gd0_act"), steps("gd0_pe")
        loaded = [lsem(f"gd_tile{s}") for s in range(8)]
        pload = lsem("gd_params")
        r_ = Region(BRANCH)
        par = r_(8, 12)
        nw = r_(1)
        wab = r_(KT, 16)
        rows = r_(2, 8, 2)
        ab = r_(NB, 16)
        al, ea, e0, z0, z1, m0 = (r_(8, 2) for _ in range(6))
        GA = r_(4, 16)
        st = r_(4, 4)
        Z = r_(8, T)
        GZ = r_(2, T)
        GB = r_(2, 4, P)
        sq, rs = r_(4, T), r_(4, T)
        KQ = r_(4, 2, P)
        KN, DT, DTs, DTi, eg, nkbe, qe = (r_(4, P) for _ in range(7))
        NLT, QKT, Kt, Vt = r_(4, P), r_(4, P), r_(4, P), r_(4, P)
        NLM = r_(6, 4, P)
        T_, TT, X = r_(4, P), r_(4, P), r_(4, P)
        Us, Rs, St = r_(2, P), r_(2, P), r_(2, P)
        O = r_(NB, 2, P)
        O4 = O.rearrange("p b h c -> p (b h) c")
        va4 = r_(4)
        b2, b3, b4, b5, b6, b7 = banks[2:8]
        four = lambda b: b[:, :].rearrange("p (m c) -> p m c", m=4)
        qs = Z[:, 0:2].rearrange("p h (b c) -> p (h b) c", b=NB)
        ks = Z[:, 2:4].rearrange("p h (b c) -> p (h b) c", b=NB)
        rsq = rs[:, 0:2].rearrange("p h (b c) -> p (h b) c", b=NB)
        rsk = rs[:, 2:4].rearrange("p h (b c) -> p (h b) c", b=NB)
        bc4 = lambda x: x.unsqueeze(1).to_broadcast([P, 4, P])

        with nc.Block() as block:
            @block.sync
            def _(sp):
                sp.dma_start(wab, A["gdn_ab"][l]).then_inc(pload, 16)
                sp.dma_start(par, A["gdn_par"][l]).then_inc(pload, 16)
                sp.dma_start(nw, A["gdn_norm"][l]).then_inc(pload, 16)
                sp.dma_start(rows, A["gdn_rows"][l]).then_inc(pload, 16)
                load_slots(sp, lambda i, s: A["w_gdn"][l, i, s], loaded, EA, [f"z{s}" for s in range(8)], NI)

            def pe_piece(te, i, s):
                te.wait_ge(loaded[s], 16 * i + 16)
                if s < 2:
                    te.wait_ge(SA.sem, SA.before(f"z{6 + s}", i))
                else:
                    te.wait_ge(VA.sem, VA.at(f"tap3_{s - 2}", i))
                project(te, banks[s % 2][:, 0:T], s).then_inc(EA.sem, EA.one(f"z{s}"))

            def act_piece(a, i, s):
                if s == 0:
                    a.wait_ge(V.sem, V.before("KN", i))
                    a.wait_ge(E.sem, E.before("vT", i))
                a.wait_ge(EA.sem, EA.at(f"z{s}", i))
                if s < 6:
                    w3 = par[:, 2 * i + s % 2, 4 * (s // 2) + 3:4 * (s // 2) + 4]
                    a.activation(Z[:, s, :], banks[s % 2][:, 0:T], ACT.Copy, scale=w3).then_inc(SA.sem, SA.one(f"z{s}"))
                else:
                    a.activation(Z[:, s, :], banks[s % 2][:, 0:T], ACT.Copy).then_inc(SA.sem, SA.one(f"z{s}"))

            def vec_piece(v, i, s):
                if s >= 6:
                    return
                v.wait_ge(SA.sem, SA.at(f"z{s}", i))
                for sh in (1, 2, 3):
                    if sh > 1:
                        v.wait_ge(VA.sem, VA.now(i))
                    tap = 4 * (s // 2) + 3 - sh
                    v.scalar_tensor_tensor(Z[:, s, sh:T], banks[s % 2][:, 0:T - sh], par[:, 2 * i + s % 2, tap:tap + 1],
                                           Z[:, s, sh:T], ALU.mult, ALU.add).then_inc(VA.sem, VA.one(f"tap{sh}_{s}"))

            def pe_body(te, i, more):
                def fill(n):
                    if more:
                        pe_piece(te, i + 1, n)

                if more:
                    EA.begin()
                E.begin()
                te.wait_ge(V.sem, V.before("y", i))
                te.wait_ge(V.sem, V.at("sq", i))
                for x, bk in enumerate((b2, b3)):
                    te.matmul(bk[:, :], ones[:], sq[:, 2 * x:2 * x + 2], start=True, stop=True).then_inc(E.sem, E.one(f"ss{x}"))
                for x, (bk, m) in enumerate(((b4, upto), (b5, ident))):
                    for q in range(4):
                        mm = te.matmul(four(bk)[:, q], GB[:, x, q], m[:], start=True, stop=True)
                    mm.then_inc(E.sem, E.one(("gcrow", "brow")[x]))
                for q in range(4):
                    mm = te.transpose(four(b7)[:, q], Z[:, 4 + q // 2, (q % 2) * P:(q % 2 + 1) * P], ident[:])
                mm.then_inc(E.sem, E.one("vT"))
                te.wait_ge(V.sem, V.at("KN", i))
                for q in range(4):
                    mm = te.transpose(four(b6)[:, q], KN[:, q], ident[:])
                mm.then_inc(E.sem, E.one("kT"))
                te.wait_ge(V.sem, V.at("kb", i))
                for q in range(4):
                    bk = (b2, b3)[q // 2]
                    mm = te.matmul(bk[:, (q % 2) * T:(q % 2 + 1) * T], KN[:, q], KQ[:, q], start=True, stop=True)
                    if q % 2:
                        mm.then_inc(E.sem, E.one(f"g{q // 2}"))
                fill(0)
                te.wait_ge(S.sem, S.at("eg", i))
                te.wait_ge(V.sem, V.at("TT0", i))
                for q in range(4):
                    mm = te.transpose(four(b4)[:, q], TT[:, q], ident[:])
                mm.then_inc(E.sem, E.one("T0"))
                te.wait_ge(V.sem, V.at("QKT", i))
                invert_levels(te, None, None, None, "inv", E, S, V, G, i, NLM, T_, TT, X, b5, b2, b3, N_LEVELS, fill)
                te.wait_ge(V.sem, V.at("inv6TT", i))
                te.wait_ge(S.sem, S.at("Vt", i))
                two = lambda b: b[:, 0:2 * P].rearrange("p (h c) -> p h c", h=2)
                for hh in range(2):
                    mm = te.matmul(two(b6)[:, hh], TT[:, 2 * hh], Vt[:, 2 * hh], start=True, stop=True)
                mm.then_inc(E.sem, E.one("U0"))
                te.wait_ge(S.sem, S.at("U0", i))
                for hh in range(2):
                    mm = te.matmul(two(b4)[:, hh], Kt[:, 2 * hh], Us[:, hh], start=True, stop=True)
                mm.then_inc(E.sem, E.one("S"))
                for hh in range(2):
                    mm = te.matmul(two(b7)[:, hh], QKT[:, 2 * hh], Us[:, hh], start=True, stop=True)
                mm.then_inc(E.sem, E.one("O0"))
                te.wait_ge(S.sem, S.at("S", i))
                for hh in range(2):
                    mm = te.matmul(two(b5)[:, hh], nkbe[:, 2 * hh + 1], St[:, hh], start=True, stop=True)
                mm.then_inc(E.sem, E.one("R"))
                fill(7)
                te.wait_ge(V.sem, V.at("R", i))
                for hh in range(2):
                    mm = te.matmul(two(b6)[:, hh], TT[:, 2 * hh + 1], Rs[:, hh], start=True, stop=True)
                mm.then_inc(E.sem, E.one("U1"))
                te.wait_ge(S.sem, S.at("U1", i))
                for hh in range(2):
                    te.matmul(two(b2)[:, hh], qe[:, 2 * hh + 1], St[:, hh], start=True, stop=False)
                    mm = te.matmul(two(b2)[:, hh], QKT[:, 2 * hh + 1], Us[:, hh], start=False, stop=True)
                mm.then_inc(E.sem, E.one("O1"))
                te.wait_ge(V.sem, V.at("on", i))
                for hh in range(2):
                    for b in range(NB):
                        mm = te.transpose(four(b3)[:, 2 * hh + b], O[:, b, hh], ident[:])
                mm.then_inc(E.sem, E.one("yT"))
                E.end()
                if more:
                    EA.end()

            @block.tensor
            def _(te):
                te.wait_ge(pload, 64)
                for b in range(NB):
                    for k in range(KT):
                        mm = te.matmul(b2[:, 16 * b:16 * b + 16], xn[:, k, b * P:(b + 1) * P], wab[:, k], start=(k == 0), stop=(k == KT - 1))
                mm.then_inc(E0.sem, E0.one("ab"))
                EA.prime(te)
                E.prime(te)
                EA.begin()
                for s in range(8):
                    pe_piece(te, 0, s)
                EA.end()
                te.wait_ge(V0.sem, V0.at("g"))
                te.matmul(b3[:, 0:16], upto[:], GA[:, 0], start=True, stop=True)
                te.matmul(b3[:, 16:32], after[:], GA[:, 0], start=True, stop=True).then_inc(E0.sem, E0.one("gc"))
                te.wait_ge(S0.sem, S0.at("erev"))
                with te.Fori(0, NI - 1) as i:
                    pe_body(te, i, True)
                pe_body(te, NI - 1, False)

            def act_body(a, i, more):
                def fill(n):
                    if more:
                        act_piece(a, i + 1, n)

                if more:
                    SA.begin()
                S.begin()
                a.wait_ge(SA.sem, SA.at("z7", i))
                a.wait_ge(VA.sem, VA.at("tap3_5", i))
                a.wait_ge(V.sem, V.before("y", i))
                a.activation(Z[:, 0:6], Z[:, 0:6], ACT.Silu).then_inc(S.sem, S.one("silu"))
                a.activation(GZ, Z[:, 6:8], ACT.Silu).then_inc(S.sem, S.one("siluz"))
                a.wait_ge(V.sem, V.at("rs0", i))
                a.activation(rs, rs, ACT.Sqrt).then_inc(S.sem, S.one("rs"))
                a.wait_ge(V.sem, V.at("DT0", i))
                a.activation(DT, DT, ACT.Exp).then_inc(S.sem, S.one("DT"))
                a.activation(eg, four(b4), ACT.Exp).then_inc(S.sem, S.one("eg"))
                a.wait_ge(E.sem, E.at("vT", i))
                for q in range(4):
                    a.activation(Vt[:, q], four(b7)[:, q], ACT.Copy, scale=st[:, 1, q:q + 1]).then_inc(S.sem, S.one("Vt"))
                a.wait_ge(E.sem, E.at("kT", i))
                for q in range(4):
                    a.activation(Kt[:, q], four(b6)[:, q], ACT.Copy, scale=st[:, 3, q:q + 1]).then_inc(S.sem, S.one("Kt"))
                fill(0)
                a.wait_ge(E.sem, E.at("T0", i))
                a.activation(T_, four(b4), ACT.Copy).then_inc(S.sem, S.one("invT"))
                invert_levels(None, a, None, None, "inv", E, S, V, G, i, NLM, T_, TT, X, b5, b2, b3, N_LEVELS, fill)
                two = lambda b: b[:, 0:2 * P].rearrange("p (h c) -> p h c", h=2)
                a.wait_ge(E.sem, E.at("U0", i))
                a.activation(Us, two(b6), ACT.Copy).then_inc(S.sem, S.one("U0"))
                a.wait_ge(E.sem, E.at("S", i))
                a.activation(St, two(b4), ACT.Copy).then_inc(S.sem, S.one("S"))
                a.wait_ge(E.sem, E.at("O0", i))
                a.activation(O[:, 0], two(b7), ACT.Copy).then_inc(S.sem, S.one("O0"))
                fill(7)
                a.wait_ge(E.sem, E.at("U1", i))
                a.activation(Us, two(b6), ACT.Copy).then_inc(S.sem, S.one("U1"))
                a.wait_ge(E.sem, E.at("O1", i))
                a.activation(O[:, 1], two(b2), ACT.Copy).then_inc(S.sem, S.one("O1"))
                a.wait_ge(V.sem, V.at("var", i))
                a.activation(va4, va4, ACT.Sqrt).then_inc(S.sem, S.one("sd"))
                S.end()
                if more:
                    SA.end()

            @block.scalar
            def _(a):
                a.wait_ge(pload, 64)
                a.wait_ge(E0.sem, E0.at("ab"))
                a.activation(ab, b2[:, 0:32].rearrange("p (b j) -> p b j", b=NB), ACT.Copy).then_inc(S0.sem, S0.one("ab"))
                a.activation(ea, rows[:, 0], ACT.Exp).then_inc(S0.sem, S0.one())
                a.wait_ge(V0.sem, V0.at("al"))
                softplus_exp(a, S0, al, e0, "sp")
                a.activation(GA[:, 1].rearrange("p (h b) -> p h b", b=NB), ab[:, :, 8:16].rearrange("p b h -> p h b"),
                             ACT.Sigmoid).then_inc(S0.sem, S0.one("beta"))
                SA.prime(a)
                S.prime(a)
                SA.begin()
                for s in range(8):
                    act_piece(a, 0, s)
                SA.end()
                a.wait_ge(E0.sem, E0.at("gc"))
                a.activation(GA[:, 2], b3[:, 0:16], ACT.Copy).then_inc(S0.sem, S0.one())
                a.activation(GA[:, 3], b3[:, 16:32], ACT.Exp).then_inc(S0.sem, S0.one("erev"))
                with a.Fori(0, NI - 1) as i:
                    act_body(a, i, True)
                act_body(a, NI - 1, False)

            def vec_body(v, i, more):
                def fill(n):
                    if more:
                        vec_piece(v, i + 1, n)

                if more:
                    VA.begin()
                V.begin()
                v.wait_ge(S.sem, S.before("Kt", i))
                v.tensor_copy(st, GA[:, :, bass.ds(4 * i, 4)]).then_inc(V.sem, V.one("st"))
                v.wait_ge(V.sem, V.now(i))
                v.tensor_copy(GB, st[:, 0:2].unsqueeze(3).to_broadcast([P, 2, 4, P])).then_inc(V.sem, V.one("GB"))
                v.wait_ge(S.sem, S.at("silu", i))
                v.tensor_tensor(sq, Z[:, 0:4], Z[:, 0:4], ALU.mult).then_inc(V.sem, V.one("sq"))
                for x, bk in enumerate((b2, b3)):
                    v.wait_ge(E.sem, E.at(f"ss{x}", i))
                    v.tensor_scalar(rs[:, 2 * x:2 * x + 2], bk[:, :].rearrange("p (h t) -> p h t", h=2), EPS, None, ALU.add)\
                        .then_inc(V.sem, V.one("rs0"))
                v.wait_ge(E.sem, E.at("gcrow", i))
                for q in range(4):
                    v.tensor_scalar(DT[:, q], four(b4)[:, q], st[:, 2, q:q + 1], 0.0, ALU.subtract, ALU.min)\
                        .then_inc(V.sem, V.one("DT0"))
                v.wait_ge(S.sem, S.at("rs", i))
                v.reciprocal(rs, rs).then_inc(V.sem, V.one())
                v.wait_ge(V.sem, V.now(i))
                v.tensor_tensor(KN, ks, rsk, ALU.mult).then_inc(V.sem, V.one())
                v.scalar_tensor_tensor(KQ[:, :, 1], qs, GDN_SCALE, rsq, ALU.mult, ALU.mult).then_inc(V.sem, V.one("KN"))
                v.wait_ge(V.sem, V.now(i))
                v.wait_ge(E.sem, E.at("brow", i))
                v.tensor_tensor(KQ[:, :, 0], KN, four(b5), ALU.mult).then_inc(V.sem, V.one("kb"))
                v.wait_ge(S.sem, S.at("DT", i))
                v.tensor_tensor(DTs, DT, bc4(gmask[:, 0]), ALU.mult).then_inc(V.sem, V.one())
                v.tensor_tensor(DTi, DT, bc4(gmask[:, 1]), ALU.mult).then_inc(V.sem, V.one())
                v.wait_ge(V.sem, V.now(i))
                for x, bk in enumerate((b2, b3)):
                    ps = bk[:, :].rearrange("p (m x c) -> p m x c", m=2, x=2)
                    v.wait_ge(E.sem, E.at(f"g{x}", i))
                    v.scalar_tensor_tensor(NLT[:, 2 * x:2 * x + 2], ps[:, :, 0], -1.0, DTs[:, 2 * x:2 * x + 2], ALU.mult, ALU.mult)\
                        .then_inc(V.sem, V.one(f"NLT{x}"))
                v.wait_ge(V.sem, V.now(i))
                v.tensor_tensor(TT, NLT, bc4(lmask[:, 0]), ALU.mult).then_inc(V.sem, V.one())
                v.wait_ge(V.sem, V.now(i))
                v.tensor_tensor(TT, TT, bc4(ident[:]), ALU.add).then_inc(V.sem, V.one("TT0"))
                for x, bk in enumerate((b2, b3)):
                    ps = bk[:, :].rearrange("p (m x c) -> p m x c", m=2, x=2)
                    v.tensor_tensor(QKT[:, 2 * x:2 * x + 2], ps[:, :, 1], DTi[:, 2 * x:2 * x + 2], ALU.mult)\
                        .then_inc(V.sem, V.one("QKT"))
                v.wait_ge(S.sem, S.at("eg", i))
                v.scalar_tensor_tensor(nkbe, KQ[:, :, 0], -1.0, eg, ALU.mult, ALU.mult).then_inc(V.sem, V.one())
                v.tensor_tensor(qe, KQ[:, :, 1], eg, ALU.mult).then_inc(V.sem, V.one("qe"))
                fill(0)
                v.wait_ge(S.sem, S.at("invT", i))
                invert_levels(None, None, v, None, "inv", E, S, V, G, i, NLM, T_, TT, X, b5, b2, b3, N_LEVELS, fill)
                two = lambda b: b[:, 0:2 * P].rearrange("p (h c) -> p h c", h=2)
                v.wait_ge(E.sem, E.at("R", i))
                v.wait_ge(S.sem, S.at("Vt", i))
                v.tensor_tensor(Rs, two(b5), Vt.rearrange("p (h b) c -> p h b c", h=2)[:, :, 1], ALU.add).then_inc(V.sem, V.one("R"))
                fill(7)
                v.wait_ge(S.sem, S.at("O1", i))
                v.tensor_tensor(eg, O4, O4, ALU.mult).then_inc(V.sem, V.one())
                v.wait_ge(V.sem, V.now(i))
                v.tensor_reduce(va4, eg, AX.X, ALU.add).then_inc(V.sem, V.one())
                v.wait_ge(V.sem, V.now(i))
                v.tensor_scalar(va4, va4, 1.0 / P, EPS, ALU.mult, ALU.add).then_inc(V.sem, V.one("var"))
                v.wait_ge(S.sem, S.at("sd", i))
                v.reciprocal(va4, va4).then_inc(V.sem, V.one())
                v.wait_ge(V.sem, V.now(i))
                v.tensor_tensor(O4, O4, va4.unsqueeze(2).to_broadcast([P, 4, P]), ALU.mult).then_inc(V.sem, V.one("on"))
                v.wait_ge(E.sem, E.at("yT", i))
                v.scalar_tensor_tensor(yb[:, bass.ds(2 * i, 2)], b3[:, :].rearrange("p (h t) -> p h t", h=2), nw, GZ, ALU.mult, ALU.mult)\
                    .then_inc(V.sem, V.one("y"))
                V.end()
                if more:
                    VA.end()

            @block.vector
            def _(v):
                v.wait_ge(pload, 64)
                v.wait_ge(S0.sem, S0.at("ab"))
                v.tensor_tensor(al, ab[:, :, 0:8].rearrange("p b h -> p h b"), rows[:, 1], ALU.add).then_inc(V0.sem, V0.one("al"))
                v.wait_ge(V0.sem, V0.now())
                v.wait_ge(S0.sem, S0.at("sp_e"))
                softplus_log(v, V0, al, e0, z0, z1, m0, e0)
                v.wait_ge(V0.sem, V0.now())
                v.scalar_tensor_tensor(GA[:, 0].rearrange("p (h b) -> p h b", b=NB), m0, -1.0, ea, ALU.mult, ALU.mult)\
                    .then_inc(V0.sem, V0.one("g"))
                v.wait_ge(S0.sem, S0.at("beta"))
                VA.prime(v)
                V.prime(v)
                VA.begin()
                for s in range(8):
                    vec_piece(v, 0, s)
                VA.end()
                v.wait_ge(S0.sem, S0.at("erev"))
                with v.Fori(0, NI - 1) as i:
                    vec_body(v, i, True)
                vec_body(v, NI - 1, False)

            @block.gpsimd
            def _(g):
                G.prime(g)
                with g.Fori(0, NI) as i:
                    G.begin()
                    g.wait_ge(V.sem, V.at("NLT1", i))
                    for lev in range(1, N_LEVELS):
                        g.tensor_tensor(NLM[:, lev - 1], NLT, bc4(lmask[:, lev]), ALU.mult).then_inc(G.sem, G.one(f"inv{lev}mask"))
                    G.end()

    def merge_phase(l):
        V, S, E = steps("mg_vec", True), steps("mg_act", True), steps("mg_pe", True)
        V2, E2 = steps("wo_vec", True), steps("wo_pe", True)
        loaded = [lsem(f"mg_tile{s}") for s in range(6)]
        loaded2 = [lsem(f"wo_tile{s}") for s in range(2)]
        pload = lsem("mg_params")
        r_ = Region(BRANCH)
        mb = r_(3, KT)
        gate, t = r_(3, T), r_(3, T)
        merged = r_(KT, T)
        ys = (ya, yb, yc)
        with nc.Block() as block:
            @block.sync
            def _(sp):
                sp.dma_start(mb, A["merge_b"][l]).then_inc(pload, 16)
                for s in range(2):
                    sp.dma_start(ring[:, 6 + s, :], A["w_out"][l, 0, s]).then_inc(loaded2[s], 16)
                load_slots(sp, lambda i, s: A["w_merge"][l, i, s], loaded, E, [f"z{s}" for s in range(6)], KT)
                with sp.Fori(1, KT // 2) as i:
                    for s in range(2):
                        sp.wait_ge(E2.sem, E2.before(f"o{s}", i))
                        sp.dma_start(ring[:, 6 + s, :], A["w_out"][l, i, s]).then_inc(loaded2[s], 16)

            @block.tensor
            def _(te):
                E.prime(te)
                with te.Fori(0, KT) as i:
                    E.begin()
                    for s in range(6):
                        te.wait_ge(loaded[s], 16 * i + 16)
                        if s % 2:
                            te.wait_ge(V.sem, V.before(f"t{s // 2}", i))
                        else:
                            te.wait_ge(S.sem, S.before(f"g{s // 2}", i))
                        project(te, banks[s][:, 0:T], s, ys[s // 2] if s % 2 else xn).then_inc(E.sem, E.one(f"z{s}"))
                    E.end()
                te.wait_ge(V.sem, V.at("merged", KT - 1))
                E2.prime(te)
                with te.Fori(0, KT // 2) as i:
                    E2.begin()
                    for s in range(2):
                        te.wait_ge(loaded2[s], 16 * i + 16)
                        te.wait_ge(V2.sem, V2.before(f"h{s}", i))
                        project(te, banks[6 + s][:, 0:T], 6 + s, merged).then_inc(E2.sem, E2.one(f"o{s}"))
                    E2.end()

            @block.scalar
            def _(a):
                a.wait_ge(pload, 16)
                S.prime(a)
                with a.Fori(0, KT) as i:
                    S.begin()
                    for x in range(3):
                        a.wait_ge(E.sem, E.at(f"z{2 * x}", i))
                        a.wait_ge(V.sem, V.before(f"t{x}", i))
                        a.activation(gate[:, x], banks[2 * x][:, 0:T], ACT.Sigmoid, bias=mb[:, x, bass.ds(i, 1)])\
                            .then_inc(S.sem, S.one(f"g{x}"))
                    S.end()

            @block.vector
            def _(v):
                V.prime(v)
                V2.prime(v)
                with v.Fori(0, KT) as i:
                    V.begin()
                    for x in range(3):
                        v.wait_ge(S.sem, S.at(f"g{x}", i))
                        v.wait_ge(E.sem, E.at(f"z{2 * x + 1}", i))
                        v.tensor_tensor(t[:, x], gate[:, x], banks[2 * x + 1][:, 0:T], ALU.mult).then_inc(V.sem, V.one(f"t{x}"))
                        if x == 1:
                            v.wait_ge(V.sem, V.now(i))
                            v.tensor_tensor(t[:, 0], t[:, 0], t[:, 1], ALU.add).then_inc(V.sem, V.one())
                    v.wait_ge(V.sem, V.now(i))
                    v.tensor_tensor(merged[:, i], t[:, 0], t[:, 2], ALU.add).then_inc(V.sem, V.one("merged"))
                    v.wait_ge(V.sem, V.now(i))
                    V.end()
                with v.Fori(0, KT // 2) as i:
                    V2.begin()
                    for s in range(2):
                        v.wait_ge(E2.sem, E2.at(f"o{s}", i))
                        v.tensor_tensor(h[:, 2 * i + s], h[:, 2 * i + s], banks[6 + s][:, 0:T], ALU.add).then_inc(V2.sem, V2.one(f"h{s}"))
                    V2.end()
                v.wait_ge(V2.sem, V2.at("h1", KT // 2 - 1))

    PQ = Region(PEER)
    scores = PQ(NB, 2 * PH, NK)
    slots = sb("slots", [P, 3, T])
    slot1, slot2, slotg = (slots[:, n] for n in range(3))
    xhigh = sb("xhigh", [P, KT, T])
    xlow = sb("xlow", [P, KT, T])
    act_low = sb("act_low", [P, 2, T])
    act_high = sb("act_high", [P, 2, T])
    f32r = lambda ap: ap.bitcast(F32R)

    def peer_query_phase(l):
        NI = 4
        V, S, E = steps("pq_vec", True), steps("pq_act", True), steps("pq_pe", True)
        loaded = [lsem(f"pq_tile{s}") for s in range(4)]
        pload = lsem("pq_keys")
        x_high, x_low = lsem("pq_x_high"), lsem("pq_x_low")
        r_ = Region(PQ.at_)
        keys = r_(2 * PH, NK)
        q = r_(4, T)
        with nc.Block() as block:
            @block.sync
            def _(sp):
                sp.dma_start(keys, A["keys"][l]).then_inc(pload, 16)
                load_slots(sp, lambda i, s: A["w_query"][l, i, s], loaded, E, [f"q{s}" for s in range(4)], NI)

            @block.tensor
            def _(te):
                def score(i, s):
                    te.wait_ge(S.sem, S.at(f"q{s}", i))
                    te.wait_ge(V.sem, V.before(f"s{s}", i))
                    for b in range(NB):
                        mm = te.matmul(banks[4 + s][:, b * NK:(b + 1) * NK], q[:, s, b * P:(b + 1) * P], keys[:, 4 * i + s],
                                       start=True, stop=True)
                    mm.then_inc(E.sem, E.one(f"s{s}"))

                te.wait_ge(pload, 16)
                E.prime(te)
                with te.Fori(0, NI) as i:
                    E.begin()
                    for s in range(4):
                        te.wait_ge(loaded[s], 16 * i + 16)
                        te.wait_ge(S.sem, S.before(f"q{s}", i))
                        project(te, banks[s][:, 0:T], s).then_inc(E.sem, E.one(f"q{s}"))
                        if s:
                            score(i, s - 1)
                    score(i, 3)
                    E.end()

            @block.scalar
            def _(a):
                a.activation(f32r(xhigh[:]), xn, ACT.Copy).then_inc(x_high, 1)
                S.prime(a)
                with a.Fori(0, NI) as i:
                    S.begin()
                    for s in range(4):
                        a.wait_ge(E.sem, E.at(f"q{s}", i))
                        a.activation(q[:, s], banks[s][:, 0:T], ACT.Copy).then_inc(S.sem, S.one(f"q{s}"))
                    S.end()

            @block.vector
            def _(v):
                v.wait_ge(x_high, 1)
                v.tensor_tensor(f32r(xlow[:]), xn, xhigh[:], ALU.subtract).then_inc(x_low, 1)
                V.prime(v)
                with v.Fori(0, NI) as i:
                    V.begin()
                    for s in range(4):
                        v.wait_ge(E.sem, E.at(f"s{s}", i))
                        v.tensor_copy(scores[:, :, 4 * i + s], banks[4 + s][:, 0:T].rearrange("p (b k) -> p b k", b=NB))\
                            .then_inc(V.sem, V.one(f"s{s}"))
                    V.end()
                v.wait_ge(V.sem, V.at("s3", NI - 1))
                v.wait_ge(x_low, 1)

    def peer_topk_phase(l):
        V, S, E = steps("tk_vec", True), steps("tk_act", True), steps("tk_pe", True)
        r_ = Region(PQ.at_)
        NS = 2 * PH
        s0, s1 = r_(NS, NK), r_(NS, NK)
        top, topi, topf = r_(NS, TOPK), r_(NS, TOPK, dt=U32), r_(NS, TOPK)
        cand, cand1 = r_(PH, TOPK * TOPK), r_(PH, TOPK * TOPK)
        best, pos = r_(PH, TOPK), r_(PH, TOPK, dt=U32)
        pi, pf = r_(PH, TOPK, dt=U32), r_(PH * TOPK)
        eq = r_(PH * TOPK, TOPK)
        e1, e2 = r_(PH, TOPK), r_(PH, TOPK)
        gate, gsum, dummy = r_(PH, TOPK), r_(PH), r_(1)
        WORST = -3.0e38
        side = lambda x, q: x.rearrange("p (h s) k -> p h s k", s=2)[:, :, q]
        flat = lambda x: x.rearrange("p h k -> p (h k)")
        with nc.Block() as block:
            @block.vector
            def _(v):
                V.prime(v)
                with v.Fori(0, NB) as i:
                    V.begin()
                    v.tensor_copy(s0, scores[:, i]).then_inc(V.sem, V.one("copy"))

                    def settled():
                        v.wait_ge(V.sem, V.now(i))
                        v.memset(dummy, 0.0).then_inc(V.sem, V.one())

                    def best16(n, x, x1, vals, idx):
                        settled()
                        for k in range(n):
                            v.max(vals[:, k, 0:8], x[:, k]).then_inc(V.sem, V.one())
                        settled()
                        for k in range(n):
                            v.max_index(idx[:, k, 0:8], vals[:, k, 0:8], x[:, k]).then_inc(V.sem, V.one())
                            v.match_replace(x1[:, k], vals[:, k, 0:8], x[:, k], WORST).then_inc(V.sem, V.one())
                        settled()
                        for k in range(n):
                            v.max(vals[:, k, 8:16], x1[:, k]).then_inc(V.sem, V.one())
                        settled()
                        for k in range(n):
                            v.max_index(idx[:, k, 8:16], vals[:, k, 8:16], x1[:, k]).then_inc(V.sem, V.one())
                        v.wait_ge(V.sem, V.now(i))

                    best16(NS, s0, s1, top, topi)
                    v.tensor_copy(topf, topi).then_inc(V.sem, V.one())
                    for a in range(TOPK):
                        v.tensor_tensor(cand[:, :, a * TOPK:(a + 1) * TOPK],
                                        side(top, 0)[:, :, a:a + 1].to_broadcast([P, PH, TOPK]), side(top, 1), ALU.add)\
                            .then_inc(V.sem, V.one())
                    best16(PH, cand, cand1, best, pos)
                    for q, (dst, op, arg) in enumerate(((e1, ALU.logical_shift_right, 4), (e2, ALU.bitwise_and, 15))):
                        v.tensor_scalar(pi, pos, arg, None, op).then_inc(V.sem, V.one())
                        v.wait_ge(V.sem, V.now(i))
                        v.tensor_copy(pf, flat(pi)).then_inc(V.sem, V.one())
                        v.wait_ge(V.sem, V.now(i))
                        v.tensor_tensor(eq, pf.unsqueeze(2).to_broadcast([P, PH * TOPK, TOPK]),
                                        iota[:, 0:TOPK].unsqueeze(1).to_broadcast([P, PH * TOPK, TOPK]), ALU.is_equal)\
                            .then_inc(V.sem, V.one())
                        v.wait_ge(V.sem, V.now(i))
                        eq4 = eq.rearrange("p (h k) a -> p h k a", h=PH)
                        v.tensor_tensor(eq4, eq4, side(topf, q).unsqueeze(2).to_broadcast([P, PH, TOPK, TOPK]), ALU.mult)\
                            .then_inc(V.sem, V.one())
                        v.wait_ge(V.sem, V.now(i))
                        v.tensor_reduce(flat(dst), eq, AX.X, ALU.add).then_inc(V.sem, V.one())
                        v.wait_ge(V.sem, V.now(i))
                    v.tensor_tensor(gate, best, best[:, :, 0:1].to_broadcast([P, PH, TOPK]), ALU.subtract).then_inc(V.sem, V.one("e"))
                    v.wait_ge(S.sem, S.at("exp", i))
                    v.tensor_reduce(gsum, gate, AX.X, ALU.add).then_inc(V.sem, V.one())
                    v.wait_ge(V.sem, V.now(i))
                    v.reciprocal(gsum, gsum).then_inc(V.sem, V.one())
                    v.wait_ge(V.sem, V.now(i))
                    v.tensor_tensor(gate, gate, gsum.unsqueeze(2).to_broadcast([P, PH, TOPK]), ALU.mult).then_inc(V.sem, V.one("gate"))
                    for n, dst in enumerate((slot1, slot2, slotg)):
                        v.wait_ge(E.sem, E.at(f"t{n}", i))
                        v.tensor_copy(dst[:, bass.ds(i * P, P)], banks[n][:, 0:P]).then_inc(V.sem, V.one(f"c{n}"))
                    v.wait_ge(V.sem, V.now(i))
                    V.end()

            @block.scalar
            def _(a):
                S.prime(a)
                with a.Fori(0, NB) as i:
                    S.begin()
                    a.wait_ge(V.sem, V.at("e", i))
                    a.activation(gate, gate, ACT.Exp).then_inc(S.sem, S.one("exp"))
                    S.end()

            @block.tensor
            def _(te):
                E.prime(te)
                with te.Fori(0, NB) as i:
                    E.begin()
                    te.wait_ge(V.sem, V.at("gate", i))
                    for n, src in enumerate((e1, e2, gate)):
                        te.transpose(banks[n][:, 0:P], flat(src), ident[:]).then_inc(E.sem, E.one(f"t{n}"))
                    E.end()

    GATES = arena[:, :].rearrange("p (t j) -> p t j", t=T)

    def peer_gate_phase(l):
        NI = T // 8
        onehot = ring[:, :, :].rearrange("p s c -> p (s c)")
        V, S, E = steps("gt_vec", True), steps("gt_act", True), steps("gt_pe", True)
        oh1 = onehot[:, 0:8 * P].rearrange("p (u k) -> p u k", u=8)
        oh2 = onehot[:, 8 * P:16 * P].rearrange("p (u k) -> p u k", u=8)
        with nc.Block() as block:
            @block.vector
            def _(v):
                V.prime(v)
                with v.Fori(0, NI) as i:
                    V.begin()
                    for u in range(8):
                        tok = bass.ds(8 * i + u, 1)
                        if u % 4 == 0:
                            v.wait_ge(E.sem, E.before(f"g{u // 4}", i))
                        v.tensor_scalar(oh1[:, u], iota[:], slot1[:, tok], None, ALU.is_equal).then_inc(V.sem, V.one())
                        v.tensor_scalar(oh2[:, u], iota[:], slot2[:, tok], slotg[:, tok], ALU.is_equal, ALU.mult)\
                            .then_inc(V.sem, V.one(f"u{u}"))
                    V.end()

            @block.tensor
            def _(te):
                E.prime(te)
                with te.Fori(0, NI) as i:
                    E.begin()
                    for g in range(2):
                        te.wait_ge(S.sem, S.before(f"g{g}", i))
                        for u in range(4 * g, 4 * g + 4):
                            te.wait_ge(V.sem, V.at(f"u{u}", i))
                            mm = te.matmul(banks[g][:, (u % 4) * NK:(u % 4 + 1) * NK], oh1[:, u], oh2[:, u], start=True, stop=True)
                        mm.then_inc(E.sem, E.one(f"g{g}"))
                    E.end()

            @block.scalar
            def _(a):
                S.prime(a)
                with a.Fori(0, NI) as i:
                    S.begin()
                    for g in range(2):
                        a.wait_ge(E.sem, E.at(f"g{g}", i))
                        a.activation(GATES[:, bass.ds(8 * i + 4 * g, 4)], banks[g][:, :].rearrange("p (u k) -> p u k", u=4), ACT.Copy)\
                            .then_inc(S.sem, S.one(f"g{g}"))
                    S.end()
                a.wait_ge(S.sem, S.at("g1", NI - 1))

    def peer_expert_phase(l, raw, parts):
        UJ = 4
        NI = NK // UJ
        H = KT * P // 2
        names = ("u_high", "u_low", "v_high", "v_low", "hidden", "gelu", "gated", "a_high", "a_low", "mixed")
        u_high, u_low, v_high, v_low, hidden, gelu, gated, a_high, a_low, mixed = [lsem("ex_" + n) for n in names]
        u_in = [lsem(f"ex_u_in{s}") for s in range(2)]
        v_in = [lsem(f"ex_v_in{s}") for s in range(2)]
        opened, added = lsem("ex_opened"), lsem("ex_added")
        u_raw, v_raw = [raw[:, s] for s in range(2)], [raw[:, 2 + s] for s in range(2)]
        u_hi, u_lo, v_hi, v_lo = (parts[:, n] for n in range(4))
        act = [slots[:, s] for s in range(2)]
        ybanks = banks[4:8]
        U = (u_in, u_raw, u_hi, u_lo, u_high, u_low, hidden)
        W = (v_in, v_raw, v_hi, v_lo, v_high, v_low, mixed)

        def steps_of(engine, one_step):
            with engine.Fori(0, NI - 1) as i:
                for u in range(UJ):
                    one_step(UJ * i, u)
            for u in range(UJ):
                one_step(UJ * (NI - 1), u)

        ends = lambda j4, u, ahead: isinstance(j4, int) and j4 + u + ahead >= NK
        with nc.Block() as block:
            @block.sync
            def _(sp):
                def load(what, sems, raw, j4, u):
                    sp.dma_start(raw[u % 2], A[what][l, j4 + u]).then_inc(sems[u % 2], 16)

                load("u", u_in, u_raw, 0, 0)
                load("u", u_in, u_raw, 0, 1)
                load("v", v_in, v_raw, 0, 0)
                sp.wait_ge(u_low, 2)
                load("u", u_in, u_raw, 0, 2)

                def step(j4, u):
                    if not ends(j4, u, 3):
                        sp.wait_ge(u_low, 2 * (j4 + u) + 4)
                        load("u", u_in, u_raw, j4, u + 3)
                    if not ends(j4, u, 1):
                        if not (isinstance(j4, int) and j4 + u < 1):
                            sp.wait_ge(v_low, 2 * (j4 + u))
                        load("v", v_in, v_raw, j4, u + 1)
                steps_of(sp, step)

            @block.tensor
            def _(te):
                def product(ps, w_hi, w_lo, x_hi, x_lo, start, stop, **kw):
                    te.matmul(ps, f32r(w_hi), f32r(x_hi), start=start, stop=False, **kw)
                    te.matmul(ps, f32r(w_hi), f32r(x_lo), start=False, stop=False, **kw)
                    return te.matmul(ps, f32r(w_lo), f32r(x_hi), start=False, stop=stop, **kw)

                def with_u(j4, u):
                    for k in range(KT):
                        if k % (KT // 2) == 0:
                            te.wait_ge(u_low, 2 * (j4 + u) + 1 + k // (KT // 2))
                        cols = slice(k * P, (k + 1) * P)
                        mm = product(banks[u % 4][:, 0:T], u_hi[:, cols], u_lo[:, cols], xhigh[:, k], xlow[:, k], k == 0, k == KT - 1)
                        if (k + 1) % (KT // 2) == 0:
                            mm.then_inc(hidden, 1)

                def with_v(j4, u):
                    s = u % 2
                    te.wait_ge(a_low, j4 + u + 1)
                    for d in range(KT):
                        if d % (KT // 2) == 0:
                            te.wait_ge(v_low, 2 * (j4 + u) + 1 + d // (KT // 2))
                        cols = slice(d * P, (d + 1) * P)
                        mm = product(ybanks[d // 2][:, (d % 2) * T:(d % 2 + 1) * T], v_hi[:, cols], v_lo[:, cols],
                                     act_high[:, s], act_low[:, s], False, False, skip_group_check=True)
                        if (d + 1) % (KT // 2) == 0:
                            mm.then_inc(mixed, 1)

                te.wait_ge(opened, 1)
                for y in ybanks:
                    te.matmul(y[:, :], f32r(act_low[:, 0, 0:P]), f32r(xhigh[:, 0:2]), start=True, stop=False, skip_group_check=True)
                with_u(0, 0)
                with_u(0, 1)

                def step(j4, u):
                    if not ends(j4, u, 2):
                        with_u(j4, u + 2)
                    with_v(j4, u)
                steps_of(te, step)

            def halves(j4, u):
                return ((n, slice(n * H, (n + 1) * H), 2 * (j4 + u) + n) for n in range(2))

            @block.scalar
            def _(a):
                def high(tiles, j4, u):
                    arrived, raw, hi, lo, high_done, low_done, used = tiles
                    a.wait_ge(arrived[u % 2], 8 * j4 + 16 * (u // 2) + 16)
                    for n, cols, half_no in halves(j4, u):
                        if not (isinstance(j4, int) and j4 + u < 1):
                            a.wait_ge(used, half_no - 1)
                        a.activation(f32r(hi[:, cols]), raw[u % 2][:, cols], ACT.Copy).then_inc(high_done, 1)

                def gelu_step(j4, u):
                    a.wait_ge(hidden, 2 * (j4 + u) + 2)
                    if not (isinstance(j4, int) and j4 + u < 2):
                        a.wait_ge(a_low, j4 + u - 1)
                    a.activation(act[u % 2], banks[u % 4][:, 0:T], ACT.Gelu_apprx_tanh).then_inc(gelu, 1)

                def a_high_step(j4, u):
                    a.wait_ge(gated, j4 + u + 1)
                    if not (isinstance(j4, int) and j4 + u < 2):
                        a.wait_ge(mixed, 2 * (j4 + u) - 2)
                    a.activation(f32r(act_high[:, u % 2]), act[u % 2], ACT.Copy).then_inc(a_high, 1)

                high(U, 0, 0)
                high(U, 0, 1)
                gelu_step(0, 0)
                high(U, 0, 2)
                a_high_step(0, 0)
                high(W, 0, 0)

                def step(j4, u):
                    if not ends(j4, u, 1):
                        gelu_step(j4, u + 1)
                    if not ends(j4, u, 3):
                        high(U, j4, u + 3)
                    if not ends(j4, u, 1):
                        a_high_step(j4, u + 1)
                        high(W, j4, u + 1)
                steps_of(a, step)

            @block.vector
            def _(v):
                def low(tiles, j4, u):
                    arrived, raw, hi, lo, high_done, low_done, used = tiles
                    for n, cols, half_no in halves(j4, u):
                        v.wait_ge(high_done, half_no + 1)
                        v.tensor_tensor(f32r(lo[:, cols]), raw[u % 2][:, cols], hi[:, cols], ALU.subtract).then_inc(low_done, 1)

                def gate_step(j4, u):
                    v.wait_ge(gelu, j4 + u + 1)
                    v.tensor_tensor(act[u % 2], act[u % 2], GATES[:, :, j4 + u], ALU.mult).then_inc(gated, 1)

                def a_low_step(j4, u):
                    v.wait_ge(a_high, j4 + u + 1)
                    v.tensor_tensor(f32r(act_low[:, u % 2]), act[u % 2], act_high[:, u % 2], ALU.subtract).then_inc(a_low, 1)

                v.tensor_scalar(f32r(act_low[:, 0, 0:P]), iota[:], 0.0, None, ALU.mult).then_inc(opened, 1)
                low(U, 0, 0)
                low(U, 0, 1)
                gate_step(0, 0)
                low(U, 0, 2)
                a_low_step(0, 0)
                low(W, 0, 0)

                def step(j4, u):
                    if not ends(j4, u, 1):
                        gate_step(j4, u + 1)
                    if not ends(j4, u, 3):
                        low(U, j4, u + 3)
                    if not ends(j4, u, 1):
                        a_low_step(j4, u + 1)
                        low(W, j4, u + 1)
                steps_of(v, step)
                v.wait_ge(mixed, 2 * NK)
                for b, y in enumerate(ybanks):
                    v.tensor_tensor(h[:, 2 * b:2 * b + 2], h[:, 2 * b:2 * b + 2], y[:, :].rearrange("p (d t) -> p d t", d=2), ALU.add)\
                        .then_inc(added, 1)
                v.wait_ge(added, KT // 2)

    final = Steps(sem("final_out"), book, "final", False)
    with nc.Fori(0, L) as l:
        with nc.sbuf_tensor("ring", [P, 8, KT * P], F32) as ring:
            rmsnorm("mixnorm", norm_w[:, 2 * l], xn)
            lru_phase(l)
            rwkv_phase(l)
            gdn_phase(l)
            merge_phase(l)
            rmsnorm("ffnnorm", norm_w[:, 2 * l + 1], xn)
            peer_query_phase(l)
            peer_topk_phase(l)
            peer_gate_phase(l)
        with nc.sbuf_tensor("raw_tiles", [P, 4, KT * P], F32) as raw, nc.sbuf_tensor("tile_parts", [P, 4, KT * P], F32) as parts:
            peer_expert_phase(l, raw, parts)
        with nc.Block() as block:
            @block.sync
            def _(sp):
                for s in cleared:
                    sp.sem_clear(s)
    del cleared[:]
    rmsnorm("outnorm", norm_w[:, 2 * L], xn)
    with nc.Block() as block:
        @block.sync
        def _(sp):
            sp.dma_start(out, xn).then_inc(final.sem, 16)
            sp.wait_ge(final.sem, 16)


def host_layout(x, norm_mix_w, norm_ffn_w, final_norm_w, w_in, lru_conv_w, lru_conv_b, lru_w_a,
                lru_b_a, lru_w_x, lru_b_x, lru_lambda, gdn_conv_w, gdn_a_log, gdn_dt_bias, gdn_norm_w,
                rwkv_mu, rwkv_w0, rwkv_w_up, rwkv_a0, rwkv_a_up, rwkv_g_up, rwkv_k_k, rwkv_k_a,
                rwkv_r_k, rwkv_lnx_w, rwkv_lnx_b, merge_b, p_lru, p_gdn, p_rwkv, w_out,
                peer_wq, peer_keys, peer_u, peer_v):
    import numpy as np

    def tiles(w):
        n = w.shape[2] // P
        return w.reshape(L, KT, P, n, P).transpose(0, 3, 2, 1, 4).reshape(L, n, P, KT * P)

    def chan(v):
        return v.reshape(L, -1, P).transpose(0, 2, 1)

    o = {}
    at = 0
    z = {}
    for name, n in (("u", 1024), ("g", 1024), ("q", 1024), ("k", 1024), ("v", 1024), ("zg", 1024),
                    ("ab", 16), ("r", 1024), ("rk", 1024), ("rv", 1024), ("lora", 256),
                    ("ma", 1024), ("mb", 1024), ("mc", 1024)):
        z[name] = w_in[:, :, at:at + n] if n == 16 else tiles(w_in[:, :, at:at + n])
        at += n
    o["x"] = x[0].T.reshape(KT, P, T).transpose(1, 0, 2)
    norms = [w for l in range(L) for w in (norm_mix_w[l], norm_ffn_w[l])] + [final_norm_w]
    o["norms"] = np.stack([w.reshape(KT, P).T for w in norms], 1)

    o["w_lru"] = np.stack([z["u"], z["g"]], 2).reshape(L, KT // 2, 4, P, KT * P)
    o["lru_par"] = np.stack([chan(lru_conv_w[:, j]) for j in range(4)]
                            + [chan(v) for v in (lru_conv_b, lru_b_a, lru_b_x, lru_lambda)], 3)
    gates = np.zeros((L, P, KT, 2, P), np.float32)
    for j, w in enumerate((lru_w_a, lru_w_x)):
        w = w.reshape(L, KT, 2, 64, 64)
        for q in range(2):
            gates[:, 64 * q:64 * q + 64, :, j, 64 * q:64 * q + 64] = w[:, :, q].transpose(0, 2, 1, 3)
    o["lru_gates"] = gates

    o["w_rwkv"] = np.stack([z["r"], z["rk"], z["rv"]], 2)
    o["w_rwkv_lora"] = z["lora"]
    mu = chan(rwkv_mu)
    o["rwkv_par"] = np.stack([mu[:, :, 0:8], mu[:, :, 8:16], mu[:, :, 16:24]]
                             + [chan(v.reshape(L, -1)) for v in (rwkv_w0, rwkv_a0, rwkv_k_k, rwkv_k_a, rwkv_r_k,
                                                                 rwkv_lnx_w, rwkv_lnx_b)], 3)
    o["rwkv_lora_par"] = mu[:, :, 24:26]
    up = np.concatenate([rwkv_w_up, rwkv_a_up], 1).reshape(L, P, KT, P).transpose(0, 2, 1, 3)
    o["rwkv_up"] = np.concatenate([up, rwkv_g_up.reshape(L, P, KT, P).transpose(0, 2, 1, 3)], 3)

    o["w_gdn"] = np.stack([z[n].reshape(L, 4, 2, P, KT * P) for n in ("q", "k", "v", "zg")], 2).reshape(L, 4, 8, P, KT * P)
    conv = gdn_conv_w.reshape(L, 4, 3, 8, P).transpose(0, 4, 3, 2, 1)
    o["gdn_par"] = conv.reshape(L, P, 8, 12)
    o["gdn_norm"] = gdn_norm_w.reshape(L, P, 1)
    o["gdn_ab"] = z["ab"].reshape(L, KT, P, 16).transpose(0, 2, 1, 3)
    rows = np.stack([gdn_a_log, gdn_dt_bias], 1)
    o["gdn_rows"] = np.broadcast_to(rows[:, None, :, :, None], (L, P, 2, 8, 2))

    o["w_merge"] = np.stack([z["ma"], tiles(p_lru), z["mb"], tiles(p_gdn), z["mc"], tiles(p_rwkv)], 2)
    o["merge_b"] = chan(merge_b).reshape(L, P, 3, KT)
    o["w_out"] = tiles(w_out).reshape(L, 4, 2, P, KT * P)

    o["w_query"] = tiles(peer_wq).reshape(L, 4, 4, P, KT * P)
    o["keys"] = peer_keys.reshape(L, 16, NK, P).transpose(0, 3, 1, 2)
    o["u"] = peer_u.reshape(L, NK, NK, KT, P).transpose(0, 2, 4, 3, 1).reshape(L, NK, P, KT * P)
    o["v"] = peer_v.reshape(L, NK, NK, D).transpose(0, 2, 1, 3)
    return {k: np.ascontiguousarray(a) for k, a in o.items()}


def kernel(**inputs):
    import numpy as np
    import concourse.bacc as bacc
    from concourse.bass_utils import run_bass_kernel_spmd

    arrays = host_layout(**{k: np.asarray(a) for k, a in inputs.items()})
    book = {"first": True}
    for _ in range(2):
        nc = bacc.Bacc("TRN2", target_bir_lowering=False, num_devices=1)
        A = {k: nc.dram_tensor("in_" + k, a.shape, mybir.dt.from_np(a.dtype), kind="ExternalInput").ap()
             for k, a in arrays.items()}
        out = nc.dram_tensor("out_y", (P, KT, T), F32, kind="ExternalOutput").ap()
        build(nc, A, out, book)
        book.pop("first", None)
    r = run_bass_kernel_spmd(nc, [{"in_" + k: a for k, a in arrays.items()}], core_ids=[0])
    y = r.results[0]["out_y"]
    return np.ascontiguousarray(y.transpose(2, 1, 0).reshape(1, T, D))
```

```python
import math
from contextlib import ExitStack

import concourse.bass as bass
from concourse import mybir

F32 = mybir.dt.float32
U32 = mybir.dt.uint32
F32R = mybir.dt.float32r
ALU = mybir.AluOpType
ACT = mybir.ActivationFunctionType
AX = mybir.AxisListType

P = 128
T = 256
D = 1024
KT = D // P
NB = T // P
L = 2
EPS = 1e-6
GN_EPS = 64e-5
LRU_C = 8.0
HD = 64
CH = 64
GDN_SCALE = 128 ** -0.5
DECAY = math.exp(-0.5)
TOPK = 16
PH = 8
NK = 128

LRU_COLS = ["w0", "w1", "w2", "w3", "cb", "ba", "bx", "lam"]
RWKV_COLS = ["mu_r", "mu_k", "mu_v", "w0", "a0", "k_k", "k_a", "r_k", "ln_w", "ln_b"]
RWKV_MADE = ["om_r", "om_k", "om_v", "om_ka"]
GDN_COLS = [f"{x}{j}" for x in "qkv" for j in range(4)]
N_LEVELS = 7


class Steps:

    def __init__(self, sem, book, name, looped):
        self.sem, self.book, self.name, self.looped, self.n = sem, book, name, looped, 0

    def per(self):
        return self.book.get((self.name, "per"), 1)

    def prime(self, engine):
        engine.sem_inc(self.sem, self.per())

    def begin(self):
        self.n = 0

    def one(self, label=None):
        self.n += 1
        if label:
            self.book[self.name, label] = self.n
        return 1

    def end(self):
        self.book[self.name, "per"] = self.n

    def index(self, label):
        assert self.book.get("first") or (self.name, label) in self.book, (self.name, label)
        return self.book.get((self.name, label), 1)

    def at(self, label, i=0):
        return (i + 1) * self.per() + self.index(label) if self.looped else self.index(label)

    def before(self, label, i):
        return i * self.per() + self.index(label)

    def now(self, i=0):
        assert self.n > 0
        return (i + 1) * self.per() + self.n if self.looped else self.n


def build(nc, A, out, book):
    ctx = ExitStack()
    with ctx:
        _program(nc, ctx, A, out, book)


def _program(nc, ctx, A, out, book):
    def sb(name, shape, dt=F32):
        return ctx.enter_context(nc.sbuf_tensor(name, shape, dt))

    def sem(name):
        return ctx.enter_context(nc.semaphore(name))

    cleared = []

    def lsem(name):
        s = sem(name)
        cleared.append(s)
        return s

    def steps(name, looped=False):
        return Steps(lsem(name), book, name, looped)

    h = sb("h", [P, KT, T])
    ident = sb("ident", [P, P])
    ones = sb("ones", [P, P])
    blk64 = sb("blk64", [P, P])
    upto = sb("upto", [P, P])
    after = sb("after", [P, P])
    gmask = sb("gmask", [P, 2, P])
    rmask = sb("rmask", [P, 2, P])
    lmask = sb("lmask", [P, N_LEVELS, P])
    restart = sb("restart", [P, T])
    half = sb("half", [P, 2])
    iota = sb("iota", [P, P])
    zrow = sb("zrow", [P, 1])
    norm_w = sb("norm_w", [P, 2 * L + 1, KT])
    ARENA = 32768
    arena = sb("arena", [P, ARENA])
    banks = [ctx.enter_context(nc.psum_tensor(f"bank{i}", [P, 512], F32)) for i in range(8)]

    class Region:

        def __init__(self, at):
            self.at_ = at

        def __call__(self, *shape, dt=F32):
            n = math.prod(shape)
            assert self.at_ + n <= ARENA, (self.at_, n)
            v = arena[:, self.at_:self.at_ + n]
            self.at_ += n
            if dt is not F32:
                v = v.bitcast(dt)
            if len(shape) == 1:
                return v
            names = "abcd"[:len(shape)]
            return v.rearrange(f"p ({' '.join(names)}) -> p {' '.join(names)}", **{k: s for k, s in zip(names[1:], shape[1:])})

    base = Region(0)
    xn = base(KT, T)
    PEER = base.at_
    ya, yb, yc = base(KT, T), base(KT, T), base(KT, T)
    BRANCH = base.at_

    consts_sem = sem("consts")
    pool_sem = sem("consts_pool")
    vec_sem = sem("consts_vec")
    load_x = sem("load_x")

    with nc.Block() as block:
        @block.sync
        def _(sp):
            sp.dma_start(h[:], A["x"]).then_inc(load_x, 16)
            sp.dma_start(norm_w[:], A["norms"]).then_inc(load_x, 16)
            sp.wait_ge(load_x, 32)

        @block.gpsimd
        def _(g):
            n = 0

            def fill(ap, value):
                nonlocal n
                g.memset(ap, value).then_inc(pool_sem, 1)
                n += 1
                g.wait_ge(pool_sem, n)

            def keep(ap, op, basev, pattern, mult, fill_value=0.0):
                nonlocal n
                g.affine_select(out=ap, in_=ap, compare_op=op, fill=fill_value, base=basev,
                                pattern=pattern, channel_multiplier=mult).then_inc(pool_sem, 1)
                n += 1
                g.wait_ge(pool_sem, n)

            for m in (ones, upto, after, gmask, rmask, lmask, restart, half, blk64):
                fill(m[:], 1.0)
            fill(ident[:], 0.0)
            keep(ident[:], ALU.not_equal, 0, [[-1, P]], 1, 1.0)
            keep(upto[:], ALU.is_ge, 0, [[1, P]], -1)
            keep(after[:], ALU.is_gt, 0, [[-1, P]], 1)
            for m in (gmask, rmask):
                keep(m[:, 0], ALU.is_gt, 0, [[1, P]], -1)
                keep(m[:, 1], ALU.is_ge, 0, [[1, P]], -1)
            for m in (blk64[:], rmask[:, 0], rmask[:, 1]):
                keep(m[:, 0:64], ALU.is_ge, 63, [[0, 64]], -1)
                keep(m[:, 64:128], ALU.is_ge, -64, [[0, 64]], 1)
            keep(half[:, 0:1], ALU.is_ge, 63, [[0, 1]], -1)
            keep(half[:, 1:2], ALU.is_ge, -64, [[0, 1]], 1)
            for lev in range(N_LEVELS):
                w = 1 << lev
                nb = P // (2 * w)
                m = lmask[:, lev].rearrange("p (b h w) -> p b h w", b=nb, h=2)
                keep(m, ALU.is_ge, 0, [[-2 * w, nb], [0, 2], [0, w]], 1)
                keep(m, ALU.is_ge, w - 1, [[2 * w, nb], [0, 2], [0, w]], -1)
                fill(m[:, :, 0, :], 0.0)
            fill(restart[:].rearrange("p (c t) -> p c t", t=CH)[:, :, 0], 0.0)
            fill(zrow[:], 0.0)
            g.iota(iota[:], pattern=[[1, P]], base=0, channel_multiplier=0,
                   allow_small_or_imprecise_dtypes=True).then_inc(pool_sem, 1)
            g.wait_ge(pool_sem, n + 1)

    def rmsnorm(tag, w, dst):
        V, E, S = steps(tag + "_vec"), steps(tag + "_pe"), steps(tag + "_act")
        r = Region(BRANCH)
        sq, rs = r(KT, T), r(T)
        ss = banks[0][:, 0:T]
        with nc.Block() as block:
            @block.vector
            def _(v):
                v.tensor_tensor(sq, h[:], h[:], ALU.mult).then_inc(V.sem, V.one("sq"))
                v.wait_ge(E.sem, E.at("ss"))
                v.tensor_scalar(rs, ss, 1.0 / D, EPS, ALU.mult, ALU.add).then_inc(V.sem, V.one("ms"))
                v.wait_ge(S.sem, S.at("root"))
                v.reciprocal(rs, rs).then_inc(V.sem, V.one())
                v.wait_ge(V.sem, V.now())
                for k in range(KT):
                    v.scalar_tensor_tensor(dst[:, k, :], h[:, k, :], w[:, k:k + 1], rs, ALU.mult, ALU.mult)\
                        .then_inc(V.sem, V.one())
                v.wait_ge(V.sem, V.now())

            @block.tensor
            def _(te):
                te.wait_ge(V.sem, V.at("sq"))
                for k in range(KT):
                    mm = te.matmul(ss, ones[:], sq[:, k, :], start=(k == 0), stop=(k == KT - 1))
                mm.then_inc(E.sem, E.one("ss"))

            @block.scalar
            def _(a):
                a.wait_ge(V.sem, V.at("ms"))
                a.activation(rs, rs, ACT.Sqrt).then_inc(S.sem, S.one("root"))

    def load_slots(sp, source, loaded, E, labels, n_iter, first=0):
        for s in range(len(labels)):
            sp.dma_start(ring[:, first + s, :], source(0, s)).then_inc(loaded[s], 16)
        with sp.Fori(1, n_iter) as i:
            for s, label in enumerate(labels):
                sp.wait_ge(E.sem, E.before(label, i))
                sp.dma_start(ring[:, first + s, :], source(i, s)).then_inc(loaded[s], 16)

    def project(te, ps, slot, x=None, ks=range(KT)):
        x = xn if x is None else x
        for k in ks:
            mm = te.matmul(ps, ring[:, slot, k * P:(k + 1) * P], x[:, k, :], start=(k == 0), stop=(k == KT - 1))
        return mm

    def softplus_exp(a, S, x, e, tag):
        a.activation(e, x, ACT.Abs).then_inc(S.sem, S.one())
        a.wait_ge(S.sem, S.now())
        a.activation(e, e, ACT.Exp, scale=-1.0).then_inc(S.sem, S.one(tag + "_e"))

    def softplus_log(v, V, x, e, z, z2, p, m):
        v.tensor_scalar(z, e, 2.0, None, ALU.add).then_inc(V.sem, V.one())
        v.wait_ge(V.sem, V.now())
        v.reciprocal(z, z).then_inc(V.sem, V.one())
        v.wait_ge(V.sem, V.now())
        v.tensor_tensor(z, z, e, ALU.mult).then_inc(V.sem, V.one())
        v.wait_ge(V.sem, V.now())
        v.tensor_tensor(z2, z, z, ALU.mult).then_inc(V.sem, V.one())
        v.wait_ge(V.sem, V.now())
        v.tensor_scalar(p, z2, 1.0 / 17, None, ALU.mult).then_inc(V.sem, V.one())
        for k in range(7, 0, -1):
            v.wait_ge(V.sem, V.now())
            v.scalar_tensor_tensor(p, p, 1.0 / (2 * k + 1), z2, ALU.add, ALU.mult).then_inc(V.sem, V.one())
        v.wait_ge(V.sem, V.now())
        v.scalar_tensor_tensor(p, p, 1.0, z, ALU.add, ALU.mult).then_inc(V.sem, V.one())
        v.tensor_scalar(m, x, 0.0, None, ALU.max).then_inc(V.sem, V.one())
        v.wait_ge(V.sem, V.now())
        v.scalar_tensor_tensor(p, p, 2.0, m, ALU.mult, ALU.add).then_inc(V.sem, V.one())

    def lru_phase(l):
        VB, SB, EB = steps("lruB_vec"), steps("lruB_act"), steps("lruB_pe")
        pload = lsem("lru_params")
        r = Region(BRANCH)
        par = r(KT, len(LRU_COLS))
        wax = r(KT, 2, P)
        rr, ii, aa, bb = r(KT, T), r(KT, T), r(KT, T), r(KT, T)
        xc = yb
        lam_n, e, z, z2, spl, m8 = (r(KT) for _ in range(6))
        c = {n: k for k, n in enumerate(LRU_COLS)}
        with nc.Block() as block:
            @block.sync
            def _(sp):
                sp.dma_start(par, A["lru_par"][l]).then_inc(pload, 16)
                sp.dma_start(wax, A["lru_gates"][l]).then_inc(pload, 16)

            @block.tensor
            def _(te):
                te.wait_ge(pload, 32)
                for k in range(KT):
                    if k >= 4:
                        te.wait_ge(SB.sem, SB.at(f"i{k - 4}"))
                    te.matmul(banks[k % 4][:, 0:T], wax[:, k, 0, :], xc[:, k, :], start=True, stop=True)\
                        .then_inc(EB.sem, EB.one(f"r{k}"))
                    te.matmul(banks[4 + k % 4][:, 0:T], wax[:, k, 1, :], xc[:, k, :], start=True, stop=True)\
                        .then_inc(EB.sem, EB.one(f"i{k}"))

            @block.scalar
            def _(a):
                a.wait_ge(pload, 32)
                a.wait_ge(VB.sem, VB.at("neg"))
                softplus_exp(a, SB, lam_n, e, "sp")
                for k in range(KT):
                    a.wait_ge(EB.sem, EB.at(f"r{k}"))
                    a.activation(rr[:, k, :], banks[k % 4][:, 0:T], ACT.Sigmoid, bias=par[:, k, c["ba"]:c["ba"] + 1])\
                        .then_inc(SB.sem, SB.one())
                    a.wait_ge(EB.sem, EB.at(f"i{k}"))
                    a.activation(ii[:, k, :], banks[4 + k % 4][:, 0:T], ACT.Sigmoid, bias=par[:, k, c["bx"]:c["bx"] + 1])\
                        .then_inc(SB.sem, SB.one(f"i{k}"))
                a.wait_ge(VB.sem, VB.at("nla"))
                a.activation(aa, rr, ACT.Exp, scale=-1.0).then_inc(SB.sem, SB.one("a"))
                a.activation(bb, rr, ACT.Tanh).then_inc(SB.sem, SB.one("tanh"))
                a.wait_ge(VB.sem, VB.at("b2"))
                a.activation(bb, bb, ACT.Sqrt).then_inc(SB.sem, SB.one("b"))
                a.activation(ya, ya, ACT.Gelu_apprx_tanh).then_inc(SB.sem, SB.one("gelu"))
                a.activation(zg[:], zg[:], ACT.Sigmoid).then_inc(SB.sem, SB.one("zg"))
                a.wait_ge(SB.sem, SB.now())

            @block.vector
            def _(v):
                v.wait_ge(pload, 32)
                v.tensor_scalar(lam_n, par[:, :, c["lam"]], -1.0, None, ALU.mult).then_inc(VB.sem, VB.one("neg"))
                v.wait_ge(SB.sem, SB.at("sp_e"))
                v.wait_ge(VB.sem, VB.now())
                softplus_log(v, VB, lam_n, e, z, z2, spl, m8)
                v.wait_ge(VB.sem, VB.now())
                v.wait_ge(SB.sem, SB.at(f"i{KT - 1}"))
                for k in range(KT):
                    v.tensor_scalar(rr[:, k, :], rr[:, k, :], spl[:, k:k + 1], LRU_C, ALU.mult, ALU.mult)\
                        .then_inc(VB.sem, VB.one("nla"))
                v.tensor_tensor(ii, ii, xc, ALU.mult).then_inc(VB.sem, VB.one("ix"))
                v.wait_ge(SB.sem, SB.at("tanh"))
                v.tensor_tensor(rr, aa, aa, ALU.mult).then_inc(VB.sem, VB.one("a2"))
                v.wait_ge(VB.sem, VB.now())
                v.scalar_tensor_tensor(bb, rr, 1.0, bb, ALU.add, ALU.mult).then_inc(VB.sem, VB.one("b2"))
                v.wait_ge(SB.sem, SB.at("b"))
                v.tensor_tensor(bb, bb, ii, ALU.mult).then_inc(VB.sem, VB.one("bx"))
                for k in range(KT):
                    v.wait_ge(VB.sem, VB.now())
                    v.tensor_tensor_scan(rr[:, k, :], aa[:, k, :], bb[:, k, :], 0.0, ALU.mult, ALU.add)\
                        .then_inc(VB.sem, VB.one("scan"))
                v.wait_ge(VB.sem, VB.now())
                v.wait_ge(SB.sem, SB.at("gelu"))
                v.tensor_tensor(ya, ya, rr, ALU.mult).then_inc(VB.sem, VB.one("ya"))

    def invert_levels(te, a, v, g, name, E, S, V, G, i, NLM, T_, TT, X, bX, bY, bYT, levels, fill=None):
        m4 = range(4)
        view = lambda b: b[:, :].rearrange("p (m c) -> p m c", m=4)
        for lev in range(1, levels):
            last = lev == levels - 1
            t = f"{name}{lev}"
            if te is not None:
                te.wait_ge(G.sem, G.at(f"{t}mask", i))
                if lev == 1:
                    te.wait_ge(S.sem, S.at(f"{name}T", i))
                else:
                    te.wait_ge(V.sem, V.at(f"{name}{lev - 1}TT", i))
                for m in m4:
                    mm = te.matmul(view(bX)[:, m], NLM[:, lev - 1, m], T_[:, m], start=True, stop=True)
                mm.then_inc(E.sem, E.one(f"{t}X"))
                if fill:
                    fill(lev, 0)
                te.wait_ge(S.sem, S.at(f"{t}X", i))
                if not last:
                    for m in m4:
                        mm = te.matmul(view(bY)[:, m], TT[:, m], X[:, m], start=True, stop=True)
                    mm.then_inc(E.sem, E.one(f"{t}Y"))
                for m in m4:
                    mm = te.matmul(view(bYT)[:, m], X[:, m], TT[:, m], start=True, stop=True)
                mm.then_inc(E.sem, E.one(f"{t}YT"))
                if fill:
                    fill(lev, 1)
            if a is not None:
                a.wait_ge(E.sem, E.at(f"{t}X", i))
                a.activation(X, view(bX), ACT.Copy).then_inc(S.sem, S.one(f"{t}X"))
                if fill:
                    fill(lev)
            if v is not None:
                if not last:
                    v.wait_ge(E.sem, E.at(f"{t}Y", i))
                    v.tensor_tensor(T_, T_, view(bY), ALU.add).then_inc(V.sem, V.one())
                v.wait_ge(E.sem, E.at(f"{t}YT", i))
                v.tensor_tensor(TT, TT, view(bYT), ALU.add).then_inc(V.sem, V.one(f"{t}TT"))
                if fill:
                    fill(lev)

    def rwkv_phase(l):
        NI = KT
        VA, SA, EA = steps("rwA_vec", True), steps("rwA_act", True), steps("rwA_pe", True)
        V, S, E, G = steps("rwB_vec", True), steps("rwB_act", True), steps("rwB_pe", True), steps("rwB_pool", True)
        VF, SF, EF = steps("rwF_vec", True), steps("rwF_act", True), steps("rwF_pe", True)
        V0, S0, E0 = steps("rw0_vec"), steps("rw0_act"), steps("rw0_pe")
        loaded = [lsem(f"rw_tile{s}") for s in range(4)]
        loaded_f = [lsem(f"rwF_tile{s}") for s in range(5)]
        pload, wload = lsem("rw_params"), lsem("rw_lora_tiles")
        r_ = Region(BRANCH)
        NC_, NM = len(RWKV_COLS), len(RWKV_MADE)
        par = r_(KT, NC_)
        made = r_(KT, NM)
        lru_par = r_(KT, len(LRU_COLS))
        merge_b = r_(3, KT)
        small = r_(2 * P)
        lmu, lom = r_(2), r_(2)
        Z = r_(3, T)
        WA, SG = r_(T), r_(T)
        (kkr, sq, sg, cs, cm, Pm, Pp, Pi, rs, aa, kk, kf, kp, rk, nb, NBt, KH, bv, gt, y) = (r_(T) for _ in range(20))
        KR = r_(NB, 2, P)
        BK = r_(4, P)
        Vt, Vh = r_(NB, P), r_(2, NB, P)
        G1, G2 = r_(4, 2, P), r_(4, 2, P)
        NLM = r_(5, 4, P)
        T_, TT, X = r_(4, P), r_(4, P), r_(4, P)
        AVO = r_(4, P)
        Rs, Um, St, SP, t1 = r_(P), r_(P), r_(P), r_(P), r_(P)
        sqo = r_(4, HD)
        mu4, va4 = r_(4), r_(4)
        c = {n: k for k, n in enumerate(RWKV_COLS)}
        lc = {n: k for k, n in enumerate(LRU_COLS)}
        cmade = {n: k for k, n in enumerate(RWKV_MADE)}
        b2, b3, b4, b5, b6, b7 = banks[2:8]
        ps_in = [banks[s % 2][:, 0:T] for s in range(3)]
        F_SLOT = 3
        f_bank = [banks[n][:, 0:T] for n in (0, 1, 1, 0, 1)]
        O = AVO[:, 2:4]
        O4 = O.rearrange("p b (h c) -> p (b h) c", h=2)

        def col(i, name):
            return par[:, i, c[name]:c[name] + 1] if name in c else made[:, i, cmade[name]:cmade[name] + 1]

        with nc.Block() as block:
            @block.sync
            def _(sp):
                sp.dma_start(par, A["rwkv_par"][l]).then_inc(pload, 16)
                sp.dma_start(lmu, A["rwkv_lora_par"][l]).then_inc(pload, 16)
                for s in range(2):
                    sp.dma_start(ring[:, 6 + s, :], A["w_rwkv_lora"][l, s]).then_inc(wload, 16)

                def source(i, s):
                    return A["w_rwkv"][l, i, s]

                def side_tile(i, n):
                    sp.dma_start(ring[:, F_SLOT + n, :], A["w_side"][l, i, n]).then_inc(loaded_f[n], 16)

                for s in range(3):
                    sp.dma_start(ring[:, s, :], source(0, s)).then_inc(loaded[s], 16)
                sp.dma_start(small, A["rwkv_up"][l, 0]).then_inc(loaded[3], 16)
                sp.dma_start(lru_par, A["lru_par"][l]).then_inc(pload, 16)
                sp.dma_start(merge_b, A["merge_b"][l]).then_inc(pload, 16)
                for n in range(3):
                    side_tile(0, n)
                sp.wait_ge(E0.sem, E0.at("lora1"))
                for n in range(3, 5):
                    side_tile(0, n)
                with sp.Fori(1, NI) as i:
                    for s, what in enumerate("rkv"):
                        sp.wait_ge(EA.sem, EA.before(what, i))
                        sp.dma_start(ring[:, s, :], source(i, s)).then_inc(loaded[s], 16)
                    sp.wait_ge(E.sem, E.before("gate", i))
                    sp.dma_start(small, A["rwkv_up"][l, i]).then_inc(loaded[3], 16)
                    for n in range(5):
                        sp.wait_ge(EF.sem, EF.before(f"f{n}", i))
                        side_tile(i, n)

            def pe_piece(te, i, j, first=False):
                s, part = divmod(j, 4)
                if part == 0:
                    te.wait_ge(loaded[s], 16 * i + 16)
                    if s == 2:
                        te.wait_ge(VA.sem, VA.at("shift0", i))
                    elif not first:
                        te.wait_ge(*((SF.sem, SF.at("f0", i - 1)) if s == 0 else (VF.sem, VF.at("tap3", i - 1))))
                mm = project(te, ps_in[s], s, ks=range(2 * part, 2 * part + 2))
                if part == 3:
                    mm.then_inc(EA.sem, EA.one("rkv"[s]))

            def pe_side(te, i, js, more):
                for j in js:
                    n, part = divmod(j, 4)
                    if part == 0:
                        te.wait_ge(loaded_f[n], 16 * i + 16)
                        if n < 2:
                            te.wait_ge(SF.sem, SF.before(f"f{n + 3}", i))
                        elif n == 4:
                            te.wait_ge(SF.sem, SF.at("f2", i))
                        elif more:
                            te.wait_ge(VA.sem, VA.at(f"shift{n - 1}", i + 1))
                        else:
                            te.wait_ge(*((VF.sem, VF.at("tap3", i)) if n == 2 else (SF.sem, SF.at("f0", i))))
                    mm = project(te, f_bank[n], F_SLOT + n, ks=range(2 * part, 2 * part + 2))
                    if part == 3:
                        mm.then_inc(EF.sem, EF.one(f"f{n}"))

            def act_side(a, i, n):
                a.wait_ge(EF.sem, EF.at(f"f{n}", i))
                if n == 0:
                    a.activation(ya[:, i], f_bank[n], ACT.Copy).then_inc(SF.sem, SF.one("f0"))
                elif n == 1:
                    a.activation(yb[:, i], f_bank[n], ACT.Identity, bias=lru_par[:, i, lc["cb"]:lc["cb"] + 1],
                                 scale=lru_par[:, i, lc["w3"]:lc["w3"] + 1]).then_inc(SF.sem, SF.one("f1"))
                else:
                    a.activation(zg[:, n - 2, i], f_bank[n], ACT.Identity, bias=merge_b[:, n - 2, bass.ds(i, 1)])\
                        .then_inc(SF.sem, SF.one(f"f{n}"))

            def vec_taps(v, i):
                v.wait_ge(SF.sem, SF.at("f1", i))
                for sh in (1, 2, 3):
                    if sh > 1:
                        v.wait_ge(VF.sem, VF.now(i))
                    v.scalar_tensor_tensor(yb[:, i, sh:T], f_bank[1][:, 0:T - sh], lru_par[:, i, 3 - sh:4 - sh],
                                           yb[:, i, sh:T], ALU.mult, ALU.add).then_inc(VF.sem, VF.one(f"tap{sh}"))

            def act_piece(a, i, s):
                if s == 0:
                    a.wait_ge(V.sem, V.before("bv", i))
                    a.wait_ge(E.sem, E.before("vT", i))
                a.wait_ge(EA.sem, EA.at("rkv"[s], i))
                a.activation(Z[:, s, :], ps_in[s], ACT.Copy, scale=col(i, "om_" + "rkv"[s])).then_inc(SA.sem, SA.one(f"z{s}"))

            def vec_piece(v, i, s):
                v.wait_ge(SA.sem, SA.at(f"z{s}", i))
                v.scalar_tensor_tensor(Z[:, s, 1:T], ps_in[s][:, 0:T - 1], col(i, "mu_" + "rkv"[s]), Z[:, s, 1:T],
                                       ALU.mult, ALU.add).then_inc(VA.sem, VA.one(f"shift{s}"))

            def pe_body(te, i, more):
                def fill(lev, y):
                    if more:
                        pe_piece(te, i + 1, 2 * lev + y)

                def side(*js):
                    pe_side(te, i, js, more)

                if more:
                    EA.begin()
                EF.begin()
                E.begin()
                rows = lambda q: slice(64 * q, 64 * q + 64)
                te.wait_ge(loaded[3], 16 * i + 16)
                te.wait_ge(V.sem, V.before("y0", i))
                te.matmul(b2[:, 0:T], small[rows(0), 0:P], WA[rows(0), :], start=True, stop=True).then_inc(E.sem, E.one("w"))
                te.matmul(b3[:, 0:T], small[rows(1), 0:P], WA[rows(1), :], start=True, stop=True).then_inc(E.sem, E.one("a"))
                te.matmul(b4[:, 0:T], small[:, P:2 * P], SG, start=True, stop=True).then_inc(E.sem, E.one("gate"))
                te.wait_ge(V.sem, V.at("sq", i))
                te.matmul(b5[:, 0:T], blk64[:], sq, start=True, stop=True).then_inc(E.sem, E.one("ss"))
                for b in range(NB):
                    mm = te.transpose(b6[:, b * P:(b + 1) * P], Z[:, 2, b * P:(b + 1) * P], ident[:])
                mm.then_inc(E.sem, E.one("vT"))
                side(0, 1, 2)
                te.wait_ge(V.sem, V.at("rk", i))
                te.matmul(b7[:, 0:T], blk64[:], rk, start=True, stop=True).then_inc(E.sem, E.one("bonus"))
                side(3, 4, 5, 6, 7)
                te.wait_ge(V.sem, V.at("KH", i))
                for x, src in enumerate((NBt, KH)):
                    for b in range(NB):
                        mm = te.transpose(b5[:, (2 * x + b) * P:(2 * x + b + 1) * P], src[:, b * P:(b + 1) * P], ident[:])
                mm.then_inc(E.sem, E.one("bkT"))
                te.wait_ge(S.sem, S.at("gate", i))
                te.wait_ge(S.sem, S.at("a", i))
                te.wait_ge(V.sem, V.at("bv", i))
                for x, (src, bk) in enumerate(((NBt, (b2, b4)), (KH, (b3, b7)))):
                    for hh in range(2):
                        for b in range(NB):
                            mm = te.matmul(bk[hh][:, b * T:(b + 1) * T], src[rows(hh), b * P:(b + 1) * P],
                                           KR[rows(hh), b], start=True, stop=True)
                        mm.then_inc(E.sem, E.one(f"g{x}{hh}"))
                fill(0, 0)
                fill(0, 1)
                te.wait_ge(S.sem, S.at("BK", i))
                te.wait_ge(V.sem, V.at("TT0", i))
                for m in range(4):
                    mm = te.transpose(b5[:, m * P:(m + 1) * P], TT[:, m], ident[:])
                mm.then_inc(E.sem, E.one("T0"))
                te.wait_ge(S.sem, S.at("Vt", i))
                te.wait_ge(V.sem, V.at("m11", i))
                for x in range(2):
                    for b in range(NB):
                        for hh in range(2):
                            mm = te.matmul(b6[:, x * T + b * P + hh * HD:x * T + b * P + hh * HD + HD], G2[:, 2 * hh + b, x],
                                           Vt[:, b, hh * HD:(hh + 1) * HD], start=True, stop=True)
                mm.then_inc(E.sem, E.one("AV"))
                invert_levels(te, None, None, None, "inv", E, S, V, G, i, NLM, T_, TT, X, b2, b3, b4, 6, fill)
                te.wait_ge(V.sem, V.at("inv5TT", i))
                te.wait_ge(S.sem, S.at("AVO", i))
                for q in range(T // CH):
                    b, hf = divmod(q, 2)
                    if q:
                        te.wait_ge(V.sem, V.at(f"S{q - 1}", i))
                        te.matmul(b5[:, 0:P], KR[:, b, 0], St, start=True, stop=True).then_inc(E.sem, E.one(f"R{q}"))
                        side(2 * q + 7)
                        te.wait_ge(V.sem, V.at(f"R{q}", i))
                    rhs = Rs if q else AVO[:, 0]
                    for hh in range(2):
                        mm = te.matmul(b7[:, hh * HD:(hh + 1) * HD], TT[:, 2 * hh + b], rhs[:, hh * HD:(hh + 1) * HD],
                                       start=True, stop=True)
                    mm.then_inc(E.sem, E.one(f"U{q}"))
                    if q:
                        te.wait_ge(V.sem, V.at(f"o{q - 1}", i))
                        te.matmul(b3[:, 0:P], KR[:, b, 1], St, start=True, stop=False)
                    side(2 * q + 8)
                    te.wait_ge(S.sem, S.at(f"U{q}", i))
                    if q < 3:
                        te.matmul(b2[:, 0:P], BK[:, 2 + b], Vh[:, hf, b], start=True, stop=False)
                        te.matmul(b2[:, 0:P], BK[:, b], Um, start=False, stop=True).then_inc(E.sem, E.one(f"S{q}"))
                    for hh in range(2):
                        mm = te.matmul(b3[:, hh * HD:(hh + 1) * HD], G1[:, 2 * hh + b, 1], Um[:, hh * HD:(hh + 1) * HD],
                                       start=(q == 0), stop=(hh == 1) or q == 0)
                    mm.then_inc(E.sem, E.one(f"O{q}"))
                side(15, 16, 17, 18)
                te.wait_ge(V.sem, V.at("on", i))
                for b in range(NB):
                    mm = te.transpose(b4[:, b * P:(b + 1) * P], O[:, b], ident[:])
                mm.then_inc(E.sem, E.one("yT"))
                side(19)
                E.end()
                EF.end()
                if more:
                    EA.end()

            @block.tensor
            def _(te):
                te.wait_ge(wload, 32)
                for s in range(2):
                    project(te, banks[2 + s][:, 0:T], 6 + s).then_inc(E0.sem, E0.one(f"lora{s}"))
                EA.prime(te)
                E.prime(te)
                EF.prime(te)
                EA.begin()
                for j in range(12):
                    pe_piece(te, 0, j, first=True)
                EA.end()
                te.wait_ge(S0.sem, S0.at("SG"))
                with te.Fori(0, NI - 1) as i:
                    pe_body(te, i, True)
                pe_body(te, NI - 1, False)

            def act_body(a, i, more):
                def fill(n):
                    if more and n in (2, 4):
                        act_piece(a, i + 1, n // 2 - 1)

                if more:
                    SA.begin()
                SF.begin()
                S.begin()
                a.wait_ge(E.sem, E.at("w", i))
                a.activation(sg, b2[:, 0:T], ACT.Sigmoid, bias=col(i, "w0")).then_inc(S.sem, S.one("sg"))
                a.wait_ge(E.sem, E.at("a", i))
                a.activation(aa, b3[:, 0:T], ACT.Sigmoid, bias=col(i, "a0")).then_inc(S.sem, S.one("a"))
                a.wait_ge(E.sem, E.at("gate", i))
                a.wait_ge(V.sem, V.before("y2", i))
                a.activation(gt, b4[:, 0:T], ACT.Copy).then_inc(S.sem, S.one("gate"))
                a.wait_ge(V.sem, V.at("cm", i))
                a.activation(Pp, cs, ACT.Exp, scale=-DECAY).then_inc(S.sem, S.one("Pp"))
                a.activation(Pm, cm, ACT.Exp, scale=-DECAY).then_inc(S.sem, S.one("Pm"))
                a.activation(Pi, cs, ACT.Exp, scale=DECAY).then_inc(S.sem, S.one("Pi"))
                a.wait_ge(V.sem, V.at("rs0", i))
                a.activation(rs, rs, ACT.Sqrt).then_inc(S.sem, S.one("rs"))
                a.wait_ge(E.sem, E.at("vT", i))
                vps = b6[:, 0:2 * P].rearrange("p (b c) -> p b c", b=NB)
                a.activation(Vt, vps, ACT.Copy).then_inc(S.sem, S.one())
                for q in range(2):
                    a.activation(Vh[:, q], vps, ACT.Copy, scale=half[:, q:q + 1]).then_inc(S.sem, S.one("Vt"))
                act_side(a, i, 0)
                act_side(a, i, 1)
                a.wait_ge(E.sem, E.at("bkT", i))
                a.activation(BK, b5[:, :].rearrange("p (m c) -> p m c", m=4), ACT.Copy).then_inc(S.sem, S.one("BK"))
                a.wait_ge(E.sem, E.at("T0", i))
                a.activation(T_, b5[:, :].rearrange("p (m c) -> p m c", m=4), ACT.Copy).then_inc(S.sem, S.one("invT"))
                a.wait_ge(E.sem, E.at("AV", i))
                a.activation(AVO, b6[:, :].rearrange("p (m c) -> p m c", m=4), ACT.Copy).then_inc(S.sem, S.one("AVO"))
                invert_levels(None, a, None, None, "inv", E, S, V, G, i, NLM, T_, TT, X, b2, b3, b4, 6, fill)
                for q in range(T // CH):
                    a.wait_ge(E.sem, E.at(f"U{q}", i))
                    if q:
                        a.wait_ge(E.sem, E.at(f"O{q - 1}", i))
                    a.activation(Um, b7[:, 0:P], ACT.Copy, scale=half[:, q % 2:q % 2 + 1]).then_inc(S.sem, S.one(f"U{q}"))
                    if q == 0 and more:
                        act_piece(a, i + 1, 2)
                    if q == 2:
                        act_side(a, i, 2)
                act_side(a, i, 3)
                a.wait_ge(V.sem, V.at("var", i))
                a.activation(va4, va4, ACT.Sqrt).then_inc(S.sem, S.one("sd"))
                act_side(a, i, 4)
                S.end()
                SF.end()
                if more:
                    SA.end()

            @block.scalar
            def _(a):
                a.wait_ge(V0.sem, V0.at("made"))
                for s in range(2):
                    a.wait_ge(E0.sem, E0.at(f"lora{s}"))
                    dst = (WA, SG)[s]
                    a.activation(dst, banks[2 + s][:, 0:T], ACT.Copy, scale=lom[:, s:s + 1]).then_inc(S0.sem, S0.one(f"l{s}"))
                a.wait_ge(V0.sem, V0.at("shift1"))
                a.activation(WA[0:64, :], WA[0:64, :], ACT.Tanh).then_inc(S0.sem, S0.one())
                a.activation(SG, SG, ACT.Sigmoid).then_inc(S0.sem, S0.one("SG"))
                SA.prime(a)
                S.prime(a)
                SF.prime(a)
                a.wait_ge(pload, 64)
                SA.begin()
                for s in range(3):
                    act_piece(a, 0, s)
                SA.end()
                with a.Fori(0, NI - 1) as i:
                    act_body(a, i, True)
                act_body(a, NI - 1, False)

            def vec_body(v, i, more):
                def fill(n):
                    if more and n in (2, 4):
                        vec_piece(v, i + 1, n // 2 - 1)

                tt = lambda o, a0, a1, op, label=None: v.tensor_tensor(o, a0, a1, op).then_inc(V.sem, V.one(label))
                if more:
                    VA.begin()
                VF.begin()
                V.begin()
                v.wait_ge(VA.sem, VA.at("shift2", i))
                v.tensor_scalar(kkr, Z[:, 1], col(i, "k_k"), None, ALU.mult).then_inc(V.sem, V.one())
                v.wait_ge(V.sem, V.now(i))
                v.tensor_tensor(sq, kkr, kkr, ALU.mult).then_inc(V.sem, V.one("sq"))
                v.wait_ge(S.sem, S.at("sg", i))
                v.tensor_tensor_scan(cs, restart[:], sg, 0.0, ALU.mult, ALU.add).then_inc(V.sem, V.one())
                v.wait_ge(V.sem, V.now(i))
                v.tensor_tensor(cm, cs, sg, ALU.subtract).then_inc(V.sem, V.one("cm"))
                v.wait_ge(E.sem, E.at("ss", i))
                v.tensor_scalar(rs, b5[:, 0:T], EPS, None, ALU.add).then_inc(V.sem, V.one("rs0"))
                v.wait_ge(S.sem, S.at("a", i))
                v.tensor_scalar(kf, aa, col(i, "k_a"), col(i, "om_ka"), ALU.mult, ALU.add).then_inc(V.sem, V.one())
                v.wait_ge(V.sem, V.now(i))
                v.tensor_tensor(kp, Z[:, 1], kf, ALU.mult).then_inc(V.sem, V.one())
                v.wait_ge(V.sem, V.now(i))
                v.scalar_tensor_tensor(rk, Z[:, 0], col(i, "r_k"), kp, ALU.mult, ALU.mult).then_inc(V.sem, V.one("rk"))
                two = lambda x: x.rearrange("p (b c) -> p b c", b=NB)
                v.wait_ge(S.sem, S.at("Pi", i))
                v.tensor_tensor(KR[:, :, 1], two(Z[:, 0]), two(Pp), ALU.mult).then_inc(V.sem, V.one())
                v.wait_ge(S.sem, S.at("rs", i))
                v.reciprocal(rs, rs).then_inc(V.sem, V.one())
                v.wait_ge(V.sem, V.now(i))
                v.tensor_tensor(kk, kkr, rs, ALU.mult).then_inc(V.sem, V.one())
                v.wait_ge(V.sem, V.now(i))
                v.tensor_tensor(KR[:, :, 0], two(kk), two(Pm), ALU.mult).then_inc(V.sem, V.one())
                v.scalar_tensor_tensor(nb, kk, -1.0, aa, ALU.mult, ALU.mult).then_inc(V.sem, V.one())
                v.wait_ge(V.sem, V.now(i))
                v.tensor_tensor(NBt, nb, Pi, ALU.mult).then_inc(V.sem, V.one())
                v.tensor_tensor(KH, kp, Pi, ALU.mult).then_inc(V.sem, V.one("KH"))
                v.wait_ge(E.sem, E.at("bonus", i))
                v.tensor_tensor(bv, b7[:, 0:T], Z[:, 2], ALU.mult).then_inc(V.sem, V.one("bv"))
                for x, (dst, bk) in enumerate(((G1, (b2, b4)), (G2, (b3, b7)))):
                    for hh in range(2):
                        v.wait_ge(E.sem, E.at(f"g{x}{hh}", i))
                        v.tensor_tensor(dst[:, 2 * hh:2 * hh + 2].rearrange("p b x c -> p b (x c)"),
                                        bk[hh][:, :].rearrange("p (b c) -> p b c", b=NB),
                                        rmask[:].rearrange("p x c -> p (x c)").unsqueeze(1).to_broadcast([P, NB, 2 * P]),
                                        ALU.mult).then_inc(V.sem, V.one(f"m{x}{hh}"))
                    if x == 0:
                        v.wait_ge(V.sem, V.now(i))
                        v.tensor_tensor(TT, G1[:, :, 0], lmask[:, 0].unsqueeze(1).to_broadcast([P, 4, P]), ALU.mult)\
                            .then_inc(V.sem, V.one())
                        v.wait_ge(V.sem, V.now(i))
                        v.tensor_tensor(TT, TT, ident[:].unsqueeze(1).to_broadcast([P, 4, P]), ALU.add)\
                            .then_inc(V.sem, V.one("TT0"))
                vec_taps(v, i)
                v.wait_ge(S.sem, S.at("invT", i))
                invert_levels(None, None, v, None, "inv", E, S, V, G, i, NLM, T_, TT, X, b2, b3, b4, 6, fill)
                for q in range(T // CH):
                    b, hf = divmod(q, 2)
                    end = Pp[:, q * CH + CH - 1:q * CH + CH]
                    if q:
                        v.wait_ge(E.sem, E.at(f"R{q}", i))
                        v.tensor_tensor(Rs, b5[:, 0:P], AVO[:, b], ALU.add).then_inc(V.sem, V.one(f"R{q}"))
                        if q < 3:
                            v.tensor_scalar(SP, St, end, None, ALU.mult).then_inc(V.sem, V.one())
                    if q < 3:
                        v.wait_ge(E.sem, E.at(f"S{q}", i))
                        v.tensor_tensor(t1, b2[:, 0:P], blk64[:], ALU.mult).then_inc(V.sem, V.one("t1"))
                        v.wait_ge(V.sem, V.now(i))
                        if q:
                            v.scalar_tensor_tensor(St, t1, end, SP, ALU.mult, ALU.add).then_inc(V.sem, V.one(f"S{q}"))
                        else:
                            v.tensor_scalar(St, t1, end, None, ALU.mult).then_inc(V.sem, V.one(f"S{q}"))
                    v.wait_ge(E.sem, E.at(f"O{q}", i))
                    v.wait_ge(S.sem, S.at("AVO", i))
                    v.scalar_tensor_tensor(O[:, b], b3[:, 0:P], half[:, hf:hf + 1], O[:, b], ALU.mult, ALU.add)\
                        .then_inc(V.sem, V.one(f"o{q}"))
                    if q == 0 and more:
                        vec_piece(v, i + 1, 2)
                bc = lambda x: x.unsqueeze(2).to_broadcast([P, 4, HD])
                v.wait_ge(V.sem, V.now(i))
                v.tensor_reduce(mu4, O4, AX.X, ALU.add).then_inc(V.sem, V.one())
                v.wait_ge(V.sem, V.now(i))
                v.tensor_scalar(mu4, mu4, -1.0 / HD, None, ALU.mult).then_inc(V.sem, V.one())
                v.wait_ge(V.sem, V.now(i))
                v.tensor_tensor(O4, O4, bc(mu4), ALU.add).then_inc(V.sem, V.one())
                v.wait_ge(V.sem, V.now(i))
                v.tensor_tensor(sqo, O4, O4, ALU.mult).then_inc(V.sem, V.one())
                v.wait_ge(V.sem, V.now(i))
                v.tensor_reduce(va4, sqo, AX.X, ALU.add).then_inc(V.sem, V.one())
                v.wait_ge(V.sem, V.now(i))
                v.tensor_scalar(va4, va4, 1.0 / HD, GN_EPS, ALU.mult, ALU.add).then_inc(V.sem, V.one("var"))
                v.wait_ge(S.sem, S.at("sd", i))
                v.reciprocal(va4, va4).then_inc(V.sem, V.one())
                v.wait_ge(V.sem, V.now(i))
                v.tensor_tensor(O4, O4, bc(va4), ALU.mult).then_inc(V.sem, V.one("on"))
                v.wait_ge(E.sem, E.at("yT", i))
                v.tensor_scalar(y, b4[:, 0:T], col(i, "ln_w"), col(i, "ln_b"), ALU.mult, ALU.add).then_inc(V.sem, V.one("y0"))
                v.wait_ge(V.sem, V.now(i))
                v.tensor_tensor(y, y, bv, ALU.add).then_inc(V.sem, V.one())
                v.wait_ge(V.sem, V.now(i))
                v.tensor_tensor(yc[:, i], y, gt, ALU.mult).then_inc(V.sem, V.one("y2"))
                V.end()
                VF.end()
                if more:
                    VA.end()

            @block.vector
            def _(v):
                v.wait_ge(pload, 64)
                v.tensor_scalar(made[:, :, 0:3], par[:, :, 0:3], -1.0, 1.0, ALU.mult, ALU.add).then_inc(V0.sem, V0.one())
                v.tensor_scalar(made[:, :, 3], par[:, :, c["k_a"]], -1.0, 1.0, ALU.mult, ALU.add).then_inc(V0.sem, V0.one())
                v.tensor_scalar(lom, lmu, -1.0, 1.0, ALU.mult, ALU.add).then_inc(V0.sem, V0.one("made"))
                for s in range(2):
                    dst = (WA, SG)[s]
                    v.wait_ge(S0.sem, S0.at(f"l{s}"))
                    v.scalar_tensor_tensor(dst[:, 1:T], banks[2 + s][:, 0:T - 1], lmu[:, s:s + 1], dst[:, 1:T],
                                           ALU.mult, ALU.add).then_inc(V0.sem, V0.one(f"shift{s}"))
                VA.prime(v)
                V.prime(v)
                VF.prime(v)
                VA.begin()
                for s in range(3):
                    vec_piece(v, 0, s)
                VA.end()
                with v.Fori(0, NI - 1) as i:
                    vec_body(v, i, True)
                vec_body(v, NI - 1, False)

            def pool_body(g, i):
                G.begin()
                g.wait_ge(V.sem, V.at("m01", i))
                for lev in range(1, 6):
                    g.tensor_tensor(NLM[:, lev - 1], G1[:, :, 0], lmask[:, lev].unsqueeze(1).to_broadcast([P, 4, P]), ALU.mult)\
                        .then_inc(G.sem, G.one(f"inv{lev}mask"))
                G.end()

            @block.gpsimd
            def _(g):
                G.prime(g)
                with g.Fori(0, NI) as i:
                    pool_body(g, i)

    def gdn_phase(l):
        NI = 4
        VA, SA, EA = steps("gdA_vec", True), steps("gdA_act", True), steps("gdA_pe", True)
        V, S, E, G = steps("gdB_vec", True), steps("gdB_act", True), steps("gdB_pe", True), steps("gdB_pool", True)
        VG, EG = steps("gdG_vec", True), steps("gdG_pe", True)
        V0, S0, E0 = steps("gd0_vec"), steps("gd0_act"), steps("gd0_pe")
        loaded = [lsem(f"gd_tile{s}") for s in range(4)]
        loaded_g = [lsem(f"gdG_tile{s}") for s in range(4)]
        pload = lsem("gd_params")
        r_ = Region(BRANCH)
        par = r_(8, 12)
        nw = r_(1)
        wab = r_(KT, 16)
        rows = r_(2, 8, 2)
        ab = r_(NB, 16)
        al, ea, e0, z0, z1, m0 = (r_(8, 2) for _ in range(6))
        GA = r_(4, 16)
        st = r_(4, 4)
        Z = r_(8, T)
        GZ = r_(2, T)
        GB = r_(2, 4, P)
        sq, rs = r_(4, T), r_(4, T)
        KQ = r_(4, 2, P)
        KN, DT, DTs, DTi, eg, nkbe, qe = (r_(4, P) for _ in range(7))
        NLT, QKT, Kt, Vt = r_(4, P), r_(4, P), r_(4, P), r_(4, P)
        NLM = r_(6, 4, P)
        T_, TT, X = r_(4, P), r_(4, P), r_(4, P)
        Us, Rs, St = r_(2, P), r_(2, P), r_(2, P)
        O = r_(NB, 2, P)
        O4 = O.rearrange("p b h c -> p (b h) c")
        va4 = r_(4)
        b2, b3, b4, b5, b6, b7 = banks[2:8]
        four = lambda b: b[:, :].rearrange("p (m c) -> p m c", m=4)
        qs = Z[:, 0:2].rearrange("p h (b c) -> p (h b) c", b=NB)
        ks = Z[:, 2:4].rearrange("p h (b c) -> p (h b) c", b=NB)
        rsq = rs[:, 0:2].rearrange("p h (b c) -> p (h b) c", b=NB)
        rsk = rs[:, 2:4].rearrange("p h (b c) -> p (h b) c", b=NB)
        bc4 = lambda x: x.unsqueeze(1).to_broadcast([P, 4, P])

        with nc.Block() as block:
            @block.sync
            def _(sp):
                sp.dma_start(wab, A["gdn_ab"][l]).then_inc(pload, 16)
                sp.dma_start(par, A["gdn_par"][l]).then_inc(pload, 16)
                sp.dma_start(nw, A["gdn_norm"][l]).then_inc(pload, 16)
                sp.dma_start(rows, A["gdn_rows"][l]).then_inc(pload, 16)

                def tile_a(i, s):
                    sp.dma_start(ring[:, s % 4, :], A["w_gdn"][l, i, s]).then_inc(loaded[s % 4], 16)

                def tile_g(i, n):
                    sp.dma_start(ring[:, 4 + n, :], A["w_gdn_side"][l, i, n]).then_inc(loaded_g[n], 16)

                for s in range(4):
                    tile_a(0, s)
                for s in range(4, 8):
                    sp.wait_ge(EA.sem, EA.at(f"z{s - 4}", 0))
                    tile_a(0, s)
                for n in range(4):
                    tile_g(0, n)
                with sp.Fori(1, NI) as i:
                    for s in range(4):
                        sp.wait_ge(EA.sem, EA.before(f"z{s + 4}", i))
                        tile_a(i, s)
                    for n in range(3):
                        sp.wait_ge(EG.sem, EG.before(f"g{n}", i))
                        tile_g(i, n)
                    for s in range(4, 8):
                        sp.wait_ge(EA.sem, EA.at(f"z{s - 4}", i))
                        tile_a(i, s)
                    sp.wait_ge(EG.sem, EG.before("g3", i))
                    tile_g(i, 3)

            ps_a = [banks[(s + 1) % 2][:, 0:T] for s in range(8)]
            ps_g = [banks[n % 2][:, 0:T] for n in range(4)]

            def pe_piece(te, i, s, parts=range(4), first=False):
                for part in parts:
                    if part == 0:
                        te.wait_ge(loaded[s % 4], 32 * i + 16 * (s // 4) + 16)
                        if s >= 2:
                            te.wait_ge(VA.sem, VA.at(f"tap3_{s - 2}", i))
                        elif not first:
                            te.wait_ge(VG.sem, VG.at(f"g{s + 1}", i - 1))
                    mm = project(te, ps_a[s], s % 4, ks=range(2 * part, 2 * part + 2))
                    if part == 3:
                        mm.then_inc(EA.sem, EA.one(f"z{s}"))

            def pe_side(te, i, n, more):
                te.wait_ge(loaded_g[n], 16 * i + 16)
                if n == 0:
                    te.wait_ge(SA.sem, SA.at("z7", i))
                elif n == 1:
                    te.wait_ge(VG.sem, VG.before("g3", i))
                elif n == 2:
                    te.wait_ge(VG.sem, VG.at("g0", i))
                elif more:
                    te.wait_ge(SA.sem, SA.at("z6", i + 1))
                else:
                    te.wait_ge(VG.sem, VG.at("g1", i))
                project(te, ps_g[n], 4 + n, (ya, yc)[n // 2]).then_inc(EG.sem, EG.one(f"g{n}"))

            def vec_side(v, i, n):
                v.wait_ge(EG.sem, EG.at(f"g{n}", i))
                z = zg[:, (0, 2)[n // 2], 2 * i + n % 2]
                v.tensor_tensor(z, z, ps_g[n], ALU.mult).then_inc(VG.sem, VG.one(f"g{n}"))

            def act_piece(a, i, s):
                if s == 0:
                    a.wait_ge(V.sem, V.before("KN", i))
                    a.wait_ge(E.sem, E.before("vT", i))
                a.wait_ge(EA.sem, EA.at(f"z{s}", i))
                if s < 6:
                    w3 = par[:, 2 * i + s % 2, 4 * (s // 2) + 3:4 * (s // 2) + 4]
                    a.activation(Z[:, s, :], ps_a[s], ACT.Copy, scale=w3).then_inc(SA.sem, SA.one(f"z{s}"))
                else:
                    a.activation(Z[:, s, :], ps_a[s], ACT.Copy).then_inc(SA.sem, SA.one(f"z{s}"))

            def vec_piece(v, i, s):
                if s >= 6:
                    return
                v.wait_ge(SA.sem, SA.at(f"z{s}", i))
                for sh in (1, 2, 3):
                    if sh > 1:
                        v.wait_ge(VA.sem, VA.now(i))
                    tap = 4 * (s // 2) + 3 - sh
                    v.scalar_tensor_tensor(Z[:, s, sh:T], ps_a[s][:, 0:T - sh], par[:, 2 * i + s % 2, tap:tap + 1],
                                           Z[:, s, sh:T], ALU.mult, ALU.add).then_inc(VA.sem, VA.one(f"tap{sh}_{s}"))

            def pe_body(te, i, more):
                def fill(n, y):
                    if more:
                        pe_piece(te, i + 1, n, (range(3), range(3, 4))[y])

                if more:
                    EA.begin()
                EG.begin()
                E.begin()
                pe_side(te, i, 0, more)
                te.wait_ge(V.sem, V.before("y", i))
                te.wait_ge(V.sem, V.at("sq", i))
                for x, bk in enumerate((b2, b3)):
                    te.matmul(bk[:, :], ones[:], sq[:, 2 * x:2 * x + 2], start=True, stop=True).then_inc(E.sem, E.one(f"ss{x}"))
                for x, (bk, m) in enumerate(((b4, upto), (b5, ident))):
                    for q in range(4):
                        mm = te.matmul(four(bk)[:, q], GB[:, x, q], m[:], start=True, stop=True)
                    mm.then_inc(E.sem, E.one(("gcrow", "brow")[x]))
                for q in range(4):
                    mm = te.transpose(four(b7)[:, q], Z[:, 4 + q // 2, (q % 2) * P:(q % 2 + 1) * P], ident[:])
                mm.then_inc(E.sem, E.one("vT"))
                pe_side(te, i, 1, more)
                pe_side(te, i, 2, more)
                te.wait_ge(V.sem, V.at("KN", i))
                for q in range(4):
                    mm = te.transpose(four(b6)[:, q], KN[:, q], ident[:])
                mm.then_inc(E.sem, E.one("kT"))
                te.wait_ge(V.sem, V.at("kb", i))
                for q in range(4):
                    bk = (b2, b3)[q // 2]
                    mm = te.matmul(bk[:, (q % 2) * T:(q % 2 + 1) * T], KN[:, q], KQ[:, q], start=True, stop=True)
                    if q % 2:
                        mm.then_inc(E.sem, E.one(f"g{q // 2}"))
                fill(0, 0)
                fill(0, 1)
                te.wait_ge(S.sem, S.at("eg", i))
                te.wait_ge(V.sem, V.at("TT0", i))
                for q in range(4):
                    mm = te.transpose(four(b4)[:, q], TT[:, q], ident[:])
                mm.then_inc(E.sem, E.one("T0"))
                te.wait_ge(V.sem, V.at("QKT", i))
                invert_levels(te, None, None, None, "inv", E, S, V, G, i, NLM, T_, TT, X, b5, b2, b3, N_LEVELS, fill)
                te.wait_ge(V.sem, V.at("inv6TT", i))
                te.wait_ge(S.sem, S.at("Vt", i))
                two = lambda b: b[:, 0:2 * P].rearrange("p (h c) -> p h c", h=2)
                for hh in range(2):
                    mm = te.matmul(two(b6)[:, hh], TT[:, 2 * hh], Vt[:, 2 * hh], start=True, stop=True)
                mm.then_inc(E.sem, E.one("U0"))
                te.wait_ge(S.sem, S.at("U0", i))
                for hh in range(2):
                    mm = te.matmul(two(b4)[:, hh], Kt[:, 2 * hh], Us[:, hh], start=True, stop=True)
                mm.then_inc(E.sem, E.one("S"))
                for hh in range(2):
                    mm = te.matmul(two(b7)[:, hh], QKT[:, 2 * hh], Us[:, hh], start=True, stop=True)
                mm.then_inc(E.sem, E.one("O0"))
                te.wait_ge(S.sem, S.at("S", i))
                for hh in range(2):
                    mm = te.matmul(two(b5)[:, hh], nkbe[:, 2 * hh + 1], St[:, hh], start=True, stop=True)
                mm.then_inc(E.sem, E.one("R"))
                fill(7, 0)
                fill(7, 1)
                te.wait_ge(V.sem, V.at("R", i))
                for hh in range(2):
                    mm = te.matmul(two(b6)[:, hh], TT[:, 2 * hh + 1], Rs[:, hh], start=True, stop=True)
                mm.then_inc(E.sem, E.one("U1"))
                te.wait_ge(S.sem, S.at("U1", i))
                for hh in range(2):
                    te.matmul(two(b2)[:, hh], qe[:, 2 * hh + 1], St[:, hh], start=True, stop=False)
                    mm = te.matmul(two(b2)[:, hh], QKT[:, 2 * hh + 1], Us[:, hh], start=False, stop=True)
                mm.then_inc(E.sem, E.one("O1"))
                pe_side(te, i, 3, more)
                te.wait_ge(V.sem, V.at("on", i))
                for hh in range(2):
                    for b in range(NB):
                        mm = te.transpose(four(b3)[:, 2 * hh + b], O[:, b, hh], ident[:])
                mm.then_inc(E.sem, E.one("yT"))
                E.end()
                EG.end()
                if more:
                    EA.end()

            @block.tensor
            def _(te):
                te.wait_ge(pload, 64)
                for b in range(NB):
                    for k in range(KT):
                        mm = te.matmul(b2[:, 16 * b:16 * b + 16], xn[:, k, b * P:(b + 1) * P], wab[:, k], start=(k == 0), stop=(k == KT - 1))
                mm.then_inc(E0.sem, E0.one("ab"))
                EA.prime(te)
                E.prime(te)
                EG.prime(te)
                EA.begin()
                for s in range(8):
                    pe_piece(te, 0, s, first=True)
                EA.end()
                te.wait_ge(V0.sem, V0.at("g"))
                te.matmul(b3[:, 0:16], upto[:], GA[:, 0], start=True, stop=True)
                te.matmul(b3[:, 16:32], after[:], GA[:, 0], start=True, stop=True).then_inc(E0.sem, E0.one("gc"))
                te.wait_ge(S0.sem, S0.at("erev"))
                with te.Fori(0, NI - 1) as i:
                    pe_body(te, i, True)
                pe_body(te, NI - 1, False)

            def act_body(a, i, more):
                def fill(n):
                    if more:
                        act_piece(a, i + 1, n)

                if more:
                    SA.begin()
                S.begin()
                a.wait_ge(SA.sem, SA.at("z7", i))
                a.wait_ge(VA.sem, VA.at("tap3_5", i))
                a.wait_ge(V.sem, V.before("y", i))
                a.activation(Z[:, 0:6], Z[:, 0:6], ACT.Silu).then_inc(S.sem, S.one("silu"))
                a.activation(GZ, Z[:, 6:8], ACT.Silu).then_inc(S.sem, S.one("siluz"))
                a.wait_ge(V.sem, V.at("rs0", i))
                a.activation(rs, rs, ACT.Sqrt).then_inc(S.sem, S.one("rs"))
                a.wait_ge(V.sem, V.at("DT0", i))
                a.activation(DT, DT, ACT.Exp).then_inc(S.sem, S.one("DT"))
                a.activation(eg, four(b4), ACT.Exp).then_inc(S.sem, S.one("eg"))
                a.wait_ge(E.sem, E.at("vT", i))
                for q in range(4):
                    a.activation(Vt[:, q], four(b7)[:, q], ACT.Copy, scale=st[:, 1, q:q + 1]).then_inc(S.sem, S.one("Vt"))
                a.wait_ge(E.sem, E.at("kT", i))
                for q in range(4):
                    a.activation(Kt[:, q], four(b6)[:, q], ACT.Copy, scale=st[:, 3, q:q + 1]).then_inc(S.sem, S.one("Kt"))
                fill(0)
                a.wait_ge(E.sem, E.at("T0", i))
                a.activation(T_, four(b4), ACT.Copy).then_inc(S.sem, S.one("invT"))
                invert_levels(None, a, None, None, "inv", E, S, V, G, i, NLM, T_, TT, X, b5, b2, b3, N_LEVELS, fill)
                two = lambda b: b[:, 0:2 * P].rearrange("p (h c) -> p h c", h=2)
                a.wait_ge(E.sem, E.at("U0", i))
                a.activation(Us, two(b6), ACT.Copy).then_inc(S.sem, S.one("U0"))
                a.wait_ge(E.sem, E.at("S", i))
                a.activation(St, two(b4), ACT.Copy).then_inc(S.sem, S.one("S"))
                a.wait_ge(E.sem, E.at("O0", i))
                a.activation(O[:, 0], two(b7), ACT.Copy).then_inc(S.sem, S.one("O0"))
                fill(7)
                a.wait_ge(E.sem, E.at("U1", i))
                a.activation(Us, two(b6), ACT.Copy).then_inc(S.sem, S.one("U1"))
                a.wait_ge(E.sem, E.at("O1", i))
                a.activation(O[:, 1], two(b2), ACT.Copy).then_inc(S.sem, S.one("O1"))
                a.wait_ge(V.sem, V.at("var", i))
                a.activation(va4, va4, ACT.Sqrt).then_inc(S.sem, S.one("sd"))
                S.end()
                if more:
                    SA.end()

            @block.scalar
            def _(a):
                a.wait_ge(pload, 64)
                a.wait_ge(E0.sem, E0.at("ab"))
                a.activation(ab, b2[:, 0:32].rearrange("p (b j) -> p b j", b=NB), ACT.Copy).then_inc(S0.sem, S0.one("ab"))
                a.activation(ea, rows[:, 0], ACT.Exp).then_inc(S0.sem, S0.one())
                a.wait_ge(V0.sem, V0.at("al"))
                softplus_exp(a, S0, al, e0, "sp")
                a.activation(GA[:, 1].rearrange("p (h b) -> p h b", b=NB), ab[:, :, 8:16].rearrange("p b h -> p h b"),
                             ACT.Sigmoid).then_inc(S0.sem, S0.one("beta"))
                SA.prime(a)
                S.prime(a)
                SA.begin()
                for s in range(8):
                    act_piece(a, 0, s)
                SA.end()
                a.wait_ge(E0.sem, E0.at("gc"))
                a.activation(GA[:, 2], b3[:, 0:16], ACT.Copy).then_inc(S0.sem, S0.one())
                a.activation(GA[:, 3], b3[:, 16:32], ACT.Exp).then_inc(S0.sem, S0.one("erev"))
                with a.Fori(0, NI - 1) as i:
                    act_body(a, i, True)
                act_body(a, NI - 1, False)

            def vec_body(v, i, more):
                def fill(n):
                    if more:
                        vec_piece(v, i + 1, n)

                if more:
                    VA.begin()
                VG.begin()
                V.begin()
                v.wait_ge(S.sem, S.before("Kt", i))
                v.tensor_copy(st, GA[:, :, bass.ds(4 * i, 4)]).then_inc(V.sem, V.one("st"))
                v.wait_ge(V.sem, V.now(i))
                v.tensor_copy(GB, st[:, 0:2].unsqueeze(3).to_broadcast([P, 2, 4, P])).then_inc(V.sem, V.one("GB"))
                v.wait_ge(S.sem, S.at("silu", i))
                v.tensor_tensor(sq, Z[:, 0:4], Z[:, 0:4], ALU.mult).then_inc(V.sem, V.one("sq"))
                for x, bk in enumerate((b2, b3)):
                    v.wait_ge(E.sem, E.at(f"ss{x}", i))
                    v.tensor_scalar(rs[:, 2 * x:2 * x + 2], bk[:, :].rearrange("p (h t) -> p h t", h=2), EPS, None, ALU.add)\
                        .then_inc(V.sem, V.one("rs0"))
                v.wait_ge(E.sem, E.at("gcrow", i))
                for q in range(4):
                    v.tensor_scalar(DT[:, q], four(b4)[:, q], st[:, 2, q:q + 1], 0.0, ALU.subtract, ALU.min)\
                        .then_inc(V.sem, V.one("DT0"))
                vec_side(v, i, 0)
                v.wait_ge(S.sem, S.at("rs", i))
                v.reciprocal(rs, rs).then_inc(V.sem, V.one())
                v.wait_ge(V.sem, V.now(i))
                v.tensor_tensor(KN, ks, rsk, ALU.mult).then_inc(V.sem, V.one())
                v.scalar_tensor_tensor(KQ[:, :, 1], qs, GDN_SCALE, rsq, ALU.mult, ALU.mult).then_inc(V.sem, V.one("KN"))
                v.wait_ge(V.sem, V.now(i))
                v.wait_ge(E.sem, E.at("brow", i))
                v.tensor_tensor(KQ[:, :, 0], KN, four(b5), ALU.mult).then_inc(V.sem, V.one("kb"))
                vec_side(v, i, 1)
                v.wait_ge(S.sem, S.at("DT", i))
                v.tensor_tensor(DTs, DT, bc4(gmask[:, 0]), ALU.mult).then_inc(V.sem, V.one())
                v.tensor_tensor(DTi, DT, bc4(gmask[:, 1]), ALU.mult).then_inc(V.sem, V.one())
                v.wait_ge(V.sem, V.now(i))
                for x, bk in enumerate((b2, b3)):
                    ps = bk[:, :].rearrange("p (m x c) -> p m x c", m=2, x=2)
                    v.wait_ge(E.sem, E.at(f"g{x}", i))
                    v.scalar_tensor_tensor(NLT[:, 2 * x:2 * x + 2], ps[:, :, 0], -1.0, DTs[:, 2 * x:2 * x + 2], ALU.mult, ALU.mult)\
                        .then_inc(V.sem, V.one(f"NLT{x}"))
                v.wait_ge(V.sem, V.now(i))
                v.tensor_tensor(TT, NLT, bc4(lmask[:, 0]), ALU.mult).then_inc(V.sem, V.one())
                v.wait_ge(V.sem, V.now(i))
                v.tensor_tensor(TT, TT, bc4(ident[:]), ALU.add).then_inc(V.sem, V.one("TT0"))
                vec_side(v, i, 2)
                for x, bk in enumerate((b2, b3)):
                    ps = bk[:, :].rearrange("p (m x c) -> p m x c", m=2, x=2)
                    v.tensor_tensor(QKT[:, 2 * x:2 * x + 2], ps[:, :, 1], DTi[:, 2 * x:2 * x + 2], ALU.mult)\
                        .then_inc(V.sem, V.one("QKT"))
                v.wait_ge(S.sem, S.at("eg", i))
                v.scalar_tensor_tensor(nkbe, KQ[:, :, 0], -1.0, eg, ALU.mult, ALU.mult).then_inc(V.sem, V.one())
                v.tensor_tensor(qe, KQ[:, :, 1], eg, ALU.mult).then_inc(V.sem, V.one("qe"))
                fill(0)
                v.wait_ge(S.sem, S.at("invT", i))
                invert_levels(None, None, v, None, "inv", E, S, V, G, i, NLM, T_, TT, X, b5, b2, b3, N_LEVELS, fill)
                two = lambda b: b[:, 0:2 * P].rearrange("p (h c) -> p h c", h=2)
                v.wait_ge(E.sem, E.at("R", i))
                v.wait_ge(S.sem, S.at("Vt", i))
                v.tensor_tensor(Rs, two(b5), Vt.rearrange("p (h b) c -> p h b c", h=2)[:, :, 1], ALU.add).then_inc(V.sem, V.one("R"))
                fill(7)
                v.wait_ge(S.sem, S.at("O1", i))
                v.tensor_tensor(eg, O4, O4, ALU.mult).then_inc(V.sem, V.one())
                v.wait_ge(V.sem, V.now(i))
                v.tensor_reduce(va4, eg, AX.X, ALU.add).then_inc(V.sem, V.one())
                v.wait_ge(V.sem, V.now(i))
                v.tensor_scalar(va4, va4, 1.0 / P, EPS, ALU.mult, ALU.add).then_inc(V.sem, V.one("var"))
                v.wait_ge(S.sem, S.at("sd", i))
                v.reciprocal(va4, va4).then_inc(V.sem, V.one())
                v.wait_ge(V.sem, V.now(i))
                v.tensor_tensor(O4, O4, va4.unsqueeze(2).to_broadcast([P, 4, P]), ALU.mult).then_inc(V.sem, V.one("on"))
                v.wait_ge(E.sem, E.at("yT", i))
                v.scalar_tensor_tensor(yb[:, bass.ds(2 * i, 2)], b3[:, :].rearrange("p (h t) -> p h t", h=2), nw, GZ, ALU.mult, ALU.mult)\
                    .then_inc(V.sem, V.one("y"))
                vec_side(v, i, 3)
                V.end()
                VG.end()
                if more:
                    VA.end()

            @block.vector
            def _(v):
                v.wait_ge(pload, 64)
                v.wait_ge(S0.sem, S0.at("ab"))
                v.tensor_tensor(al, ab[:, :, 0:8].rearrange("p b h -> p h b"), rows[:, 1], ALU.add).then_inc(V0.sem, V0.one("al"))
                v.wait_ge(V0.sem, V0.now())
                v.wait_ge(S0.sem, S0.at("sp_e"))
                softplus_log(v, V0, al, e0, z0, z1, m0, e0)
                v.wait_ge(V0.sem, V0.now())
                v.scalar_tensor_tensor(GA[:, 0].rearrange("p (h b) -> p h b", b=NB), m0, -1.0, ea, ALU.mult, ALU.mult)\
                    .then_inc(V0.sem, V0.one("g"))
                v.wait_ge(S0.sem, S0.at("beta"))
                VA.prime(v)
                V.prime(v)
                VG.prime(v)
                VA.begin()
                for s in range(8):
                    vec_piece(v, 0, s)
                VA.end()
                v.wait_ge(S0.sem, S0.at("erev"))
                with v.Fori(0, NI - 1) as i:
                    vec_body(v, i, True)
                vec_body(v, NI - 1, False)

            @block.gpsimd
            def _(g):
                G.prime(g)
                with g.Fori(0, NI) as i:
                    G.begin()
                    g.wait_ge(V.sem, V.at("NLT1", i))
                    for lev in range(1, N_LEVELS):
                        g.tensor_tensor(NLM[:, lev - 1], NLT, bc4(lmask[:, lev]), ALU.mult).then_inc(G.sem, G.one(f"inv{lev}mask"))
                    G.end()

    def merge_phase(l):
        V, E = steps("mg_vec", True), steps("mg_pe", True)
        V2, E2 = steps("wo_vec", True), steps("wo_pe", True)
        VS = steps("mg0_vec")
        loaded = [lsem(f"mg_tile{s}") for s in range(4)]
        loaded2 = [lsem(f"wo_tile{s}") for s in range(4)]
        r_ = Region(BRANCH)
        merged = r_(KT, T)
        with nc.Block() as block:
            @block.sync
            def _(sp):
                for k in range(4):
                    sp.dma_start(ring[:, k, :], A["p_gdn"][l, k]).then_inc(loaded[k], 16)
                for k in range(4):
                    sp.dma_start(ring[:, 4 + k, :], A["w_out"][l, k]).then_inc(loaded2[k], 16)
                for k in range(4):
                    sp.wait_ge(E.sem, E.at(f"z{k}", 0))
                    sp.dma_start(ring[:, k, :], A["p_gdn"][l, 4 + k]).then_inc(loaded[k], 16)
                for k in range(4):
                    sp.wait_ge(E2.sem, E2.at(f"o{k}", 0))
                    sp.dma_start(ring[:, 4 + k, :], A["w_out"][l, 4 + k]).then_inc(loaded2[k], 16)

            @block.tensor
            def _(te):
                E.prime(te)
                with te.Fori(0, 2) as i:
                    E.begin()
                    for s in range(4):
                        te.wait_ge(loaded[s], 16 * i + 16)
                        te.wait_ge(V.sem, V.before(f"t{s}", i))
                        project(te, banks[s][:, 0:T], s, yb).then_inc(E.sem, E.one(f"z{s}"))
                    E.end()
                te.wait_ge(V.sem, V.at("m3", 1))
                E2.prime(te)
                with te.Fori(0, 2) as i:
                    E2.begin()
                    for s in range(4):
                        te.wait_ge(loaded2[s], 16 * i + 16)
                        te.wait_ge(V2.sem, V2.before(f"h{s}", i))
                        project(te, banks[4 + s][:, 0:T], 4 + s, merged).then_inc(E2.sem, E2.one(f"o{s}"))
                    E2.end()

            @block.vector
            def _(v):
                v.tensor_tensor(zg[:, 0], zg[:, 0], zg[:, 2], ALU.add).then_inc(VS.sem, VS.one("sum"))
                v.wait_ge(VS.sem, VS.at("sum"))
                V.prime(v)
                V2.prime(v)
                with v.Fori(0, 2) as i:
                    V.begin()
                    for s in range(4):
                        v.wait_ge(E.sem, E.at(f"z{s}", i))
                        v.tensor_tensor(zg[:, 1, 4 * i + s], zg[:, 1, 4 * i + s], banks[s][:, 0:T], ALU.mult)\
                            .then_inc(V.sem, V.one(f"t{s}"))
                        v.wait_ge(V.sem, V.now(i))
                        v.tensor_tensor(merged[:, 4 * i + s], zg[:, 0, 4 * i + s], zg[:, 1, 4 * i + s], ALU.add)\
                            .then_inc(V.sem, V.one(f"m{s}"))
                    V.end()
                with v.Fori(0, 2) as i:
                    V2.begin()
                    for s in range(4):
                        v.wait_ge(E2.sem, E2.at(f"o{s}", i))
                        v.tensor_tensor(h[:, 4 * i + s], h[:, 4 * i + s], banks[4 + s][:, 0:T], ALU.add).then_inc(V2.sem, V2.one(f"h{s}"))
                    V2.end()
                v.wait_ge(V2.sem, V2.at("h3", 1))

    PQ = Region(PEER)
    scores = PQ(NB, 2 * PH, NK)
    f32r = lambda ap: ap.bitcast(F32R)

    def peer_query_phase(l):
        NI = 4
        V, S, E = steps("pq_vec", True), steps("pq_act", True), steps("pq_pe", True)
        loaded = [lsem(f"pq_tile{s}") for s in range(4)]
        pload = lsem("pq_keys")
        x_high, x_low = lsem("pq_x_high"), lsem("pq_x_low")
        r_ = Region(PQ.at_)
        keys = r_(2 * PH, NK)
        q = r_(4, T)
        with nc.Block() as block:
            @block.sync
            def _(sp):
                sp.dma_start(keys, A["keys"][l]).then_inc(pload, 16)
                load_slots(sp, lambda i, s: A["w_query"][l, i, s], loaded, E, [f"q{s}" for s in range(4)], NI)

            @block.tensor
            def _(te):
                def score(i, s):
                    te.wait_ge(S.sem, S.at(f"q{s}", i))
                    te.wait_ge(V.sem, V.before(f"s{s}", i))
                    for b in range(NB):
                        mm = te.matmul(banks[4 + s][:, b * NK:(b + 1) * NK], q[:, s, b * P:(b + 1) * P], keys[:, 4 * i + s],
                                       start=True, stop=True)
                    mm.then_inc(E.sem, E.one(f"s{s}"))

                te.wait_ge(pload, 16)
                E.prime(te)
                with te.Fori(0, NI) as i:
                    E.begin()
                    for s in range(4):
                        te.wait_ge(loaded[s], 16 * i + 16)
                        te.wait_ge(S.sem, S.before(f"q{s}", i))
                        project(te, banks[s][:, 0:T], s).then_inc(E.sem, E.one(f"q{s}"))
                        if s:
                            score(i, s - 1)
                    score(i, 3)
                    E.end()

            @block.scalar
            def _(a):
                a.activation(f32r(xhigh[:]), xn, ACT.Copy).then_inc(x_high, 1)
                S.prime(a)
                with a.Fori(0, NI) as i:
                    S.begin()
                    for s in range(4):
                        a.wait_ge(E.sem, E.at(f"q{s}", i))
                        a.activation(q[:, s], banks[s][:, 0:T], ACT.Copy).then_inc(S.sem, S.one(f"q{s}"))
                    S.end()

            @block.vector
            def _(v):
                v.wait_ge(x_high, 1)
                v.tensor_tensor(f32r(xlow[:]), xn, xhigh[:], ALU.subtract).then_inc(x_low, 1)
                V.prime(v)
                with v.Fori(0, NI) as i:
                    V.begin()
                    for s in range(4):
                        v.wait_ge(E.sem, E.at(f"s{s}", i))
                        v.tensor_copy(scores[:, :, 4 * i + s], banks[4 + s][:, 0:T].rearrange("p (b k) -> p b k", b=NB))\
                            .then_inc(V.sem, V.one(f"s{s}"))
                    V.end()
                v.wait_ge(V.sem, V.at("s3", NI - 1))
                v.wait_ge(x_low, 1)

    def peer_topk_phase(l):
        V, S, E = steps("tk_vec", True), steps("tk_act", True), steps("tk_pe", True)
        r_ = Region(PQ.at_)
        NS = 2 * PH
        s0, s1 = r_(NS, NK), r_(NS, NK)
        top, topi, topf = r_(NS, TOPK), r_(NS, TOPK, dt=U32), r_(NS, TOPK)
        cand, cand1 = r_(PH, TOPK * TOPK), r_(PH, TOPK * TOPK)
        best, pos = r_(PH, TOPK), r_(PH, TOPK, dt=U32)
        pi, pf = r_(PH, TOPK, dt=U32), r_(PH * TOPK)
        eq = r_(PH * TOPK, TOPK)
        e1, e2 = r_(PH, TOPK), r_(PH, TOPK)
        gate, gsum, dummy = r_(PH, TOPK), r_(PH), r_(1)
        WORST = -3.0e38
        side = lambda x, q: x.rearrange("p (h s) k -> p h s k", s=2)[:, :, q]
        flat = lambda x: x.rearrange("p h k -> p (h k)")
        with nc.Block() as block:
            @block.vector
            def _(v):
                V.prime(v)
                with v.Fori(0, NB) as i:
                    V.begin()
                    v.tensor_copy(s0, scores[:, i]).then_inc(V.sem, V.one("copy"))

                    def settled():
                        v.wait_ge(V.sem, V.now(i))
                        v.memset(dummy, 0.0).then_inc(V.sem, V.one())

                    def best16(n, x, x1, vals, idx):
                        settled()
                        for k in range(n):
                            v.max(vals[:, k, 0:8], x[:, k]).then_inc(V.sem, V.one())
                        settled()
                        for k in range(n):
                            v.max_index(idx[:, k, 0:8], vals[:, k, 0:8], x[:, k]).then_inc(V.sem, V.one())
                            v.match_replace(x1[:, k], vals[:, k, 0:8], x[:, k], WORST).then_inc(V.sem, V.one())
                        settled()
                        for k in range(n):
                            v.max(vals[:, k, 8:16], x1[:, k]).then_inc(V.sem, V.one())
                        settled()
                        for k in range(n):
                            v.max_index(idx[:, k, 8:16], vals[:, k, 8:16], x1[:, k]).then_inc(V.sem, V.one())
                        v.wait_ge(V.sem, V.now(i))

                    best16(NS, s0, s1, top, topi)
                    v.tensor_copy(topf, topi).then_inc(V.sem, V.one())
                    for a in range(TOPK):
                        v.tensor_tensor(cand[:, :, a * TOPK:(a + 1) * TOPK],
                                        side(top, 0)[:, :, a:a + 1].to_broadcast([P, PH, TOPK]), side(top, 1), ALU.add)\
                            .then_inc(V.sem, V.one())
                    best16(PH, cand, cand1, best, pos)
                    for q, (dst, op, arg) in enumerate(((e1, ALU.logical_shift_right, 4), (e2, ALU.bitwise_and, 15))):
                        v.tensor_scalar(pi, pos, arg, None, op).then_inc(V.sem, V.one())
                        v.wait_ge(V.sem, V.now(i))
                        v.tensor_copy(pf, flat(pi)).then_inc(V.sem, V.one())
                        v.wait_ge(V.sem, V.now(i))
                        v.tensor_tensor(eq, pf.unsqueeze(2).to_broadcast([P, PH * TOPK, TOPK]),
                                        iota[:, 0:TOPK].unsqueeze(1).to_broadcast([P, PH * TOPK, TOPK]), ALU.is_equal)\
                            .then_inc(V.sem, V.one())
                        v.wait_ge(V.sem, V.now(i))
                        eq4 = eq.rearrange("p (h k) a -> p h k a", h=PH)
                        v.tensor_tensor(eq4, eq4, side(topf, q).unsqueeze(2).to_broadcast([P, PH, TOPK, TOPK]), ALU.mult)\
                            .then_inc(V.sem, V.one())
                        v.wait_ge(V.sem, V.now(i))
                        v.tensor_reduce(flat(dst), eq, AX.X, ALU.add).then_inc(V.sem, V.one())
                        v.wait_ge(V.sem, V.now(i))
                    v.tensor_tensor(gate, best, best[:, :, 0:1].to_broadcast([P, PH, TOPK]), ALU.subtract).then_inc(V.sem, V.one("e"))
                    v.wait_ge(S.sem, S.at("exp", i))
                    v.tensor_reduce(gsum, gate, AX.X, ALU.add).then_inc(V.sem, V.one())
                    v.wait_ge(V.sem, V.now(i))
                    v.reciprocal(gsum, gsum).then_inc(V.sem, V.one())
                    v.wait_ge(V.sem, V.now(i))
                    v.tensor_tensor(gate, gate, gsum.unsqueeze(2).to_broadcast([P, PH, TOPK]), ALU.mult).then_inc(V.sem, V.one("gate"))
                    for n, dst in enumerate((slot1, slot2, slotg)):
                        v.wait_ge(E.sem, E.at(f"t{n}", i))
                        v.tensor_copy(dst[:, bass.ds(i * P, P)], banks[n][:, 0:P]).then_inc(V.sem, V.one(f"c{n}"))
                    v.wait_ge(V.sem, V.now(i))
                    V.end()

            @block.scalar
            def _(a):
                S.prime(a)
                with a.Fori(0, NB) as i:
                    S.begin()
                    a.wait_ge(V.sem, V.at("e", i))
                    a.activation(gate, gate, ACT.Exp).then_inc(S.sem, S.one("exp"))
                    S.end()

            @block.tensor
            def _(te):
                E.prime(te)
                with te.Fori(0, NB) as i:
                    E.begin()
                    te.wait_ge(V.sem, V.at("gate", i))
                    for n, src in enumerate((e1, e2, gate)):
                        te.transpose(banks[n][:, 0:P], flat(src), ident[:]).then_inc(E.sem, E.one(f"t{n}"))
                    E.end()

    GATES = arena[:, :].rearrange("p (t j) -> p t j", t=T)

    def peer_gate_phase(l):
        NI = T // 8
        onehot = ring[:, :, :].rearrange("p s c -> p (s c)")
        V, S, E = steps("gt_vec", True), steps("gt_act", True), steps("gt_pe", True)
        oh1 = onehot[:, 0:8 * P].rearrange("p (u k) -> p u k", u=8)
        oh2 = onehot[:, 8 * P:16 * P].rearrange("p (u k) -> p u k", u=8)
        with nc.Block() as block:
            @block.vector
            def _(v):
                V.prime(v)
                with v.Fori(0, NI) as i:
                    V.begin()
                    for u in range(8):
                        tok = bass.ds(8 * i + u, 1)
                        if u % 4 == 0:
                            v.wait_ge(E.sem, E.before(f"g{u // 4}", i))
                        v.tensor_scalar(oh1[:, u], iota[:], slot1[:, tok], None, ALU.is_equal).then_inc(V.sem, V.one())
                        v.tensor_scalar(oh2[:, u], iota[:], slot2[:, tok], slotg[:, tok], ALU.is_equal, ALU.mult)\
                            .then_inc(V.sem, V.one(f"u{u}"))
                    V.end()

            @block.tensor
            def _(te):
                E.prime(te)
                with te.Fori(0, NI) as i:
                    E.begin()
                    for g in range(2):
                        te.wait_ge(S.sem, S.before(f"g{g}", i))
                        for u in range(4 * g, 4 * g + 4):
                            te.wait_ge(V.sem, V.at(f"u{u}", i))
                            mm = te.matmul(banks[g][:, (u % 4) * NK:(u % 4 + 1) * NK], oh1[:, u], oh2[:, u], start=True, stop=True)
                        mm.then_inc(E.sem, E.one(f"g{g}"))
                    E.end()

            @block.scalar
            def _(a):
                S.prime(a)
                with a.Fori(0, NI) as i:
                    S.begin()
                    for g in range(2):
                        a.wait_ge(E.sem, E.at(f"g{g}", i))
                        a.activation(GATES[:, bass.ds(8 * i + 4 * g, 4)], banks[g][:, :].rearrange("p (u k) -> p u k", u=4), ACT.Copy)\
                            .then_inc(S.sem, S.one(f"g{g}"))
                    S.end()
                a.wait_ge(S.sem, S.at("g1", NI - 1))

    def peer_expert_phase(l):
        FIRST = 4
        UJ = 4
        NI = NK // UJ
        H = KT * P // 2
        names = ("u_high", "u_low", "v_high", "v_low", "hidden", "gelu", "gated", "a_high", "a_low", "mixed")
        u_high, u_low, v_high, v_low, hidden, gelu, gated, a_high, a_low, mixed = [lsem("ex_" + n) for n in names]
        u_in = [lsem(f"ex_u_in{s}") for s in range(2)]
        v_in = [lsem(f"ex_v_in{s}") for s in range(2)]
        opened, added = lsem("ex_opened"), lsem("ex_added")
        u_raw, v_raw = [raw[:, s] for s in range(2)], [raw[:, 2 + s] for s in range(2)]
        u_hi, u_lo, v_hi, v_lo = (parts[:, n] for n in range(4))
        act = [slots[:, s] for s in range(2)]
        ybanks = banks[4:8]
        U = (u_in, u_raw, u_hi, u_lo, u_high, u_low, hidden)
        W = (v_in, v_raw, v_hi, v_lo, v_high, v_low, mixed)

        def start(engine, *sems):
            for s in sems:
                engine.sem_inc(s, FIRST)

        def steps_of(engine, one_step):
            with engine.Fori(0, NI - 1) as i:
                for u in range(UJ):
                    one_step(UJ * i, u)
            for u in range(UJ):
                one_step(UJ * (NI - 1), u)

        ends = lambda j4, u, ahead: isinstance(j4, int) and j4 + u + ahead >= NK
        with nc.Block() as block:
            @block.sync
            def _(sp):
                def load(what, sems, raw, j4, u):
                    sp.dma_start(raw[u % 2], A[what][l, j4 + u]).then_inc(sems[u % 2], 16)

                load("u", u_in, u_raw, 0, 0)
                load("u", u_in, u_raw, 0, 1)
                load("v", v_in, v_raw, 0, 0)
                sp.wait_ge(u_low, FIRST + 2)
                load("u", u_in, u_raw, 0, 2)

                def step(j4, u):
                    if not ends(j4, u, 3):
                        sp.wait_ge(u_low, FIRST + 2 * (j4 + u) + 4)
                        load("u", u_in, u_raw, j4, u + 3)
                    if not ends(j4, u, 1):
                        sp.wait_ge(v_low, FIRST + 2 * (j4 + u))
                        load("v", v_in, v_raw, j4, u + 1)
                steps_of(sp, step)

            @block.tensor
            def _(te):
                def product(ps, w_hi, w_lo, x_hi, x_lo, start, stop, **kw):
                    te.matmul(ps, f32r(w_hi), f32r(x_hi), start=start, stop=False, **kw)
                    te.matmul(ps, f32r(w_hi), f32r(x_lo), start=False, stop=False, **kw)
                    return te.matmul(ps, f32r(w_lo), f32r(x_hi), start=False, stop=stop, **kw)

                def with_u(j4, u):
                    for k in range(KT):
                        if k % (KT // 2) == 0:
                            te.wait_ge(u_low, FIRST + 2 * (j4 + u) + 1 + k // (KT // 2))
                        cols = slice(k * P, (k + 1) * P)
                        mm = product(banks[u % 4][:, 0:T], u_hi[:, cols], u_lo[:, cols], xhigh[:, k], xlow[:, k], k == 0, k == KT - 1)
                        if (k + 1) % (KT // 2) == 0:
                            mm.then_inc(hidden, 1)

                def with_v(j4, u):
                    s = u % 2
                    te.wait_ge(a_low, FIRST + j4 + u + 1)
                    for d in range(KT):
                        if d % (KT // 2) == 0:
                            te.wait_ge(v_low, FIRST + 2 * (j4 + u) + 1 + d // (KT // 2))
                        cols = slice(d * P, (d + 1) * P)
                        mm = product(ybanks[d // 2][:, (d % 2) * T:(d % 2 + 1) * T], v_hi[:, cols], v_lo[:, cols],
                                     act_high[:, s], act_low[:, s], False, False, skip_group_check=True)
                        if (d + 1) % (KT // 2) == 0:
                            mm.then_inc(mixed, 1)

                start(te, hidden, mixed)
                te.wait_ge(opened, 1)
                for y in ybanks:
                    te.matmul(y[:, :], f32r(act_low[:, 0, 0:P]), f32r(xhigh[:, 0:2]), start=True, stop=False, skip_group_check=True)
                with_u(0, 0)
                with_u(0, 1)

                def step(j4, u):
                    if not ends(j4, u, 2):
                        with_u(j4, u + 2)
                    with_v(j4, u)
                steps_of(te, step)

            def halves(j4, u):
                return ((n, slice(n * H, (n + 1) * H), 2 * (j4 + u) + n) for n in range(2))

            @block.scalar
            def _(a):
                def high(tiles, j4, u):
                    arrived, raw, hi, lo, high_done, low_done, used = tiles
                    a.wait_ge(arrived[u % 2], 8 * j4 + 16 * (u // 2) + 16)
                    for n, cols, half_no in halves(j4, u):
                        a.wait_ge(used, FIRST + half_no - 1)
                        a.activation(f32r(hi[:, cols]), raw[u % 2][:, cols], ACT.Copy).then_inc(high_done, 1)

                def gelu_step(j4, u):
                    a.wait_ge(hidden, FIRST + 2 * (j4 + u) + 2)
                    a.wait_ge(a_low, FIRST + j4 + u - 1)
                    a.activation(act[u % 2], banks[u % 4][:, 0:T], ACT.Gelu_apprx_tanh).then_inc(gelu, 1)

                def a_high_step(j4, u):
                    a.wait_ge(gated, FIRST + j4 + u + 1)
                    a.wait_ge(mixed, FIRST + 2 * (j4 + u) - 2)
                    a.activation(f32r(act_high[:, u % 2]), act[u % 2], ACT.Copy).then_inc(a_high, 1)

                start(a, u_high, v_high, gelu, a_high)
                high(U, 0, 0)
                high(U, 0, 1)
                gelu_step(0, 0)
                high(U, 0, 2)
                a_high_step(0, 0)
                high(W, 0, 0)

                def step(j4, u):
                    if not ends(j4, u, 1):
                        gelu_step(j4, u + 1)
                    if not ends(j4, u, 3):
                        high(U, j4, u + 3)
                    if not ends(j4, u, 1):
                        a_high_step(j4, u + 1)
                        high(W, j4, u + 1)
                steps_of(a, step)

            @block.vector
            def _(v):
                def low(tiles, j4, u):
                    arrived, raw, hi, lo, high_done, low_done, used = tiles
                    for n, cols, half_no in halves(j4, u):
                        v.wait_ge(high_done, FIRST + half_no + 1)
                        v.tensor_tensor(f32r(lo[:, cols]), raw[u % 2][:, cols], hi[:, cols], ALU.subtract).then_inc(low_done, 1)

                def gate_step(j4, u):
                    v.wait_ge(gelu, FIRST + j4 + u + 1)
                    v.tensor_tensor(act[u % 2], act[u % 2], GATES[:, :, j4 + u], ALU.mult).then_inc(gated, 1)

                def a_low_step(j4, u):
                    v.wait_ge(a_high, FIRST + j4 + u + 1)
                    v.tensor_tensor(f32r(act_low[:, u % 2]), act[u % 2], act_high[:, u % 2], ALU.subtract).then_inc(a_low, 1)

                start(v, u_low, v_low, gated, a_low)
                v.tensor_scalar(f32r(act_low[:, 0, 0:P]), iota[:], 0.0, None, ALU.mult).then_inc(opened, 1)
                low(U, 0, 0)
                low(U, 0, 1)
                gate_step(0, 0)
                low(U, 0, 2)
                a_low_step(0, 0)
                low(W, 0, 0)

                def step(j4, u):
                    if not ends(j4, u, 1):
                        gate_step(j4, u + 1)
                    if not ends(j4, u, 3):
                        low(U, j4, u + 3)
                    if not ends(j4, u, 1):
                        a_low_step(j4, u + 1)
                        low(W, j4, u + 1)
                steps_of(v, step)
                v.wait_ge(mixed, FIRST + 2 * NK)
                for b, y in enumerate(ybanks):
                    v.tensor_tensor(h[:, 2 * b:2 * b + 2], h[:, 2 * b:2 * b + 2], y[:, :].rearrange("p (d t) -> p d t", d=2), ALU.add)\
                        .then_inc(added, 1)
                v.wait_ge(added, KT // 2)

    final = Steps(sem("final_out"), book, "final", False)
    with nc.Fori(0, L) as l:
        with nc.sbuf_tensor("zg", [P, 3, KT, T], F32) as zg, nc.sbuf_tensor("ring", [P, 8, KT * P], F32) as ring:
            rmsnorm("mixnorm", norm_w[:, 2 * l], xn)
            rwkv_phase(l)
            lru_phase(l)
            gdn_phase(l)
            merge_phase(l)
        with (nc.sbuf_tensor("slots", [P, 3, T], F32) as slots, nc.sbuf_tensor("xhigh", [P, KT, T], F32) as xhigh,
              nc.sbuf_tensor("xlow", [P, KT, T], F32) as xlow, nc.sbuf_tensor("act_high", [P, 2, T], F32) as act_high,
              nc.sbuf_tensor("act_low", [P, 2, T], F32) as act_low):
            slot1, slot2, slotg = (slots[:, n] for n in range(3))
            with nc.sbuf_tensor("ring2", [P, 8, KT * P], F32) as ring:
                rmsnorm("ffnnorm", norm_w[:, 2 * l + 1], xn)
                peer_query_phase(l)
                peer_topk_phase(l)
                peer_gate_phase(l)
            with nc.sbuf_tensor("raw_tiles", [P, 4, KT * P], F32) as raw, nc.sbuf_tensor("tile_parts", [P, 4, KT * P], F32) as parts:
                peer_expert_phase(l)
        with nc.Block() as block:
            @block.sync
            def _(sp):
                for s in cleared:
                    sp.sem_clear(s)
    del cleared[:]
    rmsnorm("outnorm", norm_w[:, 2 * L], xn)
    with nc.Block() as block:
        @block.sync
        def _(sp):
            sp.dma_start(out, xn).then_inc(final.sem, 16)
            sp.wait_ge(final.sem, 16)


def host_layout(x, norm_mix_w, norm_ffn_w, final_norm_w, w_in, lru_conv_w, lru_conv_b, lru_w_a,
                lru_b_a, lru_w_x, lru_b_x, lru_lambda, gdn_conv_w, gdn_a_log, gdn_dt_bias, gdn_norm_w,
                rwkv_mu, rwkv_w0, rwkv_w_up, rwkv_a0, rwkv_a_up, rwkv_g_up, rwkv_k_k, rwkv_k_a,
                rwkv_r_k, rwkv_lnx_w, rwkv_lnx_b, merge_b, p_lru, p_gdn, p_rwkv, w_out,
                peer_wq, peer_keys, peer_u, peer_v):
    import numpy as np

    def tiles(w):
        n = w.shape[2] // P
        return w.reshape(L, KT, P, n, P).transpose(0, 3, 2, 1, 4).reshape(L, n, P, KT * P)

    def chan(v):
        return v.reshape(L, -1, P).transpose(0, 2, 1)

    o = {}
    at = 0
    z = {}
    for name, n in (("u", 1024), ("g", 1024), ("q", 1024), ("k", 1024), ("v", 1024), ("zg", 1024),
                    ("ab", 16), ("r", 1024), ("rk", 1024), ("rv", 1024), ("lora", 256),
                    ("ma", 1024), ("mb", 1024), ("mc", 1024)):
        z[name] = w_in[:, :, at:at + n] if n == 16 else tiles(w_in[:, :, at:at + n])
        at += n
    o["x"] = x[0].T.reshape(KT, P, T).transpose(1, 0, 2)
    norms = [w for l in range(L) for w in (norm_mix_w[l], norm_ffn_w[l])] + [final_norm_w]
    o["norms"] = np.stack([w.reshape(KT, P).T for w in norms], 1)

    o["w_side"] = np.stack([z[n] for n in ("g", "u", "ma", "mb", "mc")], 2)
    o["lru_par"] = np.stack([chan(lru_conv_w[:, j]) for j in range(4)]
                            + [chan(v) for v in (lru_conv_b, lru_b_a, lru_b_x, lru_lambda)], 3)
    gates = np.zeros((L, P, KT, 2, P), np.float32)
    for j, w in enumerate((lru_w_a, lru_w_x)):
        w = w.reshape(L, KT, 2, 64, 64)
        for q in range(2):
            gates[:, 64 * q:64 * q + 64, :, j, 64 * q:64 * q + 64] = w[:, :, q].transpose(0, 2, 1, 3)
    o["lru_gates"] = gates

    o["w_rwkv"] = np.stack([z["r"], z["rk"], z["rv"]], 2)
    o["w_rwkv_lora"] = z["lora"]
    mu = chan(rwkv_mu)
    o["rwkv_par"] = np.stack([mu[:, :, 0:8], mu[:, :, 8:16], mu[:, :, 16:24]]
                             + [chan(v.reshape(L, -1)) for v in (rwkv_w0, rwkv_a0, rwkv_k_k, rwkv_k_a, rwkv_r_k,
                                                                 rwkv_lnx_w, rwkv_lnx_b)], 3)
    o["rwkv_lora_par"] = mu[:, :, 24:26]
    up = np.concatenate([rwkv_w_up, rwkv_a_up], 1).reshape(L, P, KT, P).transpose(0, 2, 1, 3)
    o["rwkv_up"] = np.concatenate([up, rwkv_g_up.reshape(L, P, KT, P).transpose(0, 2, 1, 3)], 3)

    o["w_gdn"] = np.stack([z[n].reshape(L, 4, 2, P, KT * P) for n in ("q", "k", "v", "zg")], 2).reshape(L, 4, 8, P, KT * P)
    conv = gdn_conv_w.reshape(L, 4, 3, 8, P).transpose(0, 4, 3, 2, 1)
    o["gdn_par"] = conv.reshape(L, P, 8, 12)
    o["gdn_norm"] = gdn_norm_w.reshape(L, P, 1)
    o["gdn_ab"] = z["ab"].reshape(L, KT, P, 16).transpose(0, 2, 1, 3)
    rows = np.stack([gdn_a_log, gdn_dt_bias], 1)
    o["gdn_rows"] = np.broadcast_to(rows[:, None, :, :, None], (L, P, 2, 8, 2))

    o["w_gdn_side"] = np.stack([tiles(w).reshape(L, 4, 2, P, KT * P) for w in (p_lru, p_rwkv)], 2).reshape(L, 4, 4, P, KT * P)
    o["p_gdn"] = tiles(p_gdn)
    o["merge_b"] = chan(merge_b).reshape(L, P, 3, KT)
    o["w_out"] = tiles(w_out)

    o["w_query"] = tiles(peer_wq).reshape(L, 4, 4, P, KT * P)
    o["keys"] = peer_keys.reshape(L, 16, NK, P).transpose(0, 3, 1, 2)
    o["u"] = peer_u.reshape(L, NK, NK, KT, P).transpose(0, 2, 4, 3, 1).reshape(L, NK, P, KT * P)
    o["v"] = peer_v.reshape(L, NK, NK, D).transpose(0, 2, 1, 3)
    return {k: np.ascontiguousarray(a) for k, a in o.items()}


def kernel(**inputs):
    import numpy as np
    import concourse.bacc as bacc
    from concourse.bass_utils import run_bass_kernel_spmd

    arrays = host_layout(**{k: np.asarray(a) for k, a in inputs.items()})
    book = {"first": True}
    for _ in range(2):
        nc = bacc.Bacc("TRN2", target_bir_lowering=False, num_devices=1)
        A = {k: nc.dram_tensor("in_" + k, a.shape, mybir.dt.from_np(a.dtype), kind="ExternalInput").ap()
             for k, a in arrays.items()}
        out = nc.dram_tensor("out_y", (P, KT, T), F32, kind="ExternalOutput").ap()
        build(nc, A, out, book)
        book.pop("first", None)
    r = run_bass_kernel_spmd(nc, [{"in_" + k: a for k, a in arrays.items()}], core_ids=[0])
    y = r.results[0]["out_y"]
    return np.ascontiguousarray(y.transpose(2, 1, 0).reshape(1, T, D))
```

```python
import math
from contextlib import ExitStack

import concourse.bass as bass
from concourse import mybir

F32 = mybir.dt.float32
U32 = mybir.dt.uint32
F32R = mybir.dt.float32r
ALU = mybir.AluOpType
ACT = mybir.ActivationFunctionType
AX = mybir.AxisListType

P = 128
T = 256
D = 1024
KT = D // P
NB = T // P
L = 2
EPS = 1e-6
GN_EPS = 64e-5
LRU_C = 8.0
HD = 64
CH = 64
GDN_SCALE = 128 ** -0.5
DECAY = math.exp(-0.5)
TOPK = 16
PH = 8
NK = 128

LRU_COLS = ["w0", "w1", "w2", "w3", "cb", "ba", "bx", "lam"]
RWKV_COLS = ["mu_r", "mu_k", "mu_v", "w0", "a0", "k_k", "k_a", "r_k", "ln_w", "ln_b"]
RWKV_MADE = ["om_r", "om_k", "om_v", "om_ka"]
GDN_COLS = [f"{x}{j}" for x in "qkv" for j in range(4)]
N_LEVELS = 7
CONST_COLS = [("ident", P), ("ones", P), ("blk64", P), ("upto", P), ("after", P), ("gmask", 2 * P), ("rmask", 2 * P),
              ("lmask", N_LEVELS * P), ("restart", T), ("half", 2), ("iota", P)]


class Steps:

    def __init__(self, sem, book, name, looped):
        self.sem, self.book, self.name, self.looped, self.n = sem, book, name, looped, 0

    def per(self):
        return self.book.get((self.name, "per"), 1)

    def prime(self, engine):
        engine.sem_inc(self.sem, self.per())

    def begin(self):
        self.n = 0

    def one(self, label=None):
        self.n += 1
        if label:
            self.book[self.name, label] = self.n
        return 1

    def end(self):
        self.book[self.name, "per"] = self.n

    def index(self, label):
        assert self.book.get("first") or (self.name, label) in self.book, (self.name, label)
        return self.book.get((self.name, label), 1)

    def at(self, label, i=0):
        return (i + 1) * self.per() + self.index(label) if self.looped else self.index(label)

    def before(self, label, i):
        return i * self.per() + self.index(label)

    def now(self, i=0):
        assert self.n > 0
        return (i + 1) * self.per() + self.n if self.looped else self.n


def build(nc, A, out, book):
    ctx = ExitStack()
    with ctx:
        _program(nc, ctx, A, out, book)


def _program(nc, ctx, A, out, book):
    def sb(name, shape, dt=F32):
        return ctx.enter_context(nc.sbuf_tensor(name, shape, dt))

    def sem(name):
        return ctx.enter_context(nc.semaphore(name))

    cleared = []

    def lsem(name):
        s = sem(name)
        cleared.append(s)
        return s

    def steps(name, looped=False):
        return Steps(lsem(name), book, name, looped)

    h = sb("h", [P, KT, T])
    made_of_shapes = sb("made_of_shapes", [P, sum(n for _, n in CONST_COLS)])

    def const(name, **kw):
        at = sum(n for other, n in CONST_COLS[:[x for x, _ in CONST_COLS].index(name)])
        v = made_of_shapes[:, at:at + dict(CONST_COLS)[name]]
        return v.rearrange("p (x c) -> p x c", c=P) if kw.get("rows") else v

    ident = const("ident")
    ones = const("ones")
    blk64 = const("blk64")
    upto = const("upto")
    after = const("after")
    gmask = const("gmask", rows=True)
    rmask = const("rmask", rows=True)
    lmask = const("lmask", rows=True)
    restart = const("restart")
    half = const("half")
    iota = const("iota")
    norm_w = sb("norm_w", [P, 2 * L + 1, KT])
    ARENA = 32768
    arena = sb("arena", [P, ARENA])
    banks = [ctx.enter_context(nc.psum_tensor(f"bank{i}", [P, 512], F32)) for i in range(8)]

    class Region:

        def __init__(self, at):
            self.at_ = at

        def __call__(self, *shape, dt=F32):
            n = math.prod(shape)
            assert self.at_ + n <= ARENA, (self.at_, n)
            v = arena[:, self.at_:self.at_ + n]
            self.at_ += n
            if dt is not F32:
                v = v.bitcast(dt)
            if len(shape) == 1:
                return v
            names = "abcd"[:len(shape)]
            return v.rearrange(f"p ({' '.join(names)}) -> p {' '.join(names)}", **{k: s for k, s in zip(names[1:], shape[1:])})

    base = Region(0)
    xn = base(KT, T)
    PEER = base.at_
    ya, yb, yc = base(KT, T), base(KT, T), base(KT, T)
    BRANCH = base.at_

    load_x = sem("load_x")

    with nc.Block() as block:
        @block.sync
        def _(sp):
            sp.dma_start(h[:], A["x"]).then_inc(load_x, 16)
            sp.dma_start(made_of_shapes[:], A["consts"]).then_inc(load_x, 16)
            sp.dma_start(norm_w[:], A["norms"]).then_inc(load_x, 16)
            sp.wait_ge(load_x, 48)

    def rmsnorm(tag, w, dst, ahead=None):
        V, E, S, G = steps(tag + "_vec"), steps(tag + "_pe"), steps(tag + "_act"), steps(tag + "_pool")
        r = Region(BRANCH)
        sq, hw, rs, root = r(KT, T), r(KT, T), r(T), r(1)
        ss = banks[0][:, 0:T]
        VEC = 5
        scaled = lambda engine, ks: engine.tensor_tensor(dst[:, ks], hw[:, ks], rs.unsqueeze(1).to_broadcast([P, ks.stop - ks.start, T]), ALU.mult)
        with nc.Block() as block:
            @block.sync
            def _(sp):
                if ahead:
                    ahead(sp)

            @block.vector
            def _(v):
                for k in range(0, KT // 2, 2):
                    v.tensor_tensor(sq[:, k:k + 2], h[:, k:k + 2], h[:, k:k + 2], ALU.mult).then_inc(V.sem, V.one(f"sq{k}"))
                v.wait_ge(E.sem, E.at("ss"))
                v.tensor_scalar(rs, ss, 1.0 / D, EPS, ALU.mult, ALU.add).then_inc(V.sem, V.one("ms"))
                v.wait_ge(S.sem, S.at("root"))
                v.reciprocal(rs, rs).then_inc(V.sem, V.one("rs"))
                v.wait_ge(V.sem, V.now())
                scaled(v, slice(0, VEC)).then_inc(V.sem, V.one())
                v.wait_ge(V.sem, V.now())

            @block.tensor
            def _(te):
                for n, k in enumerate((0, 2, 4, 6)):
                    te.wait_ge(*((V.sem, V.at(f"sq{k}")) if k < KT // 2 else (S.sem, S.at(f"sq{k}"))))
                    for j in range(2):
                        mm = te.matmul(ss, ones, sq[:, k + j, :], start=(n + j == 0), stop=(n + j == 4))
                mm.then_inc(E.sem, E.one("ss"))

            @block.scalar
            def _(a):
                for k in range(KT // 2, KT, 2):
                    a.activation(sq[:, k:k + 2], h[:, k:k + 2], ACT.Square).then_inc(S.sem, S.one(f"sq{k}"))
                for k in range(KT):
                    a.activation(hw[:, k], h[:, k], ACT.Copy, scale=w[:, k:k + 1]).then_inc(S.sem, S.one("hw"))
                a.activation(root, ones[:, 0:1], ACT.Sqrt).then_inc(S.sem, S.one())
                a.wait_ge(V.sem, V.at("ms"))
                a.activation(rs, rs, ACT.Sqrt).then_inc(S.sem, S.one("root"))

            @block.gpsimd
            def _(g):
                g.wait_ge(V.sem, V.at("rs"))
                scaled(g, slice(VEC, KT)).then_inc(G.sem, G.one())
                g.wait_ge(G.sem, G.now())

    def project(te, ps, slot, x=None, ks=range(KT)):
        x = xn if x is None else x
        for k in ks:
            mm = te.matmul(ps, ring[:, slot, k * P:(k + 1) * P], x[:, k, :], start=(k == 0), stop=(k == KT - 1))
        return mm

    def softplus_exp(a, S, x, e, tag):
        a.activation(e, x, ACT.Abs).then_inc(S.sem, S.one())
        a.wait_ge(S.sem, S.now())
        a.activation(e, e, ACT.Exp, scale=-1.0).then_inc(S.sem, S.one(tag + "_e"))

    def softplus_log(v, V, x, e, z, z2, p, m):
        v.tensor_scalar(z, e, 2.0, None, ALU.add).then_inc(V.sem, V.one())
        v.wait_ge(V.sem, V.now())
        v.reciprocal(z, z).then_inc(V.sem, V.one())
        v.wait_ge(V.sem, V.now())
        v.tensor_tensor(z, z, e, ALU.mult).then_inc(V.sem, V.one())
        v.wait_ge(V.sem, V.now())
        v.tensor_tensor(z2, z, z, ALU.mult).then_inc(V.sem, V.one())
        v.wait_ge(V.sem, V.now())
        v.tensor_scalar(p, z2, 1.0 / 17, None, ALU.mult).then_inc(V.sem, V.one())
        for k in range(7, 0, -1):
            v.wait_ge(V.sem, V.now())
            v.scalar_tensor_tensor(p, p, 1.0 / (2 * k + 1), z2, ALU.add, ALU.mult).then_inc(V.sem, V.one())
        v.wait_ge(V.sem, V.now())
        v.scalar_tensor_tensor(p, p, 1.0, z, ALU.add, ALU.mult).then_inc(V.sem, V.one())
        v.tensor_scalar(m, x, 0.0, None, ALU.max).then_inc(V.sem, V.one())
        v.wait_ge(V.sem, V.now())
        v.scalar_tensor_tensor(p, p, 2.0, m, ALU.mult, ALU.add).then_inc(V.sem, V.one())

    class Lru:

        def __init__(self, at):
            self.V, self.S, self.E = steps("lru_vec"), steps("lru_act"), steps("lru_pe")
            self.pload = lsem("lru_params")
            r = Region(at)
            self.par = r(KT, len(LRU_COLS))
            self.wax = r(KT, 2, P)
            self.rr, self.ii, self.aa, self.bb = (r(KT, T) for _ in range(4))
            self.small = [r(KT) for _ in range(6)]
            self.c = {n: k for k, n in enumerate(LRU_COLS)}

        def loads(self, sp, l):
            sp.dma_start(self.par, A["lru_par"][l]).then_inc(self.pload, 16)
            sp.dma_start(self.wax, A["lru_gates"][l]).then_inc(self.pload, 16)

        def tensor(self, te):
            S, E = self.S, self.E
            te.wait_ge(self.pload, 32)
            for k in range(KT):
                if k >= 2:
                    te.wait_ge(S.sem, S.at(f"i{k - 2}"))
                te.matmul(banks[4 + k % 2][:, 0:T], self.wax[:, k, 0, :], yb[:, k, :], start=True, stop=True)\
                    .then_inc(E.sem, E.one(f"r{k}"))
                te.matmul(banks[6 + k % 2][:, 0:T], self.wax[:, k, 1, :], yb[:, k, :], start=True, stop=True)\
                    .then_inc(E.sem, E.one(f"i{k}"))

        def scalar(self, a, tile):
            V, S, E, par, c, rr, aa, bb = self.V, self.S, self.E, self.par, self.c, self.rr, self.aa, self.bb
            lam_n, e = self.small[:2]
            a.wait_ge(self.pload, 32)
            a.wait_ge(V.sem, V.at("neg"))
            softplus_exp(a, S, lam_n, e, "sp")
            for k in range(KT):
                a.wait_ge(E.sem, E.at(f"r{k}"))
                a.activation(rr[:, k, :], banks[4 + k % 2][:, 0:T], ACT.Sigmoid, bias=par[:, k, c["ba"]:c["ba"] + 1])\
                    .then_inc(S.sem, S.one())
                a.wait_ge(E.sem, E.at(f"i{k}"))
                a.activation(self.ii[:, k, :], banks[6 + k % 2][:, 0:T], ACT.Sigmoid, bias=par[:, k, c["bx"]:c["bx"] + 1])\
                    .then_inc(S.sem, S.one(f"i{k}"))
            tile(0)
            a.wait_ge(V.sem, V.at("nla"))
            a.activation(aa, rr, ACT.Exp, scale=-1.0).then_inc(S.sem, S.one("a"))
            a.activation(bb, rr, ACT.Tanh).then_inc(S.sem, S.one("tanh"))
            tile(1)
            tile(2)
            a.wait_ge(V.sem, V.at("b2"))
            a.activation(bb, bb, ACT.Sqrt).then_inc(S.sem, S.one("b"))
            tile(3)
            tile(4)
            a.activation(ya, ya, ACT.Gelu_apprx_tanh).then_inc(S.sem, S.one("gelu"))
            tile(5)
            tile(6)
            a.activation(zg[:], zg[:], ACT.Sigmoid).then_inc(S.sem, S.one("zg"))
            tile(7)

        def vector_first(self, v):
            V, S, lam_n = self.V, self.S, self.small[0]
            v.wait_ge(self.pload, 32)
            v.tensor_scalar(lam_n, self.par[:, :, self.c["lam"]], -1.0, None, ALU.mult).then_inc(V.sem, V.one("neg"))
            v.wait_ge(S.sem, S.at("sp_e"))
            v.wait_ge(V.sem, V.now())
            softplus_log(v, V, *self.small)
            v.wait_ge(V.sem, V.now())

        def vector(self, v, tile):
            V, S, rr, ii, aa, bb = self.V, self.S, self.rr, self.ii, self.aa, self.bb
            spl = self.small[4]
            v.wait_ge(S.sem, S.at(f"i{KT - 1}"))
            for k in range(KT):
                v.tensor_scalar(rr[:, k, :], rr[:, k, :], spl[:, k:k + 1], LRU_C, ALU.mult, ALU.mult)\
                    .then_inc(V.sem, V.one("nla"))
            v.tensor_tensor(ii, ii, yb, ALU.mult).then_inc(V.sem, V.one("ix"))
            tile(0)
            v.wait_ge(S.sem, S.at("tanh"))
            v.tensor_tensor(rr, aa, aa, ALU.mult).then_inc(V.sem, V.one("a2"))
            v.wait_ge(V.sem, V.now())
            v.scalar_tensor_tensor(bb, rr, 1.0, bb, ALU.add, ALU.mult).then_inc(V.sem, V.one("b2"))
            tile(1)
            tile(2)
            v.wait_ge(S.sem, S.at("b"))
            v.tensor_tensor(bb, bb, ii, ALU.mult).then_inc(V.sem, V.one("bx"))
            for k in range(KT):
                if k in (0, 4):
                    tile(3 + k // 4)
                v.wait_ge(V.sem, V.now())
                v.tensor_tensor_scan(rr[:, k, :], aa[:, k, :], bb[:, k, :], 0.0, ALU.mult, ALU.add)\
                    .then_inc(V.sem, V.one("scan"))
            v.wait_ge(V.sem, V.now())
            v.wait_ge(S.sem, S.at("gelu"))
            tile(5)
            v.tensor_tensor(ya, ya, rr, ALU.mult).then_inc(V.sem, V.one("ya"))
            v.wait_ge(V.sem, V.now())

    def invert_levels(te, a, v, g, name, E, S, V, G, i, NLM, T_, TT, X, bX, bY, bYT, levels, fill=None):
        m4 = range(4)
        view = lambda b: b[:, :].rearrange("p (m c) -> p m c", m=4)
        for lev in range(1, levels):
            last = lev == levels - 1
            t = f"{name}{lev}"
            if te is not None:
                te.wait_ge(G.sem, G.at(f"{t}mask", i))
                if lev == 1:
                    te.wait_ge(S.sem, S.at(f"{name}T", i))
                else:
                    te.wait_ge(V.sem, V.at(f"{name}{lev - 1}TT", i))
                for m in m4:
                    mm = te.matmul(view(bX)[:, m], NLM[:, lev - 1, m], T_[:, m], start=True, stop=True)
                mm.then_inc(E.sem, E.one(f"{t}X"))
                if fill:
                    fill(lev, 0)
                te.wait_ge(S.sem, S.at(f"{t}X", i))
                if not last:
                    for m in m4:
                        mm = te.matmul(view(bY)[:, m], TT[:, m], X[:, m], start=True, stop=True)
                    mm.then_inc(E.sem, E.one(f"{t}Y"))
                for m in m4:
                    mm = te.matmul(view(bYT)[:, m], X[:, m], TT[:, m], start=True, stop=True)
                mm.then_inc(E.sem, E.one(f"{t}YT"))
                if fill:
                    fill(lev, 1)
            if a is not None:
                a.wait_ge(E.sem, E.at(f"{t}X", i))
                a.activation(X, view(bX), ACT.Copy).then_inc(S.sem, S.one(f"{t}X"))
                if fill:
                    fill(lev)
            if v is not None:
                if not last:
                    v.wait_ge(E.sem, E.at(f"{t}Y", i))
                    v.tensor_tensor(T_, T_, view(bY), ALU.add).then_inc(V.sem, V.one())
                v.wait_ge(E.sem, E.at(f"{t}YT", i))
                v.tensor_tensor(TT, TT, view(bYT), ALU.add).then_inc(V.sem, V.one(f"{t}TT"))
                if fill:
                    fill(lev)

    gdn_loaded = [lsem(f"gd_tile{s}") for s in range(4)]
    gdn_loaded_g = [lsem(f"gdG_tile{s}") for s in range(4)]
    merge_loaded = [lsem(f"mg_tile{s}") for s in range(4)]
    merge_loaded_out = [lsem(f"wo_tile{s}") for s in range(4)]

    def gdn_tile_a(sp, l, i, s):
        sp.dma_start(ring[:, s % 4, :], A["w_gdn"][l, i, s]).then_inc(gdn_loaded[s % 4], 16)

    def gdn_tile_g(sp, l, i, n):
        sp.dma_start(ring[:, 4 + n, :], A["w_gdn_side"][l, i, n]).then_inc(gdn_loaded_g[n], 16)

    def merge_tile(sp, l, k):
        sp.dma_start(ring[:, k % 4, :], A["p_gdn"][l, k]).then_inc(merge_loaded[k % 4], 16)

    def merge_tile_out(sp, l, k):
        sp.dma_start(ring[:, 4 + k % 4, :], A["w_out"][l, k]).then_inc(merge_loaded_out[k % 4], 16)

    rwkv_loaded = [lsem(f"rw_tile{s}") for s in range(4)]
    rwkv_loaded_f = [lsem(f"rwF_tile{s}") for s in range(5)]
    rwkv_loaded_lora = lsem("rw_lora_tiles")
    F_SLOT = 3

    def rwkv_tile(sp, l, i, s):
        sp.dma_start(ring[:, s, :], A["w_rwkv"][l, i, s]).then_inc(rwkv_loaded[s], 16)

    def rwkv_side_tile(sp, l, i, n):
        sp.dma_start(ring[:, F_SLOT + n, :], A["w_side"][l, i, n]).then_inc(rwkv_loaded_f[n], 16)

    def rwkv_first_tiles(sp, l):
        for s in range(2):
            sp.dma_start(ring[:, 6 + s, :], A["w_rwkv_lora"][l, s]).then_inc(rwkv_loaded_lora, 16)
        for s in range(3):
            rwkv_tile(sp, l, 0, s)
        for n in range(3):
            rwkv_side_tile(sp, l, 0, n)

    def rwkv_phase(l):
        NI = KT
        VA, SA, EA = steps("rwA_vec", True), steps("rwA_act", True), steps("rwA_pe", True)
        V, S, E, G = steps("rwB_vec", True), steps("rwB_act", True), steps("rwB_pe", True), steps("rwB_pool", True)
        VF, SF, EF = steps("rwF_vec", True), steps("rwF_act", True), steps("rwF_pe", True)
        V0, S0, E0 = steps("rw0_vec"), steps("rw0_act"), steps("rw0_pe")
        loaded, loaded_f, wload = rwkv_loaded, rwkv_loaded_f, rwkv_loaded_lora
        pload = lsem("rw_params")
        r_ = Region(BRANCH)
        NC_, NM = len(RWKV_COLS), len(RWKV_MADE)
        par = r_(KT, NC_)
        made = r_(KT, NM)
        lru_par = r_(KT, len(LRU_COLS))
        merge_b = r_(3, KT)
        small = r_(2 * P)
        lmu, lom = r_(2), r_(2)
        Z = r_(3, T)
        WA, SG = r_(T), r_(T)
        (kkr, sq, sg, cs, cm, Pm, Pp, Pi, rs, aa, kk, kf, kp, rk, nb, NBt, KH, bv, gt, y) = (r_(T) for _ in range(20))
        KR = r_(NB, 2, P)
        BK = r_(4, P)
        Vt, Vh = r_(NB, P), r_(2, NB, P)
        G1, G2 = r_(4, 2, P), r_(4, 2, P)
        NLM = r_(5, 4, P)
        T_, TT, X = r_(4, P), r_(4, P), r_(4, P)
        AVO = r_(4, P)
        Rs, Um, St, SP, t1 = r_(P), r_(P), r_(P), r_(P), r_(P)
        sqo = r_(4, HD)
        mu4, va4 = r_(4), r_(4)
        c = {n: k for k, n in enumerate(RWKV_COLS)}
        lc = {n: k for k, n in enumerate(LRU_COLS)}
        cmade = {n: k for k, n in enumerate(RWKV_MADE)}
        b2, b3, b4, b5, b6, b7 = banks[2:8]
        ps_in = [banks[s % 2][:, 0:T] for s in range(3)]
        f_bank = [banks[n][:, 0:T] for n in (0, 1, 1, 0, 1)]
        O = AVO[:, 2:4]
        O4 = O.rearrange("p b (h c) -> p (b h) c", h=2)

        def col(i, name):
            return par[:, i, c[name]:c[name] + 1] if name in c else made[:, i, cmade[name]:cmade[name] + 1]

        with nc.Block() as block:
            @block.sync
            def _(sp):
                sp.dma_start(par, A["rwkv_par"][l]).then_inc(pload, 16)
                sp.dma_start(lmu, A["rwkv_lora_par"][l]).then_inc(pload, 16)
                sp.dma_start(small, A["rwkv_up"][l, 0]).then_inc(loaded[3], 16)
                sp.dma_start(lru_par, A["lru_par"][l]).then_inc(pload, 16)
                sp.dma_start(merge_b, A["merge_b"][l]).then_inc(pload, 16)
                sp.wait_ge(E0.sem, E0.at("lora1"))
                for n in range(3, 5):
                    rwkv_side_tile(sp, l, 0, n)
                with sp.Fori(1, NI) as i:
                    for s, what in enumerate("rkv"):
                        sp.wait_ge(EA.sem, EA.before(what, i))
                        rwkv_tile(sp, l, i, s)
                    sp.wait_ge(E.sem, E.before("gate", i))
                    sp.dma_start(small, A["rwkv_up"][l, i]).then_inc(loaded[3], 16)
                    for n in range(5):
                        sp.wait_ge(EF.sem, EF.before(f"f{n}", i))
                        rwkv_side_tile(sp, l, i, n)
                for s, what in enumerate("rkv"):
                    sp.wait_ge(EA.sem, EA.at(what, NI - 1))
                    gdn_tile_a(sp, l, 0, s)
                sp.wait_ge(EF.sem, EF.at("f0", NI - 1))
                gdn_tile_a(sp, l, 0, 3)
                for n in range(4):
                    sp.wait_ge(EF.sem, EF.at(f"f{n + 1}", NI - 1))
                    gdn_tile_g(sp, l, 0, n)

            def pe_piece(te, i, j, first=False):
                s, part = divmod(j, 4)
                if part == 0:
                    te.wait_ge(loaded[s], 16 * i + 16)
                    if s == 2:
                        te.wait_ge(VA.sem, VA.at("shift0", i))
                    elif not first:
                        te.wait_ge(*((SF.sem, SF.at("f0", i - 1)) if s == 0 else (VF.sem, VF.at("tap3", i - 1))))
                mm = project(te, ps_in[s], s, ks=range(2 * part, 2 * part + 2))
                if part == 3:
                    mm.then_inc(EA.sem, EA.one("rkv"[s]))

            def pe_side(te, i, js, more):
                for j in js:
                    n, part = divmod(j, 4)
                    if part == 0:
                        te.wait_ge(loaded_f[n], 16 * i + 16)
                        if n < 2:
                            te.wait_ge(SF.sem, SF.before(f"f{n + 3}", i))
                        elif n == 4:
                            te.wait_ge(SF.sem, SF.at("f2", i))
                        elif more:
                            te.wait_ge(VA.sem, VA.at(f"shift{n - 1}", i + 1))
                        else:
                            te.wait_ge(*((VF.sem, VF.at("tap3", i)) if n == 2 else (SF.sem, SF.at("f0", i))))
                    mm = project(te, f_bank[n], F_SLOT + n, ks=range(2 * part, 2 * part + 2))
                    if part == 3:
                        mm.then_inc(EF.sem, EF.one(f"f{n}"))

            def act_side(a, i, n):
                a.wait_ge(EF.sem, EF.at(f"f{n}", i))
                if n == 0:
                    a.activation(ya[:, i], f_bank[n], ACT.Copy).then_inc(SF.sem, SF.one("f0"))
                elif n == 1:
                    a.activation(yb[:, i], f_bank[n], ACT.Identity, bias=lru_par[:, i, lc["cb"]:lc["cb"] + 1],
                                 scale=lru_par[:, i, lc["w3"]:lc["w3"] + 1]).then_inc(SF.sem, SF.one("f1"))
                else:
                    a.activation(zg[:, n - 2, i], f_bank[n], ACT.Identity, bias=merge_b[:, n - 2, bass.ds(i, 1)])\
                        .then_inc(SF.sem, SF.one(f"f{n}"))

            def vec_taps(v, i):
                v.wait_ge(SF.sem, SF.at("f1", i))
                for sh in (1, 2, 3):
                    if sh > 1:
                        v.wait_ge(VF.sem, VF.now(i))
                    v.scalar_tensor_tensor(yb[:, i, sh:T], f_bank[1][:, 0:T - sh], lru_par[:, i, 3 - sh:4 - sh],
                                           yb[:, i, sh:T], ALU.mult, ALU.add).then_inc(VF.sem, VF.one(f"tap{sh}"))

            def act_piece(a, i, s):
                if s == 0:
                    a.wait_ge(V.sem, V.before("bv", i))
                    a.wait_ge(E.sem, E.before("vT", i))
                a.wait_ge(EA.sem, EA.at("rkv"[s], i))
                a.activation(Z[:, s, :], ps_in[s], ACT.Copy, scale=col(i, "om_" + "rkv"[s])).then_inc(SA.sem, SA.one(f"z{s}"))

            def vec_piece(v, i, s):
                v.wait_ge(SA.sem, SA.at(f"z{s}", i))
                v.scalar_tensor_tensor(Z[:, s, 1:T], ps_in[s][:, 0:T - 1], col(i, "mu_" + "rkv"[s]), Z[:, s, 1:T],
                                       ALU.mult, ALU.add).then_inc(VA.sem, VA.one(f"shift{s}"))

            def pe_body(te, i, more):
                def fill(lev, y):
                    if more:
                        pe_piece(te, i + 1, 2 * lev + y)

                def side(*js):
                    pe_side(te, i, js, more)

                if more:
                    EA.begin()
                EF.begin()
                E.begin()
                rows = lambda q: slice(64 * q, 64 * q + 64)
                te.wait_ge(loaded[3], 16 * i + 16)
                te.wait_ge(V.sem, V.before("y0", i))
                te.matmul(b2[:, 0:T], small[rows(0), 0:P], WA[rows(0), :], start=True, stop=True).then_inc(E.sem, E.one("w"))
                te.matmul(b3[:, 0:T], small[rows(1), 0:P], WA[rows(1), :], start=True, stop=True).then_inc(E.sem, E.one("a"))
                te.matmul(b4[:, 0:T], small[:, P:2 * P], SG, start=True, stop=True).then_inc(E.sem, E.one("gate"))
                te.wait_ge(V.sem, V.at("sq", i))
                te.matmul(b5[:, 0:T], blk64, sq, start=True, stop=True).then_inc(E.sem, E.one("ss"))
                for b in range(NB):
                    mm = te.transpose(b6[:, b * P:(b + 1) * P], Z[:, 2, b * P:(b + 1) * P], ident)
                mm.then_inc(E.sem, E.one("vT"))
                side(0, 1, 2)
                te.wait_ge(V.sem, V.at("rk", i))
                te.matmul(b7[:, 0:T], blk64, rk, start=True, stop=True).then_inc(E.sem, E.one("bonus"))
                side(3, 4, 5, 6, 7)
                te.wait_ge(V.sem, V.at("KH", i))
                for x, src in enumerate((NBt, KH)):
                    for b in range(NB):
                        mm = te.transpose(b5[:, (2 * x + b) * P:(2 * x + b + 1) * P], src[:, b * P:(b + 1) * P], ident)
                mm.then_inc(E.sem, E.one("bkT"))
                te.wait_ge(S.sem, S.at("gate", i))
                te.wait_ge(S.sem, S.at("a", i))
                te.wait_ge(V.sem, V.at("bv", i))
                for x, (src, bk) in enumerate(((NBt, (b2, b4)), (KH, (b3, b7)))):
                    for hh in range(2):
                        for b in range(NB):
                            mm = te.matmul(bk[hh][:, b * T:(b + 1) * T], src[rows(hh), b * P:(b + 1) * P],
                                           KR[rows(hh), b], start=True, stop=True)
                        mm.then_inc(E.sem, E.one(f"g{x}{hh}"))
                fill(0, 0)
                fill(0, 1)
                te.wait_ge(S.sem, S.at("BK", i))
                te.wait_ge(V.sem, V.at("TT0", i))
                for m in range(4):
                    mm = te.transpose(b5[:, m * P:(m + 1) * P], TT[:, m], ident)
                mm.then_inc(E.sem, E.one("T0"))
                te.wait_ge(S.sem, S.at("Vt", i))
                te.wait_ge(V.sem, V.at("m11", i))
                for x in range(2):
                    for b in range(NB):
                        for hh in range(2):
                            mm = te.matmul(b6[:, x * T + b * P + hh * HD:x * T + b * P + hh * HD + HD], G2[:, 2 * hh + b, x],
                                           Vt[:, b, hh * HD:(hh + 1) * HD], start=True, stop=True)
                mm.then_inc(E.sem, E.one("AV"))
                invert_levels(te, None, None, None, "inv", E, S, V, G, i, NLM, T_, TT, X, b2, b3, b4, 6, fill)
                te.wait_ge(V.sem, V.at("inv5TT", i))
                te.wait_ge(S.sem, S.at("AVO", i))
                for q in range(T // CH):
                    b, hf = divmod(q, 2)
                    if q:
                        te.wait_ge(V.sem, V.at(f"S{q - 1}", i))
                        te.matmul(b5[:, 0:P], KR[:, b, 0], St, start=True, stop=True).then_inc(E.sem, E.one(f"R{q}"))
                        side(2 * q + 7)
                        te.wait_ge(V.sem, V.at(f"R{q}", i))
                    rhs = Rs if q else AVO[:, 0]
                    for hh in range(2):
                        mm = te.matmul(b7[:, hh * HD:(hh + 1) * HD], TT[:, 2 * hh + b], rhs[:, hh * HD:(hh + 1) * HD],
                                       start=True, stop=True)
                    mm.then_inc(E.sem, E.one(f"U{q}"))
                    if q:
                        te.wait_ge(V.sem, V.at(f"o{q - 1}", i))
                        te.matmul(b3[:, 0:P], KR[:, b, 1], St, start=True, stop=False)
                    side(2 * q + 8)
                    te.wait_ge(S.sem, S.at(f"U{q}", i))
                    if q < 3:
                        te.matmul(b2[:, 0:P], BK[:, 2 + b], Vh[:, hf, b], start=True, stop=False)
                        te.matmul(b2[:, 0:P], BK[:, b], Um, start=False, stop=True).then_inc(E.sem, E.one(f"S{q}"))
                    for hh in range(2):
                        mm = te.matmul(b3[:, hh * HD:(hh + 1) * HD], G1[:, 2 * hh + b, 1], Um[:, hh * HD:(hh + 1) * HD],
                                       start=(q == 0), stop=(hh == 1) or q == 0)
                    mm.then_inc(E.sem, E.one(f"O{q}"))
                side(15, 16, 17, 18)
                te.wait_ge(V.sem, V.at("on", i))
                for b in range(NB):
                    mm = te.transpose(b4[:, b * P:(b + 1) * P], O[:, b], ident)
                mm.then_inc(E.sem, E.one("yT"))
                side(19)
                E.end()
                EF.end()
                if more:
                    EA.end()

            @block.tensor
            def _(te):
                te.wait_ge(wload, 32)
                for s in range(2):
                    project(te, banks[2 + s][:, 0:T], 6 + s).then_inc(E0.sem, E0.one(f"lora{s}"))
                EA.prime(te)
                E.prime(te)
                EF.prime(te)
                EA.begin()
                for j in range(12):
                    pe_piece(te, 0, j, first=True)
                EA.end()
                te.wait_ge(S0.sem, S0.at("SG"))
                with te.Fori(0, NI - 1) as i:
                    pe_body(te, i, True)
                pe_body(te, NI - 1, False)

            def act_body(a, i, more):
                def fill(n):
                    if more and n in (2, 4):
                        act_piece(a, i + 1, n // 2 - 1)

                if more:
                    SA.begin()
                SF.begin()
                S.begin()
                a.wait_ge(E.sem, E.at("w", i))
                a.activation(sg, b2[:, 0:T], ACT.Sigmoid, bias=col(i, "w0")).then_inc(S.sem, S.one("sg"))
                a.wait_ge(E.sem, E.at("a", i))
                a.activation(aa, b3[:, 0:T], ACT.Sigmoid, bias=col(i, "a0")).then_inc(S.sem, S.one("a"))
                a.wait_ge(E.sem, E.at("gate", i))
                a.wait_ge(V.sem, V.before("y2", i))
                a.activation(gt, b4[:, 0:T], ACT.Copy).then_inc(S.sem, S.one("gate"))
                a.wait_ge(V.sem, V.at("cm", i))
                a.activation(Pp, cs, ACT.Exp, scale=-DECAY).then_inc(S.sem, S.one("Pp"))
                a.activation(Pm, cm, ACT.Exp, scale=-DECAY).then_inc(S.sem, S.one("Pm"))
                a.activation(Pi, cs, ACT.Exp, scale=DECAY).then_inc(S.sem, S.one("Pi"))
                a.wait_ge(V.sem, V.at("rs0", i))
                a.activation(rs, rs, ACT.Sqrt).then_inc(S.sem, S.one("rs"))
                a.wait_ge(E.sem, E.at("vT", i))
                vps = b6[:, 0:2 * P].rearrange("p (b c) -> p b c", b=NB)
                a.activation(Vt, vps, ACT.Copy).then_inc(S.sem, S.one())
                for q in range(2):
                    a.activation(Vh[:, q], vps, ACT.Copy, scale=half[:, q:q + 1]).then_inc(S.sem, S.one("Vt"))
                act_side(a, i, 0)
                act_side(a, i, 1)
                a.wait_ge(E.sem, E.at("bkT", i))
                a.activation(BK, b5[:, :].rearrange("p (m c) -> p m c", m=4), ACT.Copy).then_inc(S.sem, S.one("BK"))
                a.wait_ge(E.sem, E.at("T0", i))
                a.activation(T_, b5[:, :].rearrange("p (m c) -> p m c", m=4), ACT.Copy).then_inc(S.sem, S.one("invT"))
                a.wait_ge(E.sem, E.at("AV", i))
                a.activation(AVO, b6[:, :].rearrange("p (m c) -> p m c", m=4), ACT.Copy).then_inc(S.sem, S.one("AVO"))
                invert_levels(None, a, None, None, "inv", E, S, V, G, i, NLM, T_, TT, X, b2, b3, b4, 6, fill)
                for q in range(T // CH):
                    a.wait_ge(E.sem, E.at(f"U{q}", i))
                    if q:
                        a.wait_ge(E.sem, E.at(f"O{q - 1}", i))
                    a.activation(Um, b7[:, 0:P], ACT.Copy, scale=half[:, q % 2:q % 2 + 1]).then_inc(S.sem, S.one(f"U{q}"))
                    if q == 0 and more:
                        act_piece(a, i + 1, 2)
                    if q == 2:
                        act_side(a, i, 2)
                act_side(a, i, 3)
                a.wait_ge(V.sem, V.at("var", i))
                a.activation(va4, va4, ACT.Sqrt).then_inc(S.sem, S.one("sd"))
                act_side(a, i, 4)
                S.end()
                SF.end()
                if more:
                    SA.end()

            @block.scalar
            def _(a):
                a.wait_ge(V0.sem, V0.at("made"))
                for s in range(2):
                    a.wait_ge(E0.sem, E0.at(f"lora{s}"))
                    dst = (WA, SG)[s]
                    a.activation(dst, banks[2 + s][:, 0:T], ACT.Copy, scale=lom[:, s:s + 1]).then_inc(S0.sem, S0.one(f"l{s}"))
                a.wait_ge(V0.sem, V0.at("shift1"))
                a.activation(WA[0:64, :], WA[0:64, :], ACT.Tanh).then_inc(S0.sem, S0.one())
                a.activation(SG, SG, ACT.Sigmoid).then_inc(S0.sem, S0.one("SG"))
                SA.prime(a)
                S.prime(a)
                SF.prime(a)
                a.wait_ge(pload, 64)
                SA.begin()
                for s in range(3):
                    act_piece(a, 0, s)
                SA.end()
                with a.Fori(0, NI - 1) as i:
                    act_body(a, i, True)
                act_body(a, NI - 1, False)

            def vec_body(v, i, more):
                def fill(n):
                    if more and n in (2, 4):
                        vec_piece(v, i + 1, n // 2 - 1)

                tt = lambda o, a0, a1, op, label=None: v.tensor_tensor(o, a0, a1, op).then_inc(V.sem, V.one(label))
                if more:
                    VA.begin()
                VF.begin()
                V.begin()
                v.wait_ge(VA.sem, VA.at("shift2", i))
                v.tensor_scalar(kkr, Z[:, 1], col(i, "k_k"), None, ALU.mult).then_inc(V.sem, V.one())
                v.wait_ge(V.sem, V.now(i))
                v.tensor_tensor(sq, kkr, kkr, ALU.mult).then_inc(V.sem, V.one("sq"))
                v.wait_ge(S.sem, S.at("sg", i))
                v.tensor_tensor_scan(cs, restart, sg, 0.0, ALU.mult, ALU.add).then_inc(V.sem, V.one())
                v.wait_ge(V.sem, V.now(i))
                v.tensor_tensor(cm, cs, sg, ALU.subtract).then_inc(V.sem, V.one("cm"))
                v.wait_ge(E.sem, E.at("ss", i))
                v.tensor_scalar(rs, b5[:, 0:T], EPS, None, ALU.add).then_inc(V.sem, V.one("rs0"))
                v.wait_ge(S.sem, S.at("a", i))
                v.tensor_scalar(kf, aa, col(i, "k_a"), col(i, "om_ka"), ALU.mult, ALU.add).then_inc(V.sem, V.one())
                v.wait_ge(V.sem, V.now(i))
                v.tensor_tensor(kp, Z[:, 1], kf, ALU.mult).then_inc(V.sem, V.one())
                v.wait_ge(V.sem, V.now(i))
                v.scalar_tensor_tensor(rk, Z[:, 0], col(i, "r_k"), kp, ALU.mult, ALU.mult).then_inc(V.sem, V.one("rk"))
                two = lambda x: x.rearrange("p (b c) -> p b c", b=NB)
                v.wait_ge(S.sem, S.at("Pi", i))
                v.tensor_tensor(KR[:, :, 1], two(Z[:, 0]), two(Pp), ALU.mult).then_inc(V.sem, V.one())
                v.wait_ge(S.sem, S.at("rs", i))
                v.reciprocal(rs, rs).then_inc(V.sem, V.one())
                v.wait_ge(V.sem, V.now(i))
                v.tensor_tensor(kk, kkr, rs, ALU.mult).then_inc(V.sem, V.one())
                v.wait_ge(V.sem, V.now(i))
                v.tensor_tensor(KR[:, :, 0], two(kk), two(Pm), ALU.mult).then_inc(V.sem, V.one())
                v.scalar_tensor_tensor(nb, kk, -1.0, aa, ALU.mult, ALU.mult).then_inc(V.sem, V.one())
                v.wait_ge(V.sem, V.now(i))
                v.tensor_tensor(NBt, nb, Pi, ALU.mult).then_inc(V.sem, V.one())
                v.tensor_tensor(KH, kp, Pi, ALU.mult).then_inc(V.sem, V.one("KH"))
                v.wait_ge(E.sem, E.at("bonus", i))
                v.tensor_tensor(bv, b7[:, 0:T], Z[:, 2], ALU.mult).then_inc(V.sem, V.one("bv"))
                for x, (dst, bk) in enumerate(((G1, (b2, b4)), (G2, (b3, b7)))):
                    for hh in range(2):
                        v.wait_ge(E.sem, E.at(f"g{x}{hh}", i))
                        v.tensor_tensor(dst[:, 2 * hh:2 * hh + 2].rearrange("p b x c -> p b (x c)"),
                                        bk[hh][:, :].rearrange("p (b c) -> p b c", b=NB),
                                        rmask.rearrange("p x c -> p (x c)").unsqueeze(1).to_broadcast([P, NB, 2 * P]),
                                        ALU.mult).then_inc(V.sem, V.one(f"m{x}{hh}"))
                    if x == 0:
                        v.wait_ge(V.sem, V.now(i))
                        v.tensor_tensor(TT, G1[:, :, 0], lmask[:, 0].unsqueeze(1).to_broadcast([P, 4, P]), ALU.mult)\
                            .then_inc(V.sem, V.one())
                        v.wait_ge(V.sem, V.now(i))
                        v.tensor_tensor(TT, TT, ident.unsqueeze(1).to_broadcast([P, 4, P]), ALU.add)\
                            .then_inc(V.sem, V.one("TT0"))
                vec_taps(v, i)
                v.wait_ge(S.sem, S.at("invT", i))
                invert_levels(None, None, v, None, "inv", E, S, V, G, i, NLM, T_, TT, X, b2, b3, b4, 6, fill)
                for q in range(T // CH):
                    b, hf = divmod(q, 2)
                    end = Pp[:, q * CH + CH - 1:q * CH + CH]
                    if q:
                        v.wait_ge(E.sem, E.at(f"R{q}", i))
                        v.tensor_tensor(Rs, b5[:, 0:P], AVO[:, b], ALU.add).then_inc(V.sem, V.one(f"R{q}"))
                        if q < 3:
                            v.tensor_scalar(SP, St, end, None, ALU.mult).then_inc(V.sem, V.one())
                    if q < 3:
                        v.wait_ge(E.sem, E.at(f"S{q}", i))
                        v.tensor_tensor(t1, b2[:, 0:P], blk64, ALU.mult).then_inc(V.sem, V.one("t1"))
                        v.wait_ge(V.sem, V.now(i))
                        if q:
                            v.scalar_tensor_tensor(St, t1, end, SP, ALU.mult, ALU.add).then_inc(V.sem, V.one(f"S{q}"))
                        else:
                            v.tensor_scalar(St, t1, end, None, ALU.mult).then_inc(V.sem, V.one(f"S{q}"))
                    v.wait_ge(E.sem, E.at(f"O{q}", i))
                    v.wait_ge(S.sem, S.at("AVO", i))
                    v.scalar_tensor_tensor(O[:, b], b3[:, 0:P], half[:, hf:hf + 1], O[:, b], ALU.mult, ALU.add)\
                        .then_inc(V.sem, V.one(f"o{q}"))
                    if q == 0 and more:
                        vec_piece(v, i + 1, 2)
                bc = lambda x: x.unsqueeze(2).to_broadcast([P, 4, HD])
                v.wait_ge(V.sem, V.now(i))
                v.tensor_reduce(mu4, O4, AX.X, ALU.add).then_inc(V.sem, V.one())
                v.wait_ge(V.sem, V.now(i))
                v.tensor_scalar(mu4, mu4, -1.0 / HD, None, ALU.mult).then_inc(V.sem, V.one())
                v.wait_ge(V.sem, V.now(i))
                v.tensor_tensor(O4, O4, bc(mu4), ALU.add).then_inc(V.sem, V.one())
                v.wait_ge(V.sem, V.now(i))
                v.tensor_tensor(sqo, O4, O4, ALU.mult).then_inc(V.sem, V.one())
                v.wait_ge(V.sem, V.now(i))
                v.tensor_reduce(va4, sqo, AX.X, ALU.add).then_inc(V.sem, V.one())
                v.wait_ge(V.sem, V.now(i))
                v.tensor_scalar(va4, va4, 1.0 / HD, GN_EPS, ALU.mult, ALU.add).then_inc(V.sem, V.one("var"))
                v.wait_ge(S.sem, S.at("sd", i))
                v.reciprocal(va4, va4).then_inc(V.sem, V.one())
                v.wait_ge(V.sem, V.now(i))
                v.tensor_tensor(O4, O4, bc(va4), ALU.mult).then_inc(V.sem, V.one("on"))
                v.wait_ge(E.sem, E.at("yT", i))
                v.tensor_scalar(y, b4[:, 0:T], col(i, "ln_w"), col(i, "ln_b"), ALU.mult, ALU.add).then_inc(V.sem, V.one("y0"))
                v.wait_ge(V.sem, V.now(i))
                v.tensor_tensor(y, y, bv, ALU.add).then_inc(V.sem, V.one())
                v.wait_ge(V.sem, V.now(i))
                v.tensor_tensor(yc[:, i], y, gt, ALU.mult).then_inc(V.sem, V.one("y2"))
                V.end()
                VF.end()
                if more:
                    VA.end()

            @block.vector
            def _(v):
                v.wait_ge(pload, 64)
                v.tensor_scalar(made[:, :, 0:3], par[:, :, 0:3], -1.0, 1.0, ALU.mult, ALU.add).then_inc(V0.sem, V0.one())
                v.tensor_scalar(made[:, :, 3], par[:, :, c["k_a"]], -1.0, 1.0, ALU.mult, ALU.add).then_inc(V0.sem, V0.one())
                v.tensor_scalar(lom, lmu, -1.0, 1.0, ALU.mult, ALU.add).then_inc(V0.sem, V0.one("made"))
                for s in range(2):
                    dst = (WA, SG)[s]
                    v.wait_ge(S0.sem, S0.at(f"l{s}"))
                    v.scalar_tensor_tensor(dst[:, 1:T], banks[2 + s][:, 0:T - 1], lmu[:, s:s + 1], dst[:, 1:T],
                                           ALU.mult, ALU.add).then_inc(V0.sem, V0.one(f"shift{s}"))
                VA.prime(v)
                V.prime(v)
                VF.prime(v)
                VA.begin()
                for s in range(3):
                    vec_piece(v, 0, s)
                VA.end()
                with v.Fori(0, NI - 1) as i:
                    vec_body(v, i, True)
                vec_body(v, NI - 1, False)

            def pool_body(g, i):
                G.begin()
                g.wait_ge(V.sem, V.at("m01", i))
                for lev in range(1, 6):
                    g.tensor_tensor(NLM[:, lev - 1], G1[:, :, 0], lmask[:, lev].unsqueeze(1).to_broadcast([P, 4, P]), ALU.mult)\
                        .then_inc(G.sem, G.one(f"inv{lev}mask"))
                G.end()

            @block.gpsimd
            def _(g):
                G.prime(g)
                with g.Fori(0, NI) as i:
                    pool_body(g, i)

    def gdn_phase(l):
        NI = 4
        VA, SA, EA = steps("gdA_vec", True), steps("gdA_act", True), steps("gdA_pe", True)
        V, S, E, G = steps("gdB_vec", True), steps("gdB_act", True), steps("gdB_pe", True), steps("gdB_pool", True)
        VG, EG = steps("gdG_vec", True), steps("gdG_pe", True)
        V0, S0, E0 = steps("gd0_vec"), steps("gd0_act"), steps("gd0_pe")
        loaded, loaded_g, tile_a, tile_g = gdn_loaded, gdn_loaded_g, gdn_tile_a, gdn_tile_g
        pload = lsem("gd_params")
        r_ = Region(BRANCH)
        par = r_(8, 12)
        nw = r_(1)
        wab = r_(KT, 16)
        rows = r_(2, 8, 2)
        ab = r_(NB, 16)
        al, ea, e0, z0, z1, m0 = (r_(8, 2) for _ in range(6))
        GA = r_(4, 16)
        st = r_(4, 4)
        Z = r_(8, T)
        GZ = r_(2, T)
        GB = r_(2, 4, P)
        sq, rs = r_(4, T), r_(4, T)
        lru = Lru(r_.at_)
        KQ = r_(4, 2, P)
        KN, DT, DTs, DTi, eg, nkbe, qe = (r_(4, P) for _ in range(7))
        NLT, QKT, Kt, Vt = r_(4, P), r_(4, P), r_(4, P), r_(4, P)
        NLM = r_(6, 4, P)
        T_, TT, X = r_(4, P), r_(4, P), r_(4, P)
        Us, Rs, St = r_(2, P), r_(2, P), r_(2, P)
        O = r_(NB, 2, P)
        O4 = O.rearrange("p b h c -> p (b h) c")
        va4 = r_(4)
        b2, b3, b4, b5, b6, b7 = banks[2:8]
        four = lambda b: b[:, :].rearrange("p (m c) -> p m c", m=4)
        qs = Z[:, 0:2].rearrange("p h (b c) -> p (h b) c", b=NB)
        ks = Z[:, 2:4].rearrange("p h (b c) -> p (h b) c", b=NB)
        rsq = rs[:, 0:2].rearrange("p h (b c) -> p (h b) c", b=NB)
        rsk = rs[:, 2:4].rearrange("p h (b c) -> p (h b) c", b=NB)
        bc4 = lambda x: x.unsqueeze(1).to_broadcast([P, 4, P])

        with nc.Block() as block:
            @block.sync
            def _(sp):
                lru.loads(sp, l)
                sp.dma_start(wab, A["gdn_ab"][l]).then_inc(pload, 16)
                sp.dma_start(par, A["gdn_par"][l]).then_inc(pload, 16)
                sp.dma_start(nw, A["gdn_norm"][l]).then_inc(pload, 16)
                sp.dma_start(rows, A["gdn_rows"][l]).then_inc(pload, 16)
                for s in range(4, 8):
                    sp.wait_ge(EA.sem, EA.at(f"z{s - 4}", 0))
                    tile_a(sp, l, 0, s)
                with sp.Fori(1, NI) as i:
                    for s in range(4):
                        sp.wait_ge(EA.sem, EA.before(f"z{s + 4}", i))
                        tile_a(sp, l, i, s)
                    for n in range(3):
                        sp.wait_ge(EG.sem, EG.before(f"g{n}", i))
                        tile_g(sp, l, i, n)
                    for s in range(4, 8):
                        sp.wait_ge(EA.sem, EA.at(f"z{s - 4}", i))
                        tile_a(sp, l, i, s)
                    sp.wait_ge(EG.sem, EG.before("g3", i))
                    tile_g(sp, l, i, 3)
                for s in range(4):
                    sp.wait_ge(EA.sem, EA.at(f"z{s + 4}", NI - 1))
                    merge_tile(sp, l, s)
                for n in range(4):
                    sp.wait_ge(EG.sem, EG.at(f"g{n}", NI - 1))
                    merge_tile_out(sp, l, n)

            ps_a = [banks[(s + 1) % 2][:, 0:T] for s in range(8)]
            ps_g = [banks[n % 2][:, 0:T] for n in range(4)]

            def pe_piece(te, i, s, parts=range(4), first=False):
                for part in parts:
                    if part == 0:
                        te.wait_ge(loaded[s % 4], 32 * i + 16 * (s // 4) + 16)
                        if s >= 2:
                            te.wait_ge(VA.sem, VA.at(f"tap3_{s - 2}", i))
                        elif not first:
                            te.wait_ge(VG.sem, VG.at(f"g{s + 1}", i - 1))
                    mm = project(te, ps_a[s], s % 4, ks=range(2 * part, 2 * part + 2))
                    if part == 3:
                        mm.then_inc(EA.sem, EA.one(f"z{s}"))

            def pe_side(te, i, n, more):
                te.wait_ge(loaded_g[n], 16 * i + 16)
                if n == 0:
                    te.wait_ge(SA.sem, SA.at("z7", i))
                elif n == 1:
                    te.wait_ge(VG.sem, VG.before("g3", i))
                elif n == 2:
                    te.wait_ge(VG.sem, VG.at("g0", i))
                elif more:
                    te.wait_ge(SA.sem, SA.at("z6", i + 1))
                else:
                    te.wait_ge(VG.sem, VG.at("g1", i))
                project(te, ps_g[n], 4 + n, (ya, yc)[n // 2]).then_inc(EG.sem, EG.one(f"g{n}"))

            def vec_side(v, i, n):
                v.wait_ge(EG.sem, EG.at(f"g{n}", i))
                z = zg[:, (0, 2)[n // 2], 2 * i + n % 2]
                v.tensor_tensor(z, z, ps_g[n], ALU.mult).then_inc(VG.sem, VG.one(f"g{n}"))

            def act_piece(a, i, s):
                if s == 0:
                    a.wait_ge(V.sem, V.before("KN", i))
                    a.wait_ge(E.sem, E.before("vT", i))
                a.wait_ge(EA.sem, EA.at(f"z{s}", i))
                if s < 6:
                    w3 = par[:, 2 * i + s % 2, 4 * (s // 2) + 3:4 * (s // 2) + 4]
                    a.activation(Z[:, s, :], ps_a[s], ACT.Copy, scale=w3).then_inc(SA.sem, SA.one(f"z{s}"))
                else:
                    a.activation(Z[:, s, :], ps_a[s], ACT.Copy).then_inc(SA.sem, SA.one(f"z{s}"))

            def vec_piece(v, i, s):
                if s >= 6:
                    return
                v.wait_ge(SA.sem, SA.at(f"z{s}", i))
                for sh in (1, 2, 3):
                    if sh > 1:
                        v.wait_ge(VA.sem, VA.now(i))
                    tap = 4 * (s // 2) + 3 - sh
                    v.scalar_tensor_tensor(Z[:, s, sh:T], ps_a[s][:, 0:T - sh], par[:, 2 * i + s % 2, tap:tap + 1],
                                           Z[:, s, sh:T], ALU.mult, ALU.add).then_inc(VA.sem, VA.one(f"tap{sh}_{s}"))

            def pe_body(te, i, more):
                def fill(n, y):
                    if more:
                        pe_piece(te, i + 1, n, (range(3), range(3, 4))[y])

                if more:
                    EA.begin()
                EG.begin()
                E.begin()
                pe_side(te, i, 0, more)
                te.wait_ge(V.sem, V.before("y", i))
                te.wait_ge(V.sem, V.at("sq", i))
                for x, bk in enumerate((b2, b3)):
                    te.matmul(bk[:, :], ones, sq[:, 2 * x:2 * x + 2], start=True, stop=True).then_inc(E.sem, E.one(f"ss{x}"))
                for x, (bk, m) in enumerate(((b4, upto), (b5, ident))):
                    for q in range(4):
                        mm = te.matmul(four(bk)[:, q], GB[:, x, q], m, start=True, stop=True)
                    mm.then_inc(E.sem, E.one(("gcrow", "brow")[x]))
                for q in range(4):
                    mm = te.transpose(four(b7)[:, q], Z[:, 4 + q // 2, (q % 2) * P:(q % 2 + 1) * P], ident)
                mm.then_inc(E.sem, E.one("vT"))
                pe_side(te, i, 1, more)
                pe_side(te, i, 2, more)
                te.wait_ge(V.sem, V.at("KN", i))
                for q in range(4):
                    mm = te.transpose(four(b6)[:, q], KN[:, q], ident)
                mm.then_inc(E.sem, E.one("kT"))
                te.wait_ge(V.sem, V.at("kb", i))
                for q in range(4):
                    bk = (b2, b3)[q // 2]
                    mm = te.matmul(bk[:, (q % 2) * T:(q % 2 + 1) * T], KN[:, q], KQ[:, q], start=True, stop=True)
                    if q % 2:
                        mm.then_inc(E.sem, E.one(f"g{q // 2}"))
                fill(0, 0)
                fill(0, 1)
                te.wait_ge(S.sem, S.at("eg", i))
                te.wait_ge(V.sem, V.at("TT0", i))
                for q in range(4):
                    mm = te.transpose(four(b4)[:, q], TT[:, q], ident)
                mm.then_inc(E.sem, E.one("T0"))
                te.wait_ge(V.sem, V.at("QKT", i))
                invert_levels(te, None, None, None, "inv", E, S, V, G, i, NLM, T_, TT, X, b5, b2, b3, N_LEVELS, fill)
                te.wait_ge(V.sem, V.at("inv6TT", i))
                te.wait_ge(S.sem, S.at("Vt", i))
                two = lambda b: b[:, 0:2 * P].rearrange("p (h c) -> p h c", h=2)
                for hh in range(2):
                    mm = te.matmul(two(b6)[:, hh], TT[:, 2 * hh], Vt[:, 2 * hh], start=True, stop=True)
                mm.then_inc(E.sem, E.one("U0"))
                te.wait_ge(S.sem, S.at("U0", i))
                for hh in range(2):
                    mm = te.matmul(two(b4)[:, hh], Kt[:, 2 * hh], Us[:, hh], start=True, stop=True)
                mm.then_inc(E.sem, E.one("S"))
                for hh in range(2):
                    mm = te.matmul(two(b7)[:, hh], QKT[:, 2 * hh], Us[:, hh], start=True, stop=True)
                mm.then_inc(E.sem, E.one("O0"))
                te.wait_ge(S.sem, S.at("S", i))
                for hh in range(2):
                    mm = te.matmul(two(b5)[:, hh], nkbe[:, 2 * hh + 1], St[:, hh], start=True, stop=True)
                mm.then_inc(E.sem, E.one("R"))
                fill(7, 0)
                fill(7, 1)
                te.wait_ge(V.sem, V.at("R", i))
                for hh in range(2):
                    mm = te.matmul(two(b6)[:, hh], TT[:, 2 * hh + 1], Rs[:, hh], start=True, stop=True)
                mm.then_inc(E.sem, E.one("U1"))
                te.wait_ge(S.sem, S.at("U1", i))
                for hh in range(2):
                    te.matmul(two(b2)[:, hh], qe[:, 2 * hh + 1], St[:, hh], start=True, stop=False)
                    mm = te.matmul(two(b2)[:, hh], QKT[:, 2 * hh + 1], Us[:, hh], start=False, stop=True)
                mm.then_inc(E.sem, E.one("O1"))
                pe_side(te, i, 3, more)
                te.wait_ge(V.sem, V.at("on", i))
                for hh in range(2):
                    for b in range(NB):
                        mm = te.transpose(four(b3)[:, 2 * hh + b], O[:, b, hh], ident)
                mm.then_inc(E.sem, E.one("yT"))
                E.end()
                EG.end()
                if more:
                    EA.end()

            @block.tensor
            def _(te):
                te.wait_ge(pload, 64)
                for b in range(NB):
                    for k in range(KT):
                        mm = te.matmul(b2[:, 16 * b:16 * b + 16], xn[:, k, b * P:(b + 1) * P], wab[:, k], start=(k == 0), stop=(k == KT - 1))
                mm.then_inc(E0.sem, E0.one("ab"))
                lru.tensor(te)
                EA.prime(te)
                E.prime(te)
                EG.prime(te)
                EA.begin()
                for s in range(8):
                    pe_piece(te, 0, s, first=True)
                EA.end()
                te.wait_ge(V0.sem, V0.at("g"))
                te.matmul(b3[:, 0:16], upto, GA[:, 0], start=True, stop=True)
                te.matmul(b3[:, 16:32], after, GA[:, 0], start=True, stop=True).then_inc(E0.sem, E0.one("gc"))
                te.wait_ge(S0.sem, S0.at("erev"))
                te.wait_ge(lru.V.sem, lru.V.at("ya"))
                with te.Fori(0, NI - 1) as i:
                    pe_body(te, i, True)
                pe_body(te, NI - 1, False)

            def act_body(a, i, more):
                def fill(n):
                    if more:
                        act_piece(a, i + 1, n)

                if more:
                    SA.begin()
                S.begin()
                a.wait_ge(SA.sem, SA.at("z7", i))
                a.wait_ge(VA.sem, VA.at("tap3_5", i))
                a.wait_ge(V.sem, V.before("y", i))
                a.activation(Z[:, 0:6], Z[:, 0:6], ACT.Silu).then_inc(S.sem, S.one("silu"))
                a.activation(GZ, Z[:, 6:8], ACT.Silu).then_inc(S.sem, S.one("siluz"))
                a.wait_ge(V.sem, V.at("rs0", i))
                a.activation(rs, rs, ACT.Sqrt).then_inc(S.sem, S.one("rs"))
                a.wait_ge(V.sem, V.at("DT0", i))
                a.activation(DT, DT, ACT.Exp).then_inc(S.sem, S.one("DT"))
                a.activation(eg, four(b4), ACT.Exp).then_inc(S.sem, S.one("eg"))
                a.wait_ge(E.sem, E.at("vT", i))
                for q in range(4):
                    a.activation(Vt[:, q], four(b7)[:, q], ACT.Copy, scale=st[:, 1, q:q + 1]).then_inc(S.sem, S.one("Vt"))
                a.wait_ge(E.sem, E.at("kT", i))
                for q in range(4):
                    a.activation(Kt[:, q], four(b6)[:, q], ACT.Copy, scale=st[:, 3, q:q + 1]).then_inc(S.sem, S.one("Kt"))
                fill(0)
                a.wait_ge(E.sem, E.at("T0", i))
                a.activation(T_, four(b4), ACT.Copy).then_inc(S.sem, S.one("invT"))
                invert_levels(None, a, None, None, "inv", E, S, V, G, i, NLM, T_, TT, X, b5, b2, b3, N_LEVELS, fill)
                two = lambda b: b[:, 0:2 * P].rearrange("p (h c) -> p h c", h=2)
                a.wait_ge(E.sem, E.at("U0", i))
                a.activation(Us, two(b6), ACT.Copy).then_inc(S.sem, S.one("U0"))
                a.wait_ge(E.sem, E.at("S", i))
                a.activation(St, two(b4), ACT.Copy).then_inc(S.sem, S.one("S"))
                a.wait_ge(E.sem, E.at("O0", i))
                a.activation(O[:, 0], two(b7), ACT.Copy).then_inc(S.sem, S.one("O0"))
                fill(7)
                a.wait_ge(E.sem, E.at("U1", i))
                a.activation(Us, two(b6), ACT.Copy).then_inc(S.sem, S.one("U1"))
                a.wait_ge(E.sem, E.at("O1", i))
                a.activation(O[:, 1], two(b2), ACT.Copy).then_inc(S.sem, S.one("O1"))
                a.wait_ge(V.sem, V.at("var", i))
                a.activation(va4, va4, ACT.Sqrt).then_inc(S.sem, S.one("sd"))
                S.end()
                if more:
                    SA.end()

            @block.scalar
            def _(a):
                a.wait_ge(pload, 64)
                a.wait_ge(E0.sem, E0.at("ab"))
                a.activation(ab, b2[:, 0:32].rearrange("p (b j) -> p b j", b=NB), ACT.Copy).then_inc(S0.sem, S0.one("ab"))
                a.activation(ea, rows[:, 0], ACT.Exp).then_inc(S0.sem, S0.one())
                a.wait_ge(V0.sem, V0.at("al"))
                softplus_exp(a, S0, al, e0, "sp")
                a.activation(GA[:, 1].rearrange("p (h b) -> p h b", b=NB), ab[:, :, 8:16].rearrange("p b h -> p h b"),
                             ACT.Sigmoid).then_inc(S0.sem, S0.one("beta"))
                SA.prime(a)
                S.prime(a)
                SA.begin()
                lru.scalar(a, lambda s: act_piece(a, 0, s))
                SA.end()
                a.wait_ge(E0.sem, E0.at("gc"))
                a.activation(GA[:, 2], b3[:, 0:16], ACT.Copy).then_inc(S0.sem, S0.one())
                a.activation(GA[:, 3], b3[:, 16:32], ACT.Exp).then_inc(S0.sem, S0.one("erev"))
                with a.Fori(0, NI - 1) as i:
                    act_body(a, i, True)
                act_body(a, NI - 1, False)

            def vec_body(v, i, more):
                def fill(n):
                    if more:
                        vec_piece(v, i + 1, n)

                if more:
                    VA.begin()
                VG.begin()
                V.begin()
                v.wait_ge(S.sem, S.before("Kt", i))
                v.tensor_copy(st, GA[:, :, bass.ds(4 * i, 4)]).then_inc(V.sem, V.one("st"))
                v.wait_ge(V.sem, V.now(i))
                v.tensor_copy(GB, st[:, 0:2].unsqueeze(3).to_broadcast([P, 2, 4, P])).then_inc(V.sem, V.one("GB"))
                v.wait_ge(S.sem, S.at("silu", i))
                v.tensor_tensor(sq, Z[:, 0:4], Z[:, 0:4], ALU.mult).then_inc(V.sem, V.one("sq"))
                for x, bk in enumerate((b2, b3)):
                    v.wait_ge(E.sem, E.at(f"ss{x}", i))
                    v.tensor_scalar(rs[:, 2 * x:2 * x + 2], bk[:, :].rearrange("p (h t) -> p h t", h=2), EPS, None, ALU.add)\
                        .then_inc(V.sem, V.one("rs0"))
                v.wait_ge(E.sem, E.at("gcrow", i))
                for q in range(4):
                    v.tensor_scalar(DT[:, q], four(b4)[:, q], st[:, 2, q:q + 1], 0.0, ALU.subtract, ALU.min)\
                        .then_inc(V.sem, V.one("DT0"))
                vec_side(v, i, 0)
                v.wait_ge(S.sem, S.at("rs", i))
                v.reciprocal(rs, rs).then_inc(V.sem, V.one())
                v.wait_ge(V.sem, V.now(i))
                v.tensor_tensor(KN, ks, rsk, ALU.mult).then_inc(V.sem, V.one())
                v.scalar_tensor_tensor(KQ[:, :, 1], qs, GDN_SCALE, rsq, ALU.mult, ALU.mult).then_inc(V.sem, V.one("KN"))
                v.wait_ge(V.sem, V.now(i))
                v.wait_ge(E.sem, E.at("brow", i))
                v.tensor_tensor(KQ[:, :, 0], KN, four(b5), ALU.mult).then_inc(V.sem, V.one("kb"))
                vec_side(v, i, 1)
                v.wait_ge(S.sem, S.at("DT", i))
                v.tensor_tensor(DTs, DT, bc4(gmask[:, 0]), ALU.mult).then_inc(V.sem, V.one())
                v.tensor_tensor(DTi, DT, bc4(gmask[:, 1]), ALU.mult).then_inc(V.sem, V.one())
                v.wait_ge(V.sem, V.now(i))
                for x, bk in enumerate((b2, b3)):
                    ps = bk[:, :].rearrange("p (m x c) -> p m x c", m=2, x=2)
                    v.wait_ge(E.sem, E.at(f"g{x}", i))
                    v.scalar_tensor_tensor(NLT[:, 2 * x:2 * x + 2], ps[:, :, 0], -1.0, DTs[:, 2 * x:2 * x + 2], ALU.mult, ALU.mult)\
                        .then_inc(V.sem, V.one(f"NLT{x}"))
                v.wait_ge(V.sem, V.now(i))
                v.tensor_tensor(TT, NLT, bc4(lmask[:, 0]), ALU.mult).then_inc(V.sem, V.one())
                v.wait_ge(V.sem, V.now(i))
                v.tensor_tensor(TT, TT, bc4(ident), ALU.add).then_inc(V.sem, V.one("TT0"))
                vec_side(v, i, 2)
                for x, bk in enumerate((b2, b3)):
                    ps = bk[:, :].rearrange("p (m x c) -> p m x c", m=2, x=2)
                    v.tensor_tensor(QKT[:, 2 * x:2 * x + 2], ps[:, :, 1], DTi[:, 2 * x:2 * x + 2], ALU.mult)\
                        .then_inc(V.sem, V.one("QKT"))
                v.wait_ge(S.sem, S.at("eg", i))
                v.scalar_tensor_tensor(nkbe, KQ[:, :, 0], -1.0, eg, ALU.mult, ALU.mult).then_inc(V.sem, V.one())
                v.tensor_tensor(qe, KQ[:, :, 1], eg, ALU.mult).then_inc(V.sem, V.one("qe"))
                fill(0)
                v.wait_ge(S.sem, S.at("invT", i))
                invert_levels(None, None, v, None, "inv", E, S, V, G, i, NLM, T_, TT, X, b5, b2, b3, N_LEVELS, fill)
                two = lambda b: b[:, 0:2 * P].rearrange("p (h c) -> p h c", h=2)
                v.wait_ge(E.sem, E.at("R", i))
                v.wait_ge(S.sem, S.at("Vt", i))
                v.tensor_tensor(Rs, two(b5), Vt.rearrange("p (h b) c -> p h b c", h=2)[:, :, 1], ALU.add).then_inc(V.sem, V.one("R"))
                fill(7)
                v.wait_ge(S.sem, S.at("O1", i))
                v.tensor_tensor(eg, O4, O4, ALU.mult).then_inc(V.sem, V.one())
                v.wait_ge(V.sem, V.now(i))
                v.tensor_reduce(va4, eg, AX.X, ALU.add).then_inc(V.sem, V.one())
                v.wait_ge(V.sem, V.now(i))
                v.tensor_scalar(va4, va4, 1.0 / P, EPS, ALU.mult, ALU.add).then_inc(V.sem, V.one("var"))
                v.wait_ge(S.sem, S.at("sd", i))
                v.reciprocal(va4, va4).then_inc(V.sem, V.one())
                v.wait_ge(V.sem, V.now(i))
                v.tensor_tensor(O4, O4, va4.unsqueeze(2).to_broadcast([P, 4, P]), ALU.mult).then_inc(V.sem, V.one("on"))
                v.wait_ge(E.sem, E.at("yT", i))
                v.scalar_tensor_tensor(yb[:, bass.ds(2 * i, 2)], b3[:, :].rearrange("p (h t) -> p h t", h=2), nw, GZ, ALU.mult, ALU.mult)\
                    .then_inc(V.sem, V.one("y"))
                vec_side(v, i, 3)
                V.end()
                VG.end()
                if more:
                    VA.end()

            @block.vector
            def _(v):
                v.wait_ge(pload, 64)
                v.wait_ge(S0.sem, S0.at("ab"))
                v.tensor_tensor(al, ab[:, :, 0:8].rearrange("p b h -> p h b"), rows[:, 1], ALU.add).then_inc(V0.sem, V0.one("al"))
                v.wait_ge(V0.sem, V0.now())
                v.wait_ge(S0.sem, S0.at("sp_e"))
                softplus_log(v, V0, al, e0, z0, z1, m0, e0)
                v.wait_ge(V0.sem, V0.now())
                v.scalar_tensor_tensor(GA[:, 0].rearrange("p (h b) -> p h b", b=NB), m0, -1.0, ea, ALU.mult, ALU.mult)\
                    .then_inc(V0.sem, V0.one("g"))
                v.wait_ge(S0.sem, S0.at("beta"))
                lru.vector_first(v)
                VA.prime(v)
                V.prime(v)
                VG.prime(v)
                VA.begin()
                lru.vector(v, lambda s: vec_piece(v, 0, s))
                VA.end()
                v.wait_ge(S0.sem, S0.at("erev"))
                v.wait_ge(lru.S.sem, lru.S.at("zg"))
                with v.Fori(0, NI - 1) as i:
                    vec_body(v, i, True)
                vec_body(v, NI - 1, False)

            @block.gpsimd
            def _(g):
                G.prime(g)
                with g.Fori(0, NI) as i:
                    G.begin()
                    g.wait_ge(V.sem, V.at("NLT1", i))
                    for lev in range(1, N_LEVELS):
                        g.tensor_tensor(NLM[:, lev - 1], NLT, bc4(lmask[:, lev]), ALU.mult).then_inc(G.sem, G.one(f"inv{lev}mask"))
                    G.end()

    def merge_phase(l):
        V, E = steps("mg_vec", True), steps("mg_pe", True)
        V2, E2 = steps("wo_vec", True), steps("wo_pe", True)
        VS = steps("mg0_vec")
        r_ = Region(BRANCH)
        merged = r_(KT, T)
        with nc.Block() as block:
            @block.sync
            def _(sp):
                for k in range(4):
                    sp.wait_ge(E.sem, E.at(f"z{k}", 0))
                    merge_tile(sp, l, 4 + k)
                for k in range(4):
                    sp.wait_ge(E2.sem, E2.at(f"o{k}", 0))
                    merge_tile_out(sp, l, 4 + k)

            @block.tensor
            def _(te):
                E.prime(te)
                with te.Fori(0, 2) as i:
                    E.begin()
                    for s in range(4):
                        te.wait_ge(merge_loaded[s], 16 * i + 16)
                        te.wait_ge(V.sem, V.before(f"t{s}", i))
                        project(te, banks[s][:, 0:T], s, yb).then_inc(E.sem, E.one(f"z{s}"))
                    E.end()
                te.wait_ge(V.sem, V.at("m3", 1))
                E2.prime(te)
                with te.Fori(0, 2) as i:
                    E2.begin()
                    for s in range(4):
                        te.wait_ge(merge_loaded_out[s], 16 * i + 16)
                        te.wait_ge(V2.sem, V2.before(f"h{s}", i))
                        project(te, banks[4 + s][:, 0:T], 4 + s, merged).then_inc(E2.sem, E2.one(f"o{s}"))
                    E2.end()

            @block.vector
            def _(v):
                v.tensor_tensor(zg[:, 0], zg[:, 0], zg[:, 2], ALU.add).then_inc(VS.sem, VS.one("sum"))
                v.wait_ge(VS.sem, VS.at("sum"))
                V.prime(v)
                V2.prime(v)
                with v.Fori(0, 2) as i:
                    V.begin()
                    for s in range(4):
                        v.wait_ge(E.sem, E.at(f"z{s}", i))
                        v.tensor_tensor(zg[:, 1, 4 * i + s], zg[:, 1, 4 * i + s], banks[s][:, 0:T], ALU.mult)\
                            .then_inc(V.sem, V.one(f"t{s}"))
                        v.wait_ge(V.sem, V.now(i))
                        v.tensor_tensor(merged[:, 4 * i + s], zg[:, 0, 4 * i + s], zg[:, 1, 4 * i + s], ALU.add)\
                            .then_inc(V.sem, V.one(f"m{s}"))
                    V.end()
                with v.Fori(0, 2) as i:
                    V2.begin()
                    for s in range(4):
                        v.wait_ge(E2.sem, E2.at(f"o{s}", i))
                        v.tensor_tensor(h[:, 4 * i + s], h[:, 4 * i + s], banks[4 + s][:, 0:T], ALU.add).then_inc(V2.sem, V2.one(f"h{s}"))
                    V2.end()
                v.wait_ge(V2.sem, V2.at("h3", 1))

    PQ = Region(PEER)
    scores = PQ(NB, 2 * PH, NK)
    f32r = lambda ap: ap.bitcast(F32R)

    NQ = 2 * PH
    query_loaded = [lsem(f"pq_tile{t}") for t in range(NQ)]
    query_loaded_keys = lsem("pq_keys")
    query_region = Region(PQ.at_)
    query_keys = query_region(NQ, NK)
    query_region.at_ = max(query_region.at_, BRANCH + (2 * KT + 1) * T + 1)
    query_more = query_region(NQ - 8, KT * P)

    def query_tile(t):
        return ring[:, t] if t < 8 else query_more[:, t - 8]

    def query_first_loads(sp, l):
        sp.dma_start(query_keys, A["keys"][l]).then_inc(query_loaded_keys, 16)
        for t in range(NQ):
            sp.dma_start(query_tile(t), A["w_query"][l, t]).then_inc(query_loaded[t], 16)

    def peer_topk_phase(l):
        V, S, E = steps("tk_vec"), steps("tk_act"), steps("tk_pe")
        SQ, EQ = steps("pq_act", True), steps("pq_pe", True)
        x_high, x_low = lsem("pq_x_high"), lsem("pq_x_low")
        r_ = Region(query_region.at_)
        q = r_(2, P)
        NS, HALF = 2 * PH, TOPK // 2
        ROWS = TOPK + 1
        left = r_(NS, NK)
        top, topi, topf = r_(NS, TOPK), r_(NS, TOPK, dt=U32), r_(NS, TOPK)
        cand, cand_left = r_(PH, ROWS * HALF), r_(PH, ROWS * HALF)
        best, pos = r_(PH, TOPK), r_(PH, TOPK, dt=U32)
        rowi, coli = r_(PH * TOPK, dt=U32), r_(PH * TOPK, dt=U32)
        row, col, rank0, second = (r_(PH * TOPK) for _ in range(4))
        eq = r_(PH * TOPK, TOPK)
        out_e1, out_e2, out_gate = ([r_(PH, TOPK) for _ in range(NB)] for _ in range(3))
        gsum, dummy = r_(PH), r_(1)
        WORST = -3.0e38
        side = lambda x, q: x.rearrange("p (h s) k -> p h s k", s=2)[:, :, q]
        flat = lambda x: x.rearrange("p h k -> p (h k)")
        with nc.Block() as block:
            @block.vector
            def _(v):
                def settled():
                    v.wait_ge(V.sem, V.now())
                    v.memset(dummy, 0.0).then_inc(V.sem, V.one())

                def best16(n, x, x_left, vals, idx):
                    settled()
                    for k in range(n):
                        v.max(vals[:, k, 0:HALF], x[:, k]).then_inc(V.sem, V.one())
                    settled()
                    for k in range(n):
                        v.max_index(idx[:, k, 0:HALF], vals[:, k, 0:HALF], x[:, k]).then_inc(V.sem, V.one())
                        v.match_replace(x_left[:, k], vals[:, k, 0:HALF], x[:, k], WORST).then_inc(V.sem, V.one())
                    settled()
                    for k in range(n):
                        v.max(vals[:, k, HALF:TOPK], x_left[:, k]).then_inc(V.sem, V.one())
                    settled()
                    for k in range(n):
                        v.max_index(idx[:, k, HALF:TOPK], vals[:, k, HALF:TOPK], x_left[:, k]).then_inc(V.sem, V.one())
                    v.wait_ge(V.sem, V.now())

                v.memset(dummy, 0.0).then_inc(V.sem, V.one())
                v.wait_ge(x_high, 1)
                v.tensor_tensor(f32r(xlow[:]), xn, xhigh[:], ALU.subtract).then_inc(x_low, 1)
                for i in range(NB):
                    e1, e2, gate = out_e1[i], out_e2[i], out_gate[i]
                    v.wait_ge(SQ.sem, SQ.at("s3", i))
                    best16(NS, scores[:, i], left, top, topi)
                    v.tensor_copy(topf, topi).then_inc(V.sem, V.one())
                    v.tensor_tensor(cand[:, :, 0:TOPK], side(top, 0)[:, :, 0:1].to_broadcast([P, PH, TOPK]), side(top, 1), ALU.add)\
                        .then_inc(V.sem, V.one())
                    v.tensor_tensor(cand[:, :, TOPK:].rearrange("p h (a b) -> p h a b", b=HALF),
                                    side(top, 0)[:, :, 1:TOPK].unsqueeze(3).to_broadcast([P, PH, TOPK - 1, HALF]),
                                    side(top, 1)[:, :, 0:HALF].unsqueeze(2).to_broadcast([P, PH, TOPK - 1, HALF]), ALU.add)\
                        .then_inc(V.sem, V.one())
                    best16(PH, cand, cand_left, best, pos)
                    v.tensor_tensor(gate, best, best[:, :, 0:1].to_broadcast([P, PH, TOPK]), ALU.subtract).then_inc(V.sem, V.one(f"e{i}"))
                    v.tensor_scalar(rowi, flat(pos), 3, None, ALU.logical_shift_right).then_inc(V.sem, V.one())
                    v.tensor_scalar(coli, flat(pos), 7, None, ALU.bitwise_and).then_inc(V.sem, V.one())
                    v.wait_ge(V.sem, V.now())
                    v.tensor_copy(row, rowi).then_inc(V.sem, V.one())
                    v.tensor_copy(col, coli).then_inc(V.sem, V.one())
                    v.wait_ge(V.sem, V.now())
                    v.tensor_scalar(rank0, row, -1.0, 0.0, ALU.add, ALU.max).then_inc(V.sem, V.one())
                    v.tensor_scalar(second, row, 1.0, float(HALF), ALU.is_equal, ALU.mult).then_inc(V.sem, V.one())
                    v.wait_ge(V.sem, V.now())
                    v.tensor_tensor(col, col, second, ALU.add).then_inc(V.sem, V.one())
                    for q, (dst, rank) in enumerate(((e1, rank0), (e2, col))):
                        v.wait_ge(V.sem, V.now())
                        v.tensor_tensor(eq, rank.unsqueeze(2).to_broadcast([P, PH * TOPK, TOPK]),
                                        iota[:, 0:TOPK].unsqueeze(1).to_broadcast([P, PH * TOPK, TOPK]), ALU.is_equal)\
                            .then_inc(V.sem, V.one())
                        v.wait_ge(V.sem, V.now())
                        eq4 = eq.rearrange("p (h k) a -> p h k a", h=PH)
                        v.tensor_tensor(eq4, eq4, side(topf, q).unsqueeze(2).to_broadcast([P, PH, TOPK, TOPK]), ALU.mult)\
                            .then_inc(V.sem, V.one())
                        v.wait_ge(V.sem, V.now())
                        v.tensor_reduce(flat(dst), eq, AX.X, ALU.add).then_inc(V.sem, V.one(f"key{q}_{i}"))
                    v.wait_ge(S.sem, S.at(f"exp{i}"))
                    v.tensor_reduce(gsum, gate, AX.X, ALU.add).then_inc(V.sem, V.one())
                    v.wait_ge(V.sem, V.now())
                    v.reciprocal(gsum, gsum).then_inc(V.sem, V.one())
                    v.wait_ge(V.sem, V.now())
                    v.tensor_tensor(gate, gate, gsum.unsqueeze(2).to_broadcast([P, PH, TOPK]), ALU.mult).then_inc(V.sem, V.one(f"gate{i}"))
                v.wait_ge(x_low, 1)

            @block.scalar
            def _(a):
                a.activation(f32r(xhigh[:]), xn, ACT.Copy).then_inc(x_high, 1)
                SQ.prime(a)
                with a.Fori(0, NB) as b:
                    SQ.begin()
                    for t in range(NQ):
                        a.wait_ge(EQ.sem, EQ.at(f"q{t}", b))
                        a.activation(q[:, t % 2], banks[t % 2][:, 0:P], ACT.Copy).then_inc(SQ.sem, SQ.one(f"q{t}"))
                        if t % 4 == 3:
                            a.wait_ge(EQ.sem, EQ.at(f"s{t}", b))
                            g = t // 4
                            a.activation(scores[:, b, 4 * g:4 * g + 4], banks[2 + g % 2][:, :].rearrange("p (n k) -> p n k", n=4), ACT.Copy)\
                                .then_inc(SQ.sem, SQ.one(f"s{g}"))
                    SQ.end()
                for i in range(NB):
                    a.wait_ge(V.sem, V.at(f"e{i}"))
                    a.activation(out_gate[i], out_gate[i], ACT.Exp).then_inc(S.sem, S.one(f"exp{i}"))
                    for n in range(3):
                        a.wait_ge(E.sem, E.at(f"t{n}_{i}"))
                        a.activation(slots[:, n, i * P:(i + 1) * P], banks[4 + n][:, 0:P], ACT.Copy).then_inc(S.sem, S.one(f"c{n}_{i}"))
                a.wait_ge(S.sem, S.now())

            @block.tensor
            def _(te):
                def score(b, t):
                    te.wait_ge(SQ.sem, SQ.at(f"q{t}", b))
                    g = t // 4
                    if t % 4 == 0:
                        te.wait_ge(SQ.sem, SQ.at(f"s{g - 2}", b) if g > 1 else SQ.before(f"s{g + 2}", b))
                    te.matmul(banks[2 + g % 2][:, (t % 4) * NK:(t % 4 + 1) * NK], q[:, t % 2], query_keys[:, t], start=True, stop=True)\
                        .then_inc(EQ.sem, EQ.one(f"s{t}"))

                te.wait_ge(query_loaded_keys, 16)
                EQ.prime(te)
                with te.Fori(0, NB) as b:
                    EQ.begin()
                    for t in range(NQ):
                        te.wait_ge(query_loaded[t], 16)
                        te.wait_ge(SQ.sem, SQ.at(f"q{t - 2}", b) if t > 1 else SQ.before(f"q{NQ - 2 + t}", b))
                        for k in range(KT):
                            mm = te.matmul(banks[t % 2][:, 0:P], query_tile(t)[:, k * P:(k + 1) * P], xn[:, k, bass.ds(b * P, P)],
                                           start=(k == 0), stop=(k == KT - 1))
                        mm.then_inc(EQ.sem, EQ.one(f"q{t}"))
                        if t:
                            score(b, t - 1)
                    score(b, NQ - 1)
                    EQ.end()
                for i in range(NB):
                    for n, src in enumerate((out_e1, out_e2, out_gate)):
                        te.wait_ge(V.sem, V.at((f"key0_{i}", f"key1_{i}", f"gate{i}")[n]))
                        if i:
                            te.wait_ge(S.sem, S.at(f"c{n}_{i - 1}"))
                        te.transpose(banks[4 + n][:, 0:P], flat(src[i]), ident).then_inc(E.sem, E.one(f"t{n}_{i}"))

    GATES = arena[:, :].rearrange("p (t j) -> p t j", t=T)

    u_in = [lsem(f"ex_u_in{s}") for s in range(2)]
    v_in = [lsem(f"ex_v_in{s}") for s in range(2)]

    def u_tile(sp, l, j4, u):
        sp.dma_start(raw[:, u % 2], A["u"][l, j4 + u]).then_inc(u_in[u % 2], 16)

    def v_tile(sp, l, j4, u):
        sp.dma_start(raw[:, 2 + u % 2], A["v"][l, j4 + u]).then_inc(v_in[u % 2], 16)

    def peer_gate_phase(l):
        NI = T // 16
        V, S, E, G = steps("gt_vec", True), steps("gt_act", True), steps("gt_pe", True), steps("gt_pool", True)
        onehot = raw[:, 1:4].rearrange("p s c -> p (s c)")
        oh1 = onehot[:, 0:16 * P].rearrange("p (u k) -> p u k", u=16)
        oh2 = onehot[:, 16 * P:24 * P].rearrange("p (u k) -> p u k", u=8)

        def against_slot1(engine, i, g, op):
            return engine.tensor_tensor(oh1[:, 4 * g:4 * g + 4], iota.unsqueeze(1).to_broadcast([P, 4, NK]),
                                        slot1[:, bass.ds(16 * i + 4 * g, 4)].unsqueeze(2).to_broadcast([P, 4, NK]), op)

        with nc.Block() as block:
            @block.vector
            def _(v):
                V.prime(v)
                with v.Fori(0, NI) as i:
                    V.begin()
                    for x in range(2):
                        v.wait_ge(E.sem, E.before(f"g{2 * x}", i))
                        against_slot1(v, i, 2 * x, ALU.is_equal).then_inc(V.sem, V.one())
                        for u in range(8 * x, 8 * x + 8):
                            tok = bass.ds(16 * i + u, 1)
                            if u % 4 == 0:
                                v.wait_ge(E.sem, E.at(f"g{u // 4 - 2}", i) if x else E.before(f"g{u // 4 + 2}", i))
                            v.tensor_scalar(oh2[:, u % 8], iota, slot2[:, tok], slotg[:, tok], ALU.is_equal, ALU.mult)\
                                .then_inc(V.sem, V.one(f"u{u}"))
                    V.end()

            @block.gpsimd
            def _(g):
                G.prime(g)
                with g.Fori(0, NI) as i:
                    G.begin()
                    for x in range(2):
                        g.wait_ge(E.sem, E.before(f"g{2 * x + 1}", i))
                        against_slot1(g, i, 2 * x + 1, ALU.subtract).then_inc(G.sem, G.one(f"rows{x}"))
                    G.end()

            @block.tensor
            def _(te):
                E.prime(te)
                with te.Fori(0, NI) as i:
                    E.begin()
                    for g in range(4):
                        te.wait_ge(S.sem, S.before(f"g{g}", i))
                        for u in range(4 * g, 4 * g + 4):
                            te.wait_ge(V.sem, V.at(f"u{u}", i))
                            if u % 8 == 4:
                                te.wait_ge(S.sem, S.at(f"rows{u // 8}", i))
                            mm = te.matmul(banks[g][:, (u % 4) * NK:(u % 4 + 1) * NK], oh1[:, u], oh2[:, u % 8], start=True, stop=True)
                        mm.then_inc(E.sem, E.one(f"g{g}"))
                    E.end()

            @block.scalar
            def _(a):
                S.prime(a)
                with a.Fori(0, NI) as i:
                    S.begin()
                    for g in range(4):
                        if g < 2:
                            rows = oh1[:, 8 * g + 4:8 * g + 8]
                            a.wait_ge(G.sem, G.at(f"rows{g}", i))
                            a.activation(rows, rows, ACT.Abs).then_inc(S.sem, S.one())
                            a.wait_ge(S.sem, S.now(i))
                            a.activation(rows, rows, ACT.Relu, scale=-1.0, bias=ones[:, 0:1]).then_inc(S.sem, S.one(f"rows{g}"))
                        a.wait_ge(E.sem, E.at(f"g{g}", i))
                        a.activation(GATES[:, bass.ds(16 * i + 4 * g, 4)], banks[g][:, :].rearrange("p (u k) -> p u k", u=4), ACT.Copy)\
                            .then_inc(S.sem, S.one(f"g{g}"))
                    S.end()
                a.wait_ge(S.sem, S.at("g3", NI - 1))

            @block.sync
            def _(sp):
                u_tile(sp, l, 0, 0)

    def peer_expert_phase(l):
        FIRST = 4
        UJ = 4
        NI = NK // UJ
        H = KT * P // 2
        names = ("u_high", "u_low", "v_high", "v_low", "hidden", "gelu", "gated", "a_high", "a_low", "mixed")
        u_high, u_low, v_high, v_low, hidden, gelu, gated, a_high, a_low, mixed = [lsem("ex_" + n) for n in names]
        opened, added = lsem("ex_opened"), lsem("ex_added")
        u_raw, v_raw = [raw[:, s] for s in range(2)], [raw[:, 2 + s] for s in range(2)]
        u_hi, u_lo, v_hi, v_lo = (parts[:, n] for n in range(4))
        act = [slots[:, s] for s in range(2)]
        ybanks = banks[4:8]
        U = (u_in, u_raw, u_hi, u_lo, u_high, u_low, hidden)
        W = (v_in, v_raw, v_hi, v_lo, v_high, v_low, mixed)

        def start(engine, *sems):
            for s in sems:
                engine.sem_inc(s, FIRST)

        def steps_of(engine, one_step):
            with engine.Fori(0, NI - 1) as i:
                for u in range(UJ):
                    one_step(UJ * i, u)
            for u in range(UJ):
                one_step(UJ * (NI - 1), u)

        ends = lambda j4, u, ahead: isinstance(j4, int) and j4 + u + ahead >= NK
        with nc.Block() as block:
            @block.sync
            def _(sp):
                u_tile(sp, l, 0, 1)
                v_tile(sp, l, 0, 0)
                sp.wait_ge(u_low, FIRST + 2)
                u_tile(sp, l, 0, 2)

                def step(j4, u):
                    if not ends(j4, u, 3):
                        sp.wait_ge(u_low, FIRST + 2 * (j4 + u) + 4)
                        u_tile(sp, l, j4, u + 3)
                    if not ends(j4, u, 1):
                        sp.wait_ge(v_low, FIRST + 2 * (j4 + u))
                        v_tile(sp, l, j4, u + 1)
                steps_of(sp, step)

            @block.tensor
            def _(te):
                def product(ps, w_hi, w_lo, x_hi, x_lo, start, stop, **kw):
                    te.matmul(ps, f32r(w_hi), f32r(x_hi), start=start, stop=False, **kw)
                    te.matmul(ps, f32r(w_hi), f32r(x_lo), start=False, stop=False, **kw)
                    return te.matmul(ps, f32r(w_lo), f32r(x_hi), start=False, stop=stop, **kw)

                def with_u(j4, u):
                    for k in range(KT):
                        if k % (KT // 2) == 0:
                            te.wait_ge(u_low, FIRST + 2 * (j4 + u) + 1 + k // (KT // 2))
                        cols = slice(k * P, (k + 1) * P)
                        mm = product(banks[u % 4][:, 0:T], u_hi[:, cols], u_lo[:, cols], xhigh[:, k], xlow[:, k], k == 0, k == KT - 1)
                        if (k + 1) % (KT // 2) == 0:
                            mm.then_inc(hidden, 1)

                def with_v(j4, u):
                    s = u % 2
                    te.wait_ge(a_low, FIRST + j4 + u + 1)
                    for d in range(KT):
                        if d % (KT // 2) == 0:
                            te.wait_ge(v_low, FIRST + 2 * (j4 + u) + 1 + d // (KT // 2))
                        cols = slice(d * P, (d + 1) * P)
                        mm = product(ybanks[d // 2][:, (d % 2) * T:(d % 2 + 1) * T], v_hi[:, cols], v_lo[:, cols],
                                     act_high[:, s], act_low[:, s], False, False, skip_group_check=True)
                        if (d + 1) % (KT // 2) == 0:
                            mm.then_inc(mixed, 1)

                start(te, hidden, mixed)
                te.wait_ge(opened, 1)
                for y in ybanks:
                    te.matmul(y[:, :], f32r(act_low[:, 0, 0:P]), f32r(xhigh[:, 0:2]), start=True, stop=False, skip_group_check=True)
                with_u(0, 0)
                with_u(0, 1)

                def step(j4, u):
                    if not ends(j4, u, 2):
                        with_u(j4, u + 2)
                    with_v(j4, u)
                steps_of(te, step)

            def halves(j4, u):
                return ((n, slice(n * H, (n + 1) * H), 2 * (j4 + u) + n) for n in range(2))

            @block.scalar
            def _(a):
                def high(tiles, j4, u):
                    arrived, raw, hi, lo, high_done, low_done, used = tiles
                    a.wait_ge(arrived[u % 2], 8 * j4 + 16 * (u // 2) + 16)
                    for n, cols, half_no in halves(j4, u):
                        a.wait_ge(used, FIRST + half_no - 1)
                        a.activation(f32r(hi[:, cols]), raw[u % 2][:, cols], ACT.Copy).then_inc(high_done, 1)

                def gelu_step(j4, u):
                    a.wait_ge(hidden, FIRST + 2 * (j4 + u) + 2)
                    a.wait_ge(a_low, FIRST + j4 + u - 1)
                    a.activation(act[u % 2], banks[u % 4][:, 0:T], ACT.Gelu_apprx_tanh).then_inc(gelu, 1)

                def a_high_step(j4, u):
                    a.wait_ge(gated, FIRST + j4 + u + 1)
                    a.wait_ge(mixed, FIRST + 2 * (j4 + u) - 2)
                    a.activation(f32r(act_high[:, u % 2]), act[u % 2], ACT.Copy).then_inc(a_high, 1)

                start(a, u_high, v_high, gelu, a_high)
                high(U, 0, 0)
                high(U, 0, 1)
                gelu_step(0, 0)
                high(U, 0, 2)
                a_high_step(0, 0)
                high(W, 0, 0)

                def step(j4, u):
                    if not ends(j4, u, 1):
                        gelu_step(j4, u + 1)
                    if not ends(j4, u, 3):
                        high(U, j4, u + 3)
                    if not ends(j4, u, 1):
                        a_high_step(j4, u + 1)
                        high(W, j4, u + 1)
                steps_of(a, step)

            @block.vector
            def _(v):
                def low(tiles, j4, u):
                    arrived, raw, hi, lo, high_done, low_done, used = tiles
                    for n, cols, half_no in halves(j4, u):
                        v.wait_ge(high_done, FIRST + half_no + 1)
                        v.tensor_tensor(f32r(lo[:, cols]), raw[u % 2][:, cols], hi[:, cols], ALU.subtract).then_inc(low_done, 1)

                def gate_step(j4, u):
                    v.wait_ge(gelu, FIRST + j4 + u + 1)
                    v.tensor_tensor(act[u % 2], act[u % 2], GATES[:, :, j4 + u], ALU.mult).then_inc(gated, 1)

                def a_low_step(j4, u):
                    v.wait_ge(a_high, FIRST + j4 + u + 1)
                    v.tensor_tensor(f32r(act_low[:, u % 2]), act[u % 2], act_high[:, u % 2], ALU.subtract).then_inc(a_low, 1)

                start(v, u_low, v_low, gated, a_low)
                v.tensor_scalar(f32r(act_low[:, 0, 0:P]), iota, 0.0, None, ALU.mult).then_inc(opened, 1)
                low(U, 0, 0)
                low(U, 0, 1)
                gate_step(0, 0)
                low(U, 0, 2)
                a_low_step(0, 0)
                low(W, 0, 0)

                def step(j4, u):
                    if not ends(j4, u, 1):
                        gate_step(j4, u + 1)
                    if not ends(j4, u, 3):
                        low(U, j4, u + 3)
                    if not ends(j4, u, 1):
                        a_low_step(j4, u + 1)
                        low(W, j4, u + 1)
                steps_of(v, step)
                v.wait_ge(mixed, FIRST + 2 * NK)
                for b, y in enumerate(ybanks):
                    v.tensor_tensor(h[:, 2 * b:2 * b + 2], h[:, 2 * b:2 * b + 2], y[:, :].rearrange("p (d t) -> p d t", d=2), ALU.add)\
                        .then_inc(added, 1)
                v.wait_ge(added, KT // 2)

    final = Steps(sem("final_out"), book, "final", False)
    with nc.Fori(0, L) as l:
        with nc.sbuf_tensor("zg", [P, 3, KT, T], F32) as zg, nc.sbuf_tensor("ring", [P, 8, KT * P], F32) as ring:
            rmsnorm("mixnorm", norm_w[:, 2 * l], xn, lambda sp: rwkv_first_tiles(sp, l))
            rwkv_phase(l)
            gdn_phase(l)
            merge_phase(l)
        with (nc.sbuf_tensor("slots", [P, 3, T], F32) as slots, nc.sbuf_tensor("xhigh", [P, KT, T], F32) as xhigh,
              nc.sbuf_tensor("xlow", [P, KT, T], F32) as xlow, nc.sbuf_tensor("act_high", [P, 2, T], F32) as act_high,
              nc.sbuf_tensor("act_low", [P, 2, T], F32) as act_low):
            slot1, slot2, slotg = (slots[:, n] for n in range(3))
            with nc.sbuf_tensor("ring2", [P, 8, KT * P], F32) as ring:
                rmsnorm("ffnnorm", norm_w[:, 2 * l + 1], xn, lambda sp: query_first_loads(sp, l))
                peer_topk_phase(l)
            with nc.sbuf_tensor("raw_tiles", [P, 4, KT * P], F32) as raw, nc.sbuf_tensor("tile_parts", [P, 4, KT * P], F32) as parts:
                peer_gate_phase(l)
                peer_expert_phase(l)
        with nc.Block() as block:
            @block.sync
            def _(sp):
                for s in cleared:
                    sp.sem_clear(s)
    del cleared[:]
    rmsnorm("outnorm", norm_w[:, 2 * L], xn)
    with nc.Block() as block:
        @block.sync
        def _(sp):
            sp.dma_start(out, xn).then_inc(final.sem, 16)
            sp.wait_ge(final.sem, 16)


def constants():
    import numpy as np

    s, t = np.arange(P)[:, None], np.arange(P)[None, :]
    same = s // CH == t // CH
    c = {"ident": s == t, "ones": s >= 0 * t, "blk64": same, "upto": s <= t, "after": s > t,
         "gmask": np.stack([s < t, s <= t], 1), "rmask": np.stack([same & (s < t), same & (s <= t)], 1),
         "lmask": np.stack([(s // (2 * w) == t // (2 * w)) & (s % (2 * w) < w) & (t % (2 * w) >= w)
                            for w in (1 << lev for lev in range(N_LEVELS))], 1),
         "restart": np.broadcast_to(np.arange(T) % CH != 0, (P, T)), "half": s // CH == np.arange(2)[None, :],
         "iota": t + 0 * s}
    return np.concatenate([c[name].astype(np.float32).reshape(P, n) for name, n in CONST_COLS], 1)


def host_layout(x, norm_mix_w, norm_ffn_w, final_norm_w, w_in, lru_conv_w, lru_conv_b, lru_w_a,
                lru_b_a, lru_w_x, lru_b_x, lru_lambda, gdn_conv_w, gdn_a_log, gdn_dt_bias, gdn_norm_w,
                rwkv_mu, rwkv_w0, rwkv_w_up, rwkv_a0, rwkv_a_up, rwkv_g_up, rwkv_k_k, rwkv_k_a,
                rwkv_r_k, rwkv_lnx_w, rwkv_lnx_b, merge_b, p_lru, p_gdn, p_rwkv, w_out,
                peer_wq, peer_keys, peer_u, peer_v):
    import numpy as np

    def tiles(w):
        n = w.shape[2] // P
        return w.reshape(L, KT, P, n, P).transpose(0, 3, 2, 1, 4).reshape(L, n, P, KT * P)

    def chan(v):
        return v.reshape(L, -1, P).transpose(0, 2, 1)

    o = {}
    at = 0
    z = {}
    for name, n in (("u", 1024), ("g", 1024), ("q", 1024), ("k", 1024), ("v", 1024), ("zg", 1024),
                    ("ab", 16), ("r", 1024), ("rk", 1024), ("rv", 1024), ("lora", 256),
                    ("ma", 1024), ("mb", 1024), ("mc", 1024)):
        z[name] = w_in[:, :, at:at + n] if n == 16 else tiles(w_in[:, :, at:at + n])
        at += n
    o["consts"] = constants()
    o["x"] = x[0].T.reshape(KT, P, T).transpose(1, 0, 2)
    norms = [w for l in range(L) for w in (norm_mix_w[l], norm_ffn_w[l])] + [final_norm_w]
    o["norms"] = np.stack([w.reshape(KT, P).T for w in norms], 1)

    o["w_side"] = np.stack([z[n] for n in ("g", "u", "ma", "mb", "mc")], 2)
    o["lru_par"] = np.stack([chan(lru_conv_w[:, j]) for j in range(4)]
                            + [chan(v) for v in (lru_conv_b, lru_b_a, lru_b_x, lru_lambda)], 3)
    gates = np.zeros((L, P, KT, 2, P), np.float32)
    for j, w in enumerate((lru_w_a, lru_w_x)):
        w = w.reshape(L, KT, 2, 64, 64)
        for q in range(2):
            gates[:, 64 * q:64 * q + 64, :, j, 64 * q:64 * q + 64] = w[:, :, q].transpose(0, 2, 1, 3)
    o["lru_gates"] = gates

    o["w_rwkv"] = np.stack([z["r"], z["rk"], z["rv"]], 2)
    o["w_rwkv_lora"] = z["lora"]
    mu = chan(rwkv_mu)
    o["rwkv_par"] = np.stack([mu[:, :, 0:8], mu[:, :, 8:16], mu[:, :, 16:24]]
                             + [chan(v.reshape(L, -1)) for v in (rwkv_w0, rwkv_a0, rwkv_k_k, rwkv_k_a, rwkv_r_k,
                                                                 rwkv_lnx_w, rwkv_lnx_b)], 3)
    o["rwkv_lora_par"] = mu[:, :, 24:26]
    up = np.concatenate([rwkv_w_up, rwkv_a_up], 1).reshape(L, P, KT, P).transpose(0, 2, 1, 3)
    o["rwkv_up"] = np.concatenate([up, rwkv_g_up.reshape(L, P, KT, P).transpose(0, 2, 1, 3)], 3)

    o["w_gdn"] = np.stack([z[n].reshape(L, 4, 2, P, KT * P) for n in ("q", "k", "v", "zg")], 2).reshape(L, 4, 8, P, KT * P)
    conv = gdn_conv_w.reshape(L, 4, 3, 8, P).transpose(0, 4, 3, 2, 1)
    o["gdn_par"] = conv.reshape(L, P, 8, 12)
    o["gdn_norm"] = gdn_norm_w.reshape(L, P, 1)
    o["gdn_ab"] = z["ab"].reshape(L, KT, P, 16).transpose(0, 2, 1, 3)
    rows = np.stack([gdn_a_log, gdn_dt_bias], 1)
    o["gdn_rows"] = np.broadcast_to(rows[:, None, :, :, None], (L, P, 2, 8, 2))

    o["w_gdn_side"] = np.stack([tiles(w).reshape(L, 4, 2, P, KT * P) for w in (p_lru, p_rwkv)], 2).reshape(L, 4, 4, P, KT * P)
    o["p_gdn"] = tiles(p_gdn)
    o["merge_b"] = chan(merge_b).reshape(L, P, 3, KT)
    o["w_out"] = tiles(w_out)

    o["w_query"] = tiles(peer_wq)
    o["keys"] = peer_keys.reshape(L, 16, NK, P).transpose(0, 3, 1, 2)
    o["u"] = peer_u.reshape(L, NK, NK, KT, P).transpose(0, 2, 4, 3, 1).reshape(L, NK, P, KT * P)
    o["v"] = peer_v.reshape(L, NK, NK, D).transpose(0, 2, 1, 3)
    return {k: np.ascontiguousarray(a) for k, a in o.items()}


def kernel(**inputs):
    import numpy as np
    import concourse.bacc as bacc
    from concourse.bass_utils import run_bass_kernel_spmd

    arrays = host_layout(**{k: np.asarray(a) for k, a in inputs.items()})
    book = {"first": True}
    for _ in range(2):
        nc = bacc.Bacc("TRN2", target_bir_lowering=False, num_devices=1)
        A = {k: nc.dram_tensor("in_" + k, a.shape, mybir.dt.from_np(a.dtype), kind="ExternalInput").ap()
             for k, a in arrays.items()}
        out = nc.dram_tensor("out_y", (P, KT, T), F32, kind="ExternalOutput").ap()
        build(nc, A, out, book)
        book.pop("first", None)
    r = run_bass_kernel_spmd(nc, [{"in_" + k: a for k, a in arrays.items()}], core_ids=[0])
    y = r.results[0]["out_y"]
    return np.ascontiguousarray(y.transpose(2, 1, 0).reshape(1, T, D))
```
